# Optimizing a Trainium2 kernel written in Bass

```python
import jax, jax.numpy as jnp
from jax import lax
import numpy as np

D_MODEL = 2048
BATCH = 1
SEQ = 256
DEPTH = 1

D_FF = 5632
A_HEADS = 8
A_HEAD_DIM = 128
Q_LORA = 512
KV_LORA = 256
IDX_HEADS = 16
IDX_DIM = 128
TOPK_MAX = 256
Q_BLOCK = 128
B_HEADS = 8
B_HEAD_DIM = 128
CONV_WIDTH = 4
CHUNK = 64
B_WIDTH = B_HEADS * B_HEAD_DIM
D_MIX = A_HEADS * A_HEAD_DIM + B_WIDTH
IN_SPLITS = (Q_LORA, KV_LORA, IDX_DIM, IDX_HEADS, B_WIDTH, B_WIDTH, B_WIDTH, B_WIDTH, B_HEADS, B_HEADS)
D_IN = sum(IN_SPLITS)
DEEPNORM_ALPHA = (2.0 * DEPTH) ** 0.25
DEEPNORM_BETA = (8.0 * DEPTH) ** -0.25
EPS = 1e-6

kernel_name = 'hybrid_dsa_gdn_macaron_block'

def layer_norm(x, g, b):
    xf = x.astype(jnp.float32)
    mu = jnp.mean(xf, -1, keepdims=True)
    xc = xf - mu
    var = jnp.mean(xc * xc, -1, keepdims=True)
    return (xc * lax.rsqrt(var + EPS) * g.astype(jnp.float32) + b.astype(jnp.float32)).astype(x.dtype)

def rms_norm(x, g):
    xf = x.astype(jnp.float32)
    y = xf * lax.rsqrt(jnp.mean(xf * xf, -1, keepdims=True) + EPS)
    return (y * g.astype(jnp.float32)).astype(x.dtype)

def l2_norm(x):
    return x * lax.rsqrt(jnp.sum(x * x, -1, keepdims=True) + EPS)

def swiglu(x, w_gate, w_up, w_down):
    return (jax.nn.silu(x @ w_gate) * (x @ w_up)) @ w_down

def causal_depthwise_conv(x, w):
    c = x.shape[-1]
    return lax.conv_general_dilated(x, w.astype(x.dtype)[:, None, :], window_strides=(1,),
                                    padding=[(CONV_WIDTH - 1, 0)],
                                    dimension_numbers=('NWC', 'WIO', 'NWC'),
                                    feature_group_count=c)

def dsa_attention(c_q, c_kv, k_idx_raw, w_idx_raw, q_norm_g, kv_norm_g, w_uq, w_uk, w_uv,
                  w_q_idx, k_idx_ln_g, k_idx_ln_b):
    bsz, seq, _ = c_q.shape
    dtype = c_q.dtype
    cq = rms_norm(c_q, q_norm_g)
    ckv = rms_norm(c_kv, kv_norm_g)
    q = jnp.einsum('bsr,rhd->bshd', cq, w_uq)
    q_lat = jnp.einsum('bshd,hdr->bshr', q, w_uk)
    q_idx = (cq @ w_q_idx).reshape(bsz, seq, IDX_HEADS, IDX_DIM)
    k_idx = layer_norm(k_idx_raw, k_idx_ln_g, k_idx_ln_b)
    w_idx = w_idx_raw.astype(jnp.float32) * (IDX_HEADS ** -0.5 * IDX_DIM ** -0.5)
    n_sel = min(TOPK_MAX, seq // 4)
    slopes = 2.0 ** (-8.0 * (jnp.arange(A_HEADS, dtype=jnp.float32) + 1.0) / A_HEADS)
    n_blk = seq // Q_BLOCK
    s_pos = jnp.arange(seq, dtype=jnp.int32)

    def to_blocks(t):
        return jnp.swapaxes(t.reshape(bsz, n_blk, Q_BLOCK, *t.shape[2:]), 0, 1)

    def block(args):
        q_lat_b, q_idx_b, w_b, t_pos = args
        idx_logits = jnp.einsum('bqhd,bsd->bqhs', q_idx_b, k_idx).astype(jnp.float32)
        score = jnp.einsum('bqhs,bqh->bqs', jax.nn.relu(idx_logits), w_b)
        score = jnp.where(s_pos[None, None, :] <= t_pos[None, :, None], score, -jnp.inf)
        _, sel = lax.top_k(score, n_sel)
        kv_sel = jax.vmap(lambda c, i: c[i])(ckv, sel)
        att = jnp.einsum('bqhr,bqkr->bqhk', q_lat_b, kv_sel).astype(jnp.float32) * (A_HEAD_DIM ** -0.5)
        dist = (t_pos[None, :, None] - sel).astype(jnp.float32)
        att = att - slopes[None, None, :, None] * dist[:, :, None, :]
        valid = (sel <= t_pos[None, :, None])[:, :, None, :]
        p = jax.nn.softmax(jnp.where(valid, att, -jnp.inf), axis=-1).astype(dtype)
        o_lat = jnp.einsum('bqhk,bqkr->bqhr', p, kv_sel)
        return jnp.einsum('bqhr,hrd->bqhd', o_lat, w_uv)

    t_blocks = jnp.arange(seq, dtype=jnp.int32).reshape(n_blk, Q_BLOCK)
    out = lax.map(block, (to_blocks(q_lat), to_blocks(q_idx), to_blocks(w_idx), t_blocks))
    return jnp.swapaxes(out, 0, 1).reshape(bsz, seq, A_HEADS * A_HEAD_DIM)

def chunk_gated_delta_rule(q, k, v, g, beta):
    bsz, seq, nh, dk = q.shape
    dv = v.shape[-1]
    n_chk = seq // CHUNK

    def chunks4(t):
        return t.reshape(bsz, n_chk, CHUNK, nh, t.shape[-1]).transpose(0, 3, 1, 2, 4)

    def chunks3(t):
        return t.reshape(bsz, n_chk, CHUNK, nh).transpose(0, 3, 1, 2)

    q, k, v = chunks4(q), chunks4(k), chunks4(v)
    g, beta = chunks3(g), chunks3(beta)
    g_cum = jnp.cumsum(g, axis=-1)
    ar = jnp.arange(CHUNK)
    lower_incl = ar[:, None] >= ar[None, :]
    strict = ar[:, None] > ar[None, :]
    decay = jnp.exp(jnp.where(lower_incl, g_cum[..., :, None] - g_cum[..., None, :], -jnp.inf))
    k_beta = k * beta[..., None]
    v_beta = v * beta[..., None]
    a_mat = jnp.where(strict, jnp.einsum('bhncd,bhned->bhnce', k_beta, k) * decay, 0.0)
    m_mat = a_mat + jnp.eye(CHUNK, dtype=a_mat.dtype)

    def solve(rhs):
        return lax.linalg.triangular_solve(m_mat, rhs, left_side=True, lower=True, unit_diagonal=True)

    value = solve(v_beta)
    k_cumdecay = solve(k_beta * jnp.exp(g_cum)[..., None])
    attn_intra = jnp.einsum('bhncd,bhned->bhnce', q, k) * decay
    q_dec = q * jnp.exp(g_cum)[..., None]
    g_last = g_cum[..., -1]
    k_dec = k * jnp.exp(g_last[..., None] - g_cum)[..., None]
    chunk_decay = jnp.exp(g_last)

    def n_first(t):
        return jnp.moveaxis(t, 2, 0)

    xs = (n_first(q_dec), n_first(k_dec), n_first(value), n_first(k_cumdecay), n_first(attn_intra), n_first(chunk_decay))

    def step(state, inp):
        qd, kd, val, kcd, ai, cd = inp
        v_new = val - jnp.einsum('bhcd,bhde->bhce', kcd, state)
        o = jnp.einsum('bhcd,bhde->bhce', qd, state) + jnp.einsum('bhcj,bhje->bhce', ai, v_new)
        state = state * cd[..., None, None] + jnp.einsum('bhcd,bhce->bhde', kd, v_new)
        return state, o

    state0 = jnp.zeros((bsz, nh, dk, dv), jnp.float32)
    _, o = lax.scan(step, state0, xs)
    return o.transpose(1, 0, 3, 2, 4).reshape(bsz, seq, nh, dv)

def gated_deltanet(q_raw, k_raw, v_raw, z, a, b, conv_w, a_log, dt_bias, o_norm_g):
    bsz, seq, _ = q_raw.shape
    dtype = q_raw.dtype
    qkv = jax.nn.silu(causal_depthwise_conv(jnp.concatenate([q_raw, k_raw, v_raw], -1), conv_w))
    q, k, v = jnp.split(qkv.astype(jnp.float32), 3, axis=-1)
    q = l2_norm(q.reshape(bsz, seq, B_HEADS, B_HEAD_DIM)) * (B_HEAD_DIM ** -0.5)
    k = l2_norm(k.reshape(bsz, seq, B_HEADS, B_HEAD_DIM))
    v = v.reshape(bsz, seq, B_HEADS, B_HEAD_DIM)
    beta = jax.nn.sigmoid(b.astype(jnp.float32))
    g = -jnp.exp(a_log.astype(jnp.float32)) * jax.nn.softplus(a.astype(jnp.float32) + dt_bias.astype(jnp.float32))
    o = chunk_gated_delta_rule(q, k, v, g, beta)
    zf = z.astype(jnp.float32).reshape(bsz, seq, B_HEADS, B_HEAD_DIM)
    y = rms_norm(o, o_norm_g) * jax.nn.silu(zf)
    return y.reshape(bsz, seq, B_WIDTH).astype(dtype)

def hybrid_mixer(h, w_in, q_norm_g, kv_norm_g, w_uq, w_uk, w_uv, w_q_idx, k_idx_ln_g, k_idx_ln_b,
                 conv_w, a_log, dt_bias, o_norm_g, w_out):
    proj = h @ w_in
    cuts = [int(c) for c in np.cumsum(IN_SPLITS)[:-1]]
    c_q, c_kv, k_idx_raw, w_idx_raw, q_b, k_b, v_b, z_b, a_b, b_b = jnp.split(proj, cuts, axis=-1)
    o_a = dsa_attention(c_q, c_kv, k_idx_raw, w_idx_raw, q_norm_g, kv_norm_g, w_uq, w_uk, w_uv,
                        w_q_idx, k_idx_ln_g, k_idx_ln_b)
    o_b = gated_deltanet(q_b, k_b, v_b, z_b, a_b, b_b, conv_w, a_log, dt_bias, o_norm_g)
    return jnp.concatenate([o_a, o_b], axis=-1) @ w_out

def setup_inputs(seed: int = 0) -> dict:
    key = jax.random.key(seed)
    ks = iter(jax.random.split(key, 40))
    f32 = jnp.float32
    L = DEPTH

    def nrm(shape, fan_in, scale=1.0):
        return jax.random.normal(next(ks), shape, f32) * (scale * fan_in ** -0.5)

    def gain(shape):
        return 1.0 + 0.02 * jax.random.normal(next(ks), shape, f32)

    def bias(shape):
        return 0.02 * jax.random.normal(next(ks), shape, f32)

    x = jax.random.normal(next(ks), (BATCH, SEQ, D_MODEL), f32)
    ffn1_w_gate = nrm((L, D_MODEL, D_FF), D_MODEL)
    ffn1_w_up = nrm((L, D_MODEL, D_FF), D_MODEL)
    ffn1_w_down = nrm((L, D_FF, D_MODEL), D_FF, DEEPNORM_BETA)
    ln1_g = gain((L, D_MODEL))
    ln1_b = bias((L, D_MODEL))
    w_in = nrm((L, D_MODEL, D_IN), D_MODEL)
    q_norm_g = gain((L, Q_LORA))
    kv_norm_g = gain((L, KV_LORA))
    w_uq = nrm((L, Q_LORA, A_HEADS, A_HEAD_DIM), Q_LORA)
    w_uk = nrm((L, A_HEADS, A_HEAD_DIM, KV_LORA), KV_LORA)
    w_uv = nrm((L, A_HEADS, KV_LORA, A_HEAD_DIM), KV_LORA)
    w_q_idx = nrm((L, Q_LORA, IDX_HEADS * IDX_DIM), Q_LORA)
    k_idx_ln_g = gain((L, IDX_DIM))
    k_idx_ln_b = bias((L, IDX_DIM))
    conv_w = nrm((L, CONV_WIDTH, 3 * B_WIDTH), CONV_WIDTH)
    a_log = jnp.log(jax.random.uniform(next(ks), (L, B_HEADS), f32, 1.0, 16.0))
    dt = jnp.exp(jax.random.uniform(next(ks), (L, B_HEADS), f32, np.log(1e-3), np.log(1e-1)))
    dt_bias = dt + jnp.log(-jnp.expm1(-dt))
    o_norm_g = gain((L, B_HEAD_DIM))
    w_out = nrm((L, D_MIX, D_MODEL), D_MIX, DEEPNORM_BETA)
    ln2_g = gain((L, D_MODEL))
    ln2_b = bias((L, D_MODEL))
    ffn2_w_gate = nrm((L, D_MODEL, D_FF), D_MODEL)
    ffn2_w_up = nrm((L, D_MODEL, D_FF), D_MODEL)
    ffn2_w_down = nrm((L, D_FF, D_MODEL), D_FF, DEEPNORM_BETA)
    ln3_g = gain((L, D_MODEL))
    ln3_b = bias((L, D_MODEL))
    return {'x': x, 'ffn1_w_gate': ffn1_w_gate, 'ffn1_w_up': ffn1_w_up, 'ffn1_w_down': ffn1_w_down,
            'ln1_g': ln1_g, 'ln1_b': ln1_b, 'w_in': w_in, 'q_norm_g': q_norm_g, 'kv_norm_g': kv_norm_g,
            'w_uq': w_uq, 'w_uk': w_uk, 'w_uv': w_uv, 'w_q_idx': w_q_idx, 'k_idx_ln_g': k_idx_ln_g,
            'k_idx_ln_b': k_idx_ln_b, 'conv_w': conv_w, 'a_log': a_log, 'dt_bias': dt_bias,
            'o_norm_g': o_norm_g, 'w_out': w_out, 'ln2_g': ln2_g, 'ln2_b': ln2_b,
            'ffn2_w_gate': ffn2_w_gate, 'ffn2_w_up': ffn2_w_up, 'ffn2_w_down': ffn2_w_down,
            'ln3_g': ln3_g, 'ln3_b': ln3_b}

def reference(x, ffn1_w_gate, ffn1_w_up, ffn1_w_down, ln1_g, ln1_b, w_in, q_norm_g, kv_norm_g,
              w_uq, w_uk, w_uv, w_q_idx, k_idx_ln_g, k_idx_ln_b, conv_w, a_log, dt_bias, o_norm_g,
              w_out, ln2_g, ln2_b, ffn2_w_gate, ffn2_w_up, ffn2_w_down, ln3_g, ln3_b):
    h = x
    for l in range(DEPTH):
        h = layer_norm(DEEPNORM_ALPHA * h + 0.5 * swiglu(h, ffn1_w_gate[l], ffn1_w_up[l], ffn1_w_down[l]),
                       ln1_g[l], ln1_b[l])
        mix = hybrid_mixer(h, w_in[l], q_norm_g[l], kv_norm_g[l], w_uq[l], w_uk[l], w_uv[l], w_q_idx[l],
                           k_idx_ln_g[l], k_idx_ln_b[l], conv_w[l], a_log[l], dt_bias[l], o_norm_g[l], w_out[l])
        h = layer_norm(DEEPNORM_ALPHA * h + mix, ln2_g[l], ln2_b[l])
        h = layer_norm(DEEPNORM_ALPHA * h + 0.5 * swiglu(h, ffn2_w_gate[l], ffn2_w_up[l], ffn2_w_down[l]),
                       ln3_g[l], ln3_b[l])
    return h


_drawn_inputs = setup_inputs


def setup_inputs(seed=0):
    import zlib

    import numpy as np

    out = dict(_drawn_inputs(seed))
    spreads = {}
    factors = {'q_norm_g': 3.129,
     'kv_norm_g': 8.0,
     'k_idx_ln_g': 3.967,
     'k_idx_ln_b': 3.942,
     'o_norm_g': 8.0,
     'ln2_g': 2.848,
     'ln2_b': 2.742,
     'ln3_g': 2.726,
     'ln3_b': 2.9}
    for name, (base, spread) in spreads.items():
        noise = np.random.default_rng([zlib.crc32(name.encode()), seed]).standard_normal(out[name].shape)
        drawn = base * np.exp(spread * noise) if base else spread * noise
        out[name] = __import__('jax').numpy.asarray(drawn.astype(out[name].dtype))
    for name, factor in factors.items():
        out[name] = (out[name] * factor).astype(out[name].dtype)
    return out
```

```python
from contextlib import ExitStack

import concourse.bass as bass
from concourse import mybir

ALU = mybir.AluOpType
ACT = mybir.ActivationFunctionType
F32 = mybir.dt.float32
F32R = mybir.dt.float32r
I32 = mybir.dt.int32
AX_X = mybir.AxisListType.X

P = 128
BANK = 512
EPS = 1e-6
ALPHA = 2.0 ** 0.25
UNIT_KT = 2
RAW_SLOTS = 8
SPLIT_SLOTS = 3
LEAD = 2
KEPT = 64
KB = 1024


class Phase:

    def __init__(self, name, iters, units, width):
        self.name, self.iters, self.units, self.width = name, iters, units, width


def ring_place(u, units, slots):
    if slots != SPLIT_SLOTS:
        return u % slots
    back = {0: 0, 1: 2, 2: 1}[units % slots]
    middle = max(1, units // 2)
    steps_back = min(max(u - middle, 0), back)
    return (u - 2 * steps_back) % slots


class Stream:

    def __init__(self, phases):
        self.phases = phases
        self.base = []
        self.loads = []
        at, loads = 0, [0] * RAW_SLOTS
        for ph in phases:
            self.base.append(at)
            self.loads.append(list(loads))
            at += ph.iters * ph.units
            for s in range(RAW_SLOTS):
                loads[s] += ph.iters * self.uses(ph, s)

    @staticmethod
    def uses(ph, s):
        return sum(ring_place(u, ph.units, RAW_SLOTS) == s for u in range(ph.units))

    def index(self, p, it, u):
        return it * self.phases[p].units + (self.base[p] + u)

    def loaded(self, p, it, u):
        n = self.phases[p].units
        if u >= n:
            it, u = it + 1, u - n
        s = ring_place(u, n, RAW_SLOTS)
        earlier = sum(ring_place(v, n, RAW_SLOTS) == s for v in range(u))
        return it * (16 * self.uses(self.phases[p], s)) + 16 * (self.loads[p][s] + earlier + 1)

    def freed(self, p, it, u, slots):
        n = self.phases[p].units
        over = u >= n
        if over:
            it, u = it + 1, u - n
        s = ring_place(u, n, slots)
        same = [v for v in range(u) if ring_place(v, n, slots) == s]
        if same:
            c = same[-1] + 1
        else:
            prev = [v for v in range(n) if ring_place(v, n, slots) == s]
            c = prev[-1] - n + 1 if prev else -n
            if not over:
                if p > 0:
                    m = self.phases[p - 1].units
                    prev = [v for v in range(m) if ring_place(v, m, slots) == s]
                    before = prev[-1] - m + 1 if prev else -m
                    c = max(c, before) if self.phases[p].iters > 1 else before
                elif isinstance(it, int) and it == 0:
                    return None
        return it * n + (self.base[p] + c)


def hybrid_block(nc, x, ffn1_w_gate, ffn1_w_up, ffn1_w_down, ln1_g, ln1_b, w_in, q_norm_g, kv_norm_g,
                 w_uq, w_uk, w_uv, w_q_idx, k_idx_ln_g, k_idx_ln_b, conv_w, a_log, dt_bias, o_norm_g,
                 w_out, ln2_g, ln2_b, ffn2_w_gate, ffn2_w_up, ffn2_w_down, ln3_g, ln3_b, out,
                 dump=None, upto=99):
    T = x.shape[1] // P
    D = x.shape[2]
    KT = D // P
    FF = ffn1_w_gate.shape[2]
    FT = FF // P
    QR = q_norm_g.shape[1]
    KR = kv_norm_g.shape[1]
    AH, AD = w_uq.shape[2], w_uq.shape[3]
    ID = k_idx_ln_g.shape[1]
    IH = w_q_idx.shape[2] // ID
    BH = a_log.shape[1]
    BD = o_norm_g.shape[1]
    BW = BH * BD
    TAPS = conv_w.shape[1]
    S = T * P
    RT = KR // P
    QT = QR // P
    A_COLS = QR + KR + ID + IH
    Z_COLS = BW + 2 * BH
    CONV_TILES = 3 * BW // P
    A_SCALE = AD ** -0.5
    W_SCALE = IH ** -0.5 * ID ** -0.5
    assert T == 2 and D == 2048 and FT == 44 and AD == P and BD == P and ID == P

    GATE_CHUNKS = FF // BANK
    OUT_CHUNKS = D // BANK
    KU = KT // UNIT_KT
    DOWN_U = FT // UNIT_KT
    A_ITERS, C_ITERS = 2, 4
    A_W, C_W = A_COLS // A_ITERS, Z_COLS // C_ITERS
    B_ITERS = 3 * BW // BANK
    F1GU, F1D, WA, WB, WC, WQI, WUQ, WO, F2GU, F2D = range(10)
    QI_CHUNKS, UQ_CHUNKS, QU = IH * ID // BANK, AH * AD // BANK, QT // UNIT_KT
    st = Stream([
        Phase("ffn1 gate and up", GATE_CHUNKS, 2 * KU, BANK),
        Phase("ffn1 down", OUT_CHUNKS, DOWN_U, BANK),
        Phase("w_in: latents and index key", A_ITERS, KU, A_W),
        Phase("w_in: q k v", B_ITERS, KU, BANK),
        Phase("w_in: z a b", C_ITERS, KU, C_W),
        Phase("w_q_idx", 1, QI_CHUNKS * QU, BANK),
        Phase("w_uq", 1, UQ_CHUNKS * QU, BANK),
        Phase("w_out", OUT_CHUNKS, KU, BANK),
        Phase("ffn2 gate and up", GATE_CHUNKS, 2 * KU, BANK),
        Phase("ffn2 down", OUT_CHUNKS, DOWN_U, BANK),
    ])
    n0 = {F1GU: 0, F1D: 11, WA: 15, WB: 17, WC: 23, WQI: 27, WUQ: 29, WO: 30, F2GU: 34, F2D: 45}
    n1 = {F1GU: 0, WQI: 11, WUQ: 13, F2GU: 14}

    with ExitStack() as ctx:
        base = 16512
        MZ = base + 104 * KB

        def at(name, offset, shape, dt=F32):
            return nc.alloc_sbuf_tensor_at(name, shape, dt, offset=offset)

        def mz(name, kb, shape, dt=F32):
            return at(name, MZ + int(kb * KB), shape, dt)

        raw = at("raw", base, [P, RAW_SLOTS, UNIT_KT, BANK])
        whi = at("whi", base + 32 * KB, [P, SPLIT_SLOTS, UNIT_KT, BANK], F32R)
        wlo = at("wlo", base + 44 * KB, [P, SPLIT_SLOTS, UNIT_KT, BANK], F32R)
        xT = at("xT", base + 56 * KB, [P, KT, 2, S], F32R)
        resid = at("resid", base + 88 * KB, [P, T, D])

        hT = mz("hT", 0, [P, FT, 2, S], F32R)
        gated = mz("gated", 88, [P, T, BANK])
        ln_g = mz("ln_g", 0, [P, D])
        ln_b = mz("ln_b", 8, [P, D])

        qkvT = mz("qkvT", 0, [P, CONV_TILES, S])
        zab = mz("zab", 24, [P, T, Z_COLS])
        lat = mz("lat", 32.5, [P, T, A_COLS])
        xs = mz("xs", 40, [P, 4, S + TAPS - 1])
        up_to = mz("up_to", 45, [P, P])
        later = mz("later", 45.5, [P, P])
        in_half = mz("in_half", 46, [P, 2, P])
        not_ahead = mz("not_ahead", 47, [P, P])
        pair_mask = mz("pair_mask", 47.5, [P, 6, P])
        wuk = mz("wuk", 50.5, [P, AH, KR])
        wuv = mz("wuv", 90.5, [P, AH, RT, AD])
        qidxT = mz("qidxT", 66.5, [P, IH, S])
        th = mz("th", 66.5, [P, 4, S])
        qT = mz("qT", 82.5, [P, AH, S])
        cq_g = mz("cq_g", 82.5, [P, QR])
        ckv_g = mz("ckv_g", 84.5, [P, KR])
        ki_g = mz("ki_g", 85.5, [P, ID])
        ki_b = mz("ki_b", 86, [P, ID])
        cqT = mz("cqT", 90.5, [P, QT, 2, S], F32R)
        ckv = mz("ckv", 58.5, [P, T, KR])
        ckvT = mz("ckvT", 60.5, [P, RT, S])
        kidxT = mz("kidxT", 62.5, [P, S])
        sel = at("sel", base + 56 * KB, [P, T, S])
        ndist_i = at("ndist_i", base + 56 * KB, [P, T, S], I32)
        ndist = at("ndist", base + 58 * KB, [P, T, S])
        score = mz("score", 33, [P, T, S])
        work = mz("work", 35, [P, T, S])
        relu = mz("relu", 37, [P, 2, 2, S])
        qlatT = at("qlatT", base + 72 * KB, [P, RT, AH, S])
        prob0 = mz("prob0", 82.5, [P, AH, P])
        prob1 = mz("prob1", 50.5, [P, AH, S])
        pT0 = mz("pT0", 33, [P, AH, S])
        pT1 = mz("pT1", 41, [P, AH, P])
        olatT = mz("olatT", 66.5, [P, RT, AH, S])
        vb = mz("vb", 50.5, [P, T, BH, BD])
        kbeg = mz("kbeg", 58.5, [P, T, BH, BD])
        kdec = mz("kdec", 66.5, [P, T, BH, BD])
        aiT = mz("aiT", 74.5, [P, T, BH, P])
        aT = mz("aT", 82.5, [P, T, BH, P])
        sq = mz("sq", 82.5, [P, 2 * BH, S])
        dT = mz("dT", 90.5, [P, T, BH, P])
        xinv = mz("xinv", 90.5, [P, T, BH, P])
        kbT = mz("kbT", 33, [P, T, BH, P])
        yinv = mz("yinv", 33, [P, T, BH, P])
        kb = mz("kb", 82.5, [P, T, BH, BD])
        lev = mz("lev", 8, [P, T, BH, P])
        t1 = mz("t1", 16, [P, T, BH, P])
        nkcdT = mz("nkcdT", 82.5, [P, T, BH, P])
        state = mz("state", 90.5, [P, BH, BD])
        vnew = mz("vnew", 94.5, [P, BH, BD])
        thz_sb = at("thz_sb", base + 72 * KB, [P, T, BW])
        oy = mz("oy", 8, [P, T, BH, BD])
        small = mz("small", 41, [P, 40, T, BH])

        cz = base + 204 * KB
        ident = at("ident", cz, [P, P])
        cw = at("cw", cz + 512, [P, TAPS, CONV_TILES])
        cw_rows = mz("cw_rows", 89, [TAPS * CONV_TILES, P])
        stats = at("stats", cz + 896, [P, T, OUT_CHUNKS, 6])
        mv = at("mv", cz + 1088, [P, T, 2])
        rstd = at("rstd", cz + 1120, [P, T])
        half_neg = at("half_neg", cz + 1152, [P, 32])
        ss = at("ss", cz + 1280, [P, 3, T])
        rs = at("rs", cz + 1312, [P, 3, T])
        kmv = at("kmv", cz + 1344, [P, T, 2])
        kstats = at("kstats", cz + 1376, [P, T, 6])
        widx = at("widx", cz + 1440, [P, T, IH])
        top8 = at("top8", cz + 1568, [P, T, 8])
        amax = at("amax", cz + 1632, [P, T, AH])
        nmax = at("nmax", cz + 1696, [P, T, AH])
        psumm = at("psumm", cz + 1760, [P, T, AH])
        pinv = at("pinv", cz + 1824, [P, T, AH])
        alog = at("alog", cz + 1888, [P, BH])
        dtb = at("dtb", cz + 1920, [P, BH])
        og = at("og", cz + 1952, [P, BD])
        ones = at("ones", cz + 2464, [P, 2])
        half_scale = at("half_scale", cz + 2496, [P, 32])

        def psum(name, shape):
            return ctx.enter_context(nc.psum_tensor(name, shape, F32))

        acc0 = psum("acc0", [P, 2, BANK])
        acc1 = psum("acc1", [P, 2, BANK])
        tp = psum("tp", [P, 4, BANK])

        class Sems:

            def __init__(self):
                self.made = {}

            def __call__(self, name):
                if name not in self.made:
                    self.made[name] = ctx.enter_context(nc.semaphore("s_" + name))
                return self.made[name]

        sem = Sems()
        raw_loaded = [sem(f"raw_loaded{i}") for i in range(RAW_SLOTS)]
        hi_done, lo_done, unit_used = sem("hi_done"), sem("lo_done"), sem("unit_used")
        acc0a_done = sem("acc0a_done")
        acc0_free = [sem("acc0a_free"), sem("acc0b_free")]
        acc1_free = [sem("acc1a_free"), sem("acc1b_free")]

        def wait(eng, s, value):
            if not (isinstance(value, int) and value <= 0):
                eng.wait_ge(s, value)

        def load_unit(sp, p, it, u, src):
            s = ring_place(u, st.phases[p].units, RAW_SLOTS)
            free = st.freed(p, it, u, RAW_SLOTS)
            if free is not None:
                wait(sp, lo_done, free)
            sp.dma_start(raw[:, s, :, 0:src.shape[2]], src).then_inc(raw_loaded[s], 16)

        def cut_width(p, u):
            return st.phases[p].width if u < st.phases[p].units else BANK

        def split_hi(act, p, it, u):
            n, w = st.phases[p].units, cut_width(p, u)
            s, r = ring_place(u % n, n, SPLIT_SLOTS), ring_place(u % n, n, RAW_SLOTS)
            act.wait_ge(raw_loaded[r], st.loaded(p, it, u))
            free = st.freed(p, it, u, SPLIT_SLOTS)
            if free is not None:
                wait(act, unit_used, free)
            act.activation(whi[:, s, :, 0:w], raw[:, r, :, 0:w], ACT.Copy).then_inc(hi_done, 1)

        def split_lo(dve, p, it, u):
            n, w = st.phases[p].units, cut_width(p, u)
            s, r = ring_place(u % n, n, SPLIT_SLOTS), ring_place(u % n, n, RAW_SLOTS)
            dve.wait_ge(hi_done, st.index(p, it, u + 1))
            dve.tensor_tensor(wlo[:, s, :, 0:w], raw[:, r, :, 0:w], whi[:, s, :, 0:w].bitcast(F32),
                              ALU.subtract).then_inc(lo_done, 1)

        def unit_mm(pe, p, it, u, acc, free, n_chunk, moving, stat, kt0, first, last, a_done=None,
                    ready=None, width=None):
            n = st.phases[p].units
            s = ring_place(u, n, SPLIT_SLOTS)
            width = width or st.phases[p].width
            pe.wait_ge(lo_done, st.index(p, it, u + 1))
            for half in range(2):
                if first and n_chunk is not None:
                    wait(pe, free[half], n_chunk)
                if moving == "w":
                    for k in range(UNIT_KT):
                        kt = kt0 + k
                        hi = stat[:, kt, 0, half * P:half * P + P]
                        lo = stat[:, kt, 1, half * P:half * P + P]
                        o = acc[:, half, 0:width]
                        pe.matmul(o, hi, whi[:, s, k, 0:width], start=first and k == 0, stop=False)
                        pe.matmul(o, hi, wlo[:, s, k, 0:width], start=False, stop=False)
                        ins = pe.matmul(o, lo, whi[:, s, k, 0:width], start=False,
                                        stop=last and k == UNIT_KT - 1)
                else:
                    for c in range(2):
                        cols = slice((2 * half + c) * P, (2 * half + c) * P + P)
                        o = acc[:, half, c * S:c * S + S]
                        for k in range(UNIT_KT):
                            hi, lo = stat[:, kt0 + k, 0, :], stat[:, kt0 + k, 1, :]
                            end = last and k == UNIT_KT - 1
                            pe.matmul(o, whi[:, s, k, cols], hi, start=first and k == 0 and c == 0,
                                      stop=False, skip_group_check=True)
                            pe.matmul(o, whi[:, s, k, cols], lo, start=False, stop=False,
                                      skip_group_check=True)
                            ins = pe.matmul(o, wlo[:, s, k, cols], hi, start=False, stop=end,
                                            skip_group_check=True)
                if half == 0 and last and a_done is not None:
                    ins.then_inc(a_done, 1)
            ins.then_inc(unit_used, 1)

        def to_xT_pe(pe, e):
            if e == 0:
                pe.wait_ge(sem("ident"), 2)
            for q in range(4):
                if e == 0:
                    pe.wait_ge(sem(f"x_loaded{q}"), 16)
                if e > 0:
                    pe.wait_ge(sem("ln_out"), 8 * (e - 1) + 2 * q + 2)
                if 4 * e + q >= 2:
                    pe.wait_ge(sem("xT_lo"), 4 * e + q - 1)
                for k in range(4):
                    for t in range(T):
                        ins = pe.transpose(tp[:, 2 * (q % 2) + k // 2, (k % 2) * S + t * P:(k % 2) * S + t * P + P],
                                           resid[:, t, (4 * q + k) * P:(4 * q + k + 1) * P], ident[:])
                ins.then_inc(sem("xT_ps"), 1)

        def tp_pair(i):
            return tp[:, 2 * i:2 * i + 2, :].rearrange("p b (k s) -> p (b k) s", k=2)

        def to_xT_act(act, e):
            for q in range(4):
                act.wait_ge(sem("xT_ps"), 4 * e + q + 1)
                act.activation(xT[:, 4 * q:4 * q + 4, 0, :], tp_pair(q % 2), ACT.Copy).then_inc(sem("xT_hi"), 1)

        def to_xT_dve_step(dve, e, q):
            dve.wait_ge(sem("xT_hi"), 4 * e + q + 1)
            dve.tensor_tensor(xT[:, 4 * q:4 * q + 4, 1, :], tp_pair(q % 2),
                              xT[:, 4 * q:4 * q + 4, 0, :].bitcast(F32), ALU.subtract).then_inc(sem("xT_lo"), 1)

        def norm_dve(dve, e, transposed):
            for t in range(T):
                dve.wait_ge(sem("stats"), T * OUT_CHUNKS * (e + 1))
                dve.bn_aggr(mv[:, t], stats[:, t]).then_inc(sem("ln_mv"), 1)
            dve.wait_ge(sem("ln_rstd"), 2 * e + 2)
            dve.wait_ge(sem("ln_gains"), 32 * (e + 1))
            for q in range(4):
                cols = slice(q * BANK, q * BANK + BANK)
                for t in range(T):
                    dve.scalar_tensor_tensor(out=resid[:, t, cols], in0=resid[:, t, cols], scalar=mv[:, t, 0:1],
                                             in1=ln_g[:, cols], op0=ALU.subtract, op1=ALU.mult)\
                       .then_inc(sem("ln_mid"), 1)
                for t in range(T):
                    dve.wait_ge(sem("ln_mid"), 8 * e + 2 * q + t + 1)
                    dve.scalar_tensor_tensor(out=resid[:, t, cols], in0=resid[:, t, cols], scalar=rstd[:, t:t + 1],
                                             in1=ln_b[:, cols], op0=ALU.mult, op1=ALU.add)\
                       .then_inc(sem("ln_out"), 1)
                if transposed and q >= 1:
                    to_xT_dve_step(dve, e + 1, q - 1)
            if transposed:
                to_xT_dve_step(dve, e + 1, 3)

        def norm_gains(pool, g, b):
            for dst, src in ((ln_g, g), (ln_b, b)):
                pool.dma_start(dst[:], src.to_broadcast([P, D])).then_inc(sem("ln_gains"), 16)

        def norm_pool(pool, e):
            pool.wait_ge(sem("ln_mv"), 2 * e + 2)
            pool.tensor_scalar(rstd[:], mv[:, :, 1], EPS / ALPHA ** 2, None, ALU.add).then_inc(sem("ln_rstd"), 1)
            pool.wait_ge(sem("ln_rstd"), 2 * e + 1)
            pool.tensor_tensor(rstd[:], rstd[:], half_neg[:, 0:T], ALU.pow).then_inc(sem("ln_rstd"), 1)

        GU, DN = [F1GU, F2GU], [F1D, F2D]

        def ffn_loads(sp, f, w_gate, w_up, w_down):
            gate_v = w_gate.rearrange("(k p) n -> p k n", p=P)
            up_v = w_up.rearrange("(k p) n -> p k n", p=P)
            down_v = w_down.rearrange("(k p) n -> p k n", p=P)

            def gate_up(c):
                for v, view in ((0, gate_v), (KU, up_v)):
                    for u in range(KU):
                        load_unit(sp, GU[f], c, v + u, view[:, 2 * u:2 * u + 2, bass.ds(c * BANK, BANK)])

            gate_up(0)
            with sp.Fori(1, GATE_CHUNKS) as c:
                gate_up(c)
            with sp.Fori(0, OUT_CHUNKS) as c:
                for u in range(DOWN_U):
                    load_unit(sp, DN[f], c, u, down_v[:, 2 * u:2 * u + 2, bass.ds(c * BANK, BANK)])

        def hT_pe(pe, f, c):
            for half in range(2):
                pe.wait_ge(acc1_free[half], c + n1[GU[f]])
            for k in range(4):
                for t in range(T):
                    ins = pe.transpose(tp[:, k // 2, (k % 2) * S + t * P:(k % 2) * S + t * P + P],
                                       gated[:, t, k * P:k * P + P], ident[:])
            ins.then_inc(sem("hT_ps"), 1)

        def hT_act(act, f, c):
            act.wait_ge(sem("hT_ps"), c + f * GATE_CHUNKS)
            act.activation(hT[:, bass.ds(4 * (c - 1), 4), 0, :], tp_pair(0), ACT.Copy).then_inc(sem("hT_hi"), 1)

        def hT_dve(dve, f, c):
            dve.wait_ge(sem("hT_hi"), c + f * GATE_CHUNKS)
            dve.tensor_tensor(hT[:, bass.ds(4 * (c - 1), 4), 1, :], tp_pair(0),
                              hT[:, bass.ds(4 * (c - 1), 4), 0, :].bitcast(F32), ALU.subtract)\
               .then_inc(sem("hT_lo"), 1)

        def gate_times_up(dve, f, c):
            dve.wait_ge(unit_used, st.index(GU[f], c, 0))
            for t in range(T):
                dve.wait_ge(acc0_free[t], c + n0[GU[f]])
                dve.tensor_tensor(gated[:, t], gated[:, t], acc1[:, t], ALU.mult).then_inc(acc1_free[t], 1)

        def ffn_pe(pe, f):
            def gate_up(c, prev):
                for u in range(KU):
                    pe.wait_ge(sem("xT_lo"), 8 * f + u // 2 + 1)
                    unit_mm(pe, GU[f], c, u, acc0, acc0_free, c + n0[GU[f]], "w", xT, 2 * u, u == 0, u == KU - 1,
                            acc0a_done)
                    if u == 3 and prev:
                        hT_pe(pe, f, c)
                for u in range(KU):
                    unit_mm(pe, GU[f], c, KU + u, acc1, acc1_free, c + n1[GU[f]], "w", xT, 2 * u, u == 0,
                            u == KU - 1)

            gate_up(0, False)
            with pe.Fori(1, GATE_CHUNKS) as c:
                gate_up(c, True)

            def down(c, tail):
                for u in range(DOWN_U):
                    if tail and u == 0:
                        pe.wait_ge(sem("hT_lo"), (f + 1) * GATE_CHUNKS - 1)
                    if tail and 4 * (GATE_CHUNKS - 1) == 2 * u:
                        pe.wait_ge(sem("hT_lo"), (f + 1) * GATE_CHUNKS)
                    unit_mm(pe, DN[f], c, u, acc0, acc0_free, c + n0[DN[f]], "w", hT, 2 * u, u == 0,
                            u == DOWN_U - 1, acc0a_done)
                    if tail and u == 3:
                        hT_pe(pe, f, GATE_CHUNKS)

            down(0, True)
            with pe.Fori(1, OUT_CHUNKS) as c:
                down(c, False)

        def ffn_act(act, f, last):
            def gate_up(c, prev):
                for u in range(LEAD, 2 * KU + LEAD):
                    split_hi(act, GU[f], c, u)
                    if u == 6 and prev:
                        hT_act(act, f, c)
                    if u == KU + 1:
                        act.wait_ge(unit_used, st.index(GU[f], c, KU))
                        if prev or f > 0:
                            act.wait_ge(sem("hT_ps"), c + f * GATE_CHUNKS)
                        act.activation(gated[:], acc0[:], ACT.Tanh, scale=0.5).then_inc(sem("tanh_gate"), 1)

            gate_up(0, False)
            with act.Fori(1, GATE_CHUNKS) as c:
                gate_up(c, True)

            def down(c, tail, lead):
                for u in range(LEAD, DOWN_U + lead):
                    split_hi(act, DN[f], c, u)
                    if u == 6 and tail:
                        hT_act(act, f, GATE_CHUNKS)

            down(0, True, LEAD)
            with act.Fori(1, OUT_CHUNKS - 1) as c:
                down(c, False, LEAD)
            down(OUT_CHUNKS - 1, False, 0 if last else LEAD)

        def into_resid(dve, p, c, scale, e, in_phase):
            for t in range(T):
                if t == 0:
                    dve.wait_ge(acc0a_done, c + (n0[p] + 1))
                else:
                    dve.wait_ge(unit_used, st.index(p, c, in_phase))
                cols = bass.ds(c * BANK, BANK)
                dve.scalar_tensor_tensor(out=resid[:, t, cols], in0=acc0[:, t], scalar=scale,
                                         in1=resid[:, t, cols], op0=ALU.mult, op1=ALU.add)\
                   .then_inc(acc0_free[t], 1)
            for t in range(T):
                dve.wait_ge(acc0_free[t], c + (n0[p] + 1))
                if isinstance(c, int):
                    where = stats[:, t, c]
                else:
                    where = stats[:, t, bass.ds(c, 1), :].rearrange("p a s -> p (a s)")
                dve.bn_stats(where, resid[:, t, bass.ds(c * BANK, BANK)]).then_inc(sem("stats"), 1)

        def ffn_dve(dve, f, last):
            def gate_up(c, prev):
                if prev:
                    gate_times_up(dve, f, c)
                for u in range(LEAD, 2 * KU + LEAD):
                    split_lo(dve, GU[f], c, u)
                    if u == 6 and prev:
                        hT_dve(dve, f, c)
                    if u == KU + 1:
                        dve.wait_ge(sem("tanh_gate"), c + (f * GATE_CHUNKS + 1))
                        for t in range(T):
                            dve.scalar_tensor_tensor(out=gated[:, t], in0=gated[:, t], scalar=1.0, in1=acc0[:, t],
                                                     op0=ALU.add, op1=ALU.mult).then_inc(acc0_free[t], 1)

            gate_up(0, False)
            with dve.Fori(1, GATE_CHUNKS) as c:
                gate_up(c, True)

            def down(c, tail, lead):
                if tail:
                    gate_times_up(dve, f, GATE_CHUNKS)
                for u in range(LEAD, DOWN_U + lead):
                    split_lo(dve, DN[f], c, u)
                    if u == 6 and tail:
                        hT_dve(dve, f, GATE_CHUNKS)
                into_resid(dve, DN[f], c, 0.25 / ALPHA, 2 * f, DOWN_U)

            down(0, True, LEAD)
            with dve.Fori(1, OUT_CHUNKS - 1) as c:
                down(c, False, LEAD)
            down(OUT_CHUNKS - 1, False, 0 if last else LEAD)

        NEG = -1e30
        CAUSAL_FILL, TAKEN = -3e38, -3.3e38
        G8 = BH // 2
        GROUPS = [(t, hh) for t in range(T) for hh in range(2)]
        LEVELS = 5
        NAMES = ["xa", "ax", "ex", "spl", "sp", "beta", "tb", "g", "eg", "ekd", "gc", "rq", "rk", "cd0", "cd1",
                 "c1", "c2", "c3", "vbs", "qs", "sso", "a1", "a2", "ro", "co"]
        assert len(NAMES) <= 40

        def sm(name):
            return small[:, NAMES.index(name)]

        def sm_group(name, t, hh):
            return sm(name)[:, t, G8 * hh:G8 * hh + G8].unsqueeze(2).to_broadcast([P, G8, P])

        def group(tile, t, hh):
            return tile[:, t, G8 * hh:G8 * hh + G8, :]

        def bankE(i):
            return (acc0, acc0, acc1, acc1)[i][:, i % 2]

        def bankF(i):
            return tp[:, i]

        def heads4(bank):
            return bank.rearrange("p (h c) -> p h c", h=G8)

        def halves(bank):
            return bank.rearrange("p (k s) -> p k s", k=2)

        def kT_of(h, t):
            return qkvT[:, BH + h, t * P:t * P + P]

        def vT_of(h, t):
            return qkvT[:, 2 * BH + h, t * P:t * P + P]

        def qT_of(h, t):
            return qkvT[:, h, t * P:t * P + P]

        def mixer_loads(sp):
            in_v = w_in[0].rearrange("(k p) n -> p k n", p=P)
            for p, iters, width, col0 in ((WA, A_ITERS, A_W, 0), (WB, B_ITERS, BANK, A_COLS),
                                          (WC, C_ITERS, C_W, A_COLS + 3 * BW)):
                with sp.Fori(0, iters) as c:
                    for u in range(KU):
                        load_unit(sp, p, c, u, in_v[:, 2 * u:2 * u + 2, bass.ds(c * width + col0, width)])
            qi_v = w_q_idx[0].rearrange("(k p) n -> p k n", p=P)
            uq_v = w_uq[0].rearrange("(k p) h d -> p k (h d)", p=P)
            for p, view, chunks in ((WQI, qi_v, QI_CHUNKS), (WUQ, uq_v, UQ_CHUNKS)):
                for j in range(chunks):
                    for u in range(QU):
                        load_unit(sp, p, 0, j * QU + u, view[:, 2 * u:2 * u + 2, j * BANK:(j + 1) * BANK])
            out_v = w_out[0].rearrange("(k p) n -> p k n", p=P)
            if upto < 9:
                for u in range(LEAD):
                    load_unit(sp, WO, 0, u, out_v[:, 2 * u:2 * u + 2, 0:BANK])
                return
            with sp.Fori(0, OUT_CHUNKS) as c:
                for u in range(KU):
                    load_unit(sp, WO, c, u, out_v[:, 2 * u:2 * u + 2, bass.ds(c * BANK, BANK)])

        def mixer_pool(pool):
            pool.wait_ge(unit_used, st.index(WA, 0, 0))
            for dst, src, n in ((cq_g, q_norm_g, QR), (ckv_g, kv_norm_g, KR), (ki_g, k_idx_ln_g, ID),
                                (ki_b, k_idx_ln_b, ID)):
                pool.dma_start(dst[:], src.to_broadcast([P, n])).then_inc(sem("latent_gains"), 16)
            for dst, src, n in ((alog, a_log, BH), (dtb, dt_bias, BH), (og, o_norm_g, BD)):
                pool.dma_start(dst[:], src.to_broadcast([P, n])).then_inc(sem("delta_gains"), 16)
            pool.memset(xs[:, :, 0:TAPS - 1], 0.0).then_inc(sem("xs_th_free"), 1)
            pool.memset(ones[:], 1.0).then_inc(sem("ones"), 1)
            pool.dma_start(wuk[:], w_uk[0].rearrange("h d r -> d h r")).then_inc(sem("wuk"), 16)
            pool.wait_ge(sem("lat_ss"), 2 * T)
            pool.wait_ge(sem("k_mv"), T)
            pool.tensor_scalar(rs[:, 0], ss[:, 0], 1.0 / QR, EPS, ALU.mult, ALU.add).then_inc(sem("lat_rs"), 1)
            pool.tensor_scalar(rs[:, 1], ss[:, 1], 1.0 / KR, EPS, ALU.mult, ALU.add).then_inc(sem("lat_rs"), 1)
            pool.tensor_scalar(rs[:, 2], kmv[:, :, 1], EPS, None, ALU.add).then_inc(sem("lat_rs"), 1)
            pool.wait_ge(sem("lat_rs"), 3)
            rs_flat = rs[:].rearrange("p a t -> p (a t)")
            pool.tensor_tensor(rs_flat, rs_flat, half_neg[:, 0:3 * T], ALU.pow).then_inc(sem("lat_rs"), 1)
            pool.wait_ge(unit_used, st.index(WQI, 0, 0))
            pool.iota(ndist_i[:], pattern=[[-P, T], [1, S]], base=0, channel_multiplier=-1).then_inc(sem("ndist"), 1)
            pool.wait_ge(sem("ndist"), 1)
            pool.tensor_copy(ndist[:], ndist_i[:]).then_inc(sem("ndist"), 1)

            CH = P // 2
            marks = [0]

            def mark(ins):
                ins.then_inc(sem("masks"), 1)
                marks[0] += 1

            def chunked(ap):
                return ap.rearrange("p (b j) -> p b j", b=2)

            mark(pool.memset(up_to[:], 1.0))
            mark(pool.memset(later[:], 1.0))
            mark(pool.memset(in_half[:], 1.0))
            mark(pool.memset(not_ahead[:], 0.0))
            mark(pool.memset(pair_mask[:], 0.0))
            pool.wait_ge(sem("masks"), marks[0])
            for i in range(6):
                m = 1 << i
                v = pair_mask[:, i].rearrange("p (b h j) -> p b h j", h=2, j=m)
                mark(pool.memset(v[:, :, 1, :], 1.0))

            def keep(ap, base_, pattern, mult, fill=0.0):
                mark(pool.affine_select(out=ap, in_=ap, compare_op=ALU.is_ge, fill=fill, base=base_,
                                        pattern=pattern, channel_multiplier=mult))

            keep(chunked(up_to[:]), 0, [[CH, 2], [1, CH]], -1)
            keep(chunked(not_ahead[:]), 0, [[CH, 2], [1, CH]], -1, NEG)
            keep(chunked(later[:]), -1, [[-CH, 2], [-1, CH]], 1)
            keep(in_half[:, 0], CH - 1, [[0, P]], -1)
            keep(in_half[:, 1], -CH, [[0, P]], 1)
            pool.wait_ge(sem("masks"), marks[0])
            keep(chunked(up_to[:]), 0, [[-CH, 2], [0, CH]], 1)
            keep(chunked(not_ahead[:]), 0, [[-CH, 2], [0, CH]], 1, NEG)
            keep(chunked(later[:]), CH - 1, [[CH, 2], [0, CH]], -1)
            views = []
            for i in range(6):
                m = 1 << i
                v = pair_mask[:, i].rearrange("p (b h j) -> p b (h j)", h=2, j=m)
                views.append((m, P // (2 * m), v))
                keep(v, 0, [[-2 * m, P // (2 * m)], [0, 2 * m]], 1)
            pool.wait_ge(sem("masks"), marks[0])
            for m, nb, v in views:
                keep(v, m - 1, [[2 * m, nb], [0, 2 * m]], -1)
            assert marks[0] == MASKS

            if upto < 2:
                return
            pool.wait_ge(unit_used, st.index(WO, 0, 0))
            pool.dma_start(wuv[:], w_uv[0].rearrange("h (t r) d -> r h t d", r=P)).then_inc(sem("wuv"), 16)
            pool.wait_ge(sem("score_acc"), 2 * IH)
            for t in range(T):
                n = (t + 1) * P
                pool.affine_select(out=score[:, t, 0:n], in_=score[:, t, 0:n], compare_op=ALU.is_ge,
                                   fill=CAUSAL_FILL, base=t * P, pattern=[[-1, n]], channel_multiplier=1)\
                    .then_inc(sem("score_masked"), 1)
            for t in range(T):
                n = (t + 1) * P
                pool.wait_ge(sem("sel_raw"), 2 * T)
                pool.affine_select(out=sel[:, t, 0:n], in_=sel[:, t, 0:n], compare_op=ALU.is_ge,
                                   fill=NEG, base=t * P, pattern=[[-1, n]], channel_multiplier=1)\
                    .then_inc(sem("sel"), 1)
            if upto < 3:
                return
            pool.wait_ge(sem("qk_ss"), 1)
            qk = small[:, NAMES.index("rq"):NAMES.index("rq") + 2].rearrange("p a t h -> p (a t h)")
            pool.tensor_scalar(qk, qk, 4 * EPS, None, ALU.add).then_inc(sem("qk_r"), 1)
            pool.wait_ge(sem("qk_r"), 1)
            pool.tensor_tensor(qk, qk, half_neg[:, 0:2 * T * BH], ALU.pow).then_inc(sem("qk_r"), 1)
            pool.wait_ge(sem("y_up"), 4 * (LEVELS + 1))
            pool.memset(state[:], 0.0).then_inc(sem("state0"), 1)
            ro = sm("ro").rearrange("p t h -> p (t h)")
            pool.wait_ge(sem("o_a2"), 1)
            pool.tensor_scalar(ro, sm("a2").rearrange("p t h -> p (t h)"), EPS, None, ALU.add)\
                .then_inc(sem("o_r"), 1)
            pool.wait_ge(sem("o_r"), 1)
            pool.tensor_tensor(ro, ro, half_neg[:, 0:T * BH], ALU.pow).then_inc(sem("o_r"), 1)
            if upto < 9:
                return
            pool.wait_ge(sem("y_lo"), 2)
            norm_gains(pool, ln2_g, ln2_b)
            norm_pool(pool, 1)

        MASKS = 5 + 6 + 5 + 3 + 6 + 6
        SCORE_ITEMS = IH

        def mixer_act(act):
            def read_acc0(p, c, units, dst):
                for t in range(T):
                    if t == 0:
                        act.wait_ge(acc0a_done, c + (n0[p] + 1))
                    else:
                        act.wait_ge(unit_used, st.index(p, c, units))
                    w = st.phases[p].width
                    act.activation(dst[:, t, bass.ds(c * w, w)], acc0[:, t, 0:w], ACT.Copy)\
                       .then_inc(acc0_free[t], 1)

            with act.Fori(0, A_ITERS) as c:
                for u in range(LEAD, KU + LEAD):
                    split_hi(act, WA, c, u)
                read_acc0(WA, c, KU, lat)
            for t in range(T):
                act.wait_ge(acc0_free[t], n0[WB])
            flat = qidxT[:].rearrange("p h s -> p (h s)")
            for t in range(T):
                act.activation(flat[:, 1024 * t:1024 * t + QR], lat[:, t, 0:QR], ACT.Square,
                               accum_out=ss[:, 0, t:t + 1]).then_inc(sem("lat_ss"), 1)
                act.activation(flat[:, 1024 * t + QR:1024 * t + QR + KR], lat[:, t, QR:QR + KR], ACT.Square,
                               accum_out=ss[:, 1, t:t + 1]).then_inc(sem("lat_ss"), 1)
            act.wait_ge(sem("lat_ss"), 2 * T)

            def conv_tanh(c):
                act.wait_ge(sem("conv_sum"), c * 16 + 16)
                act.activation(th[:], qkvT[:, bass.ds(4 * c, 4), :], ACT.Tanh, scale=0.5)\
                   .then_inc(sem("qkv_tanh"), 1)

            def qkv_chunk(c, prev):
                for u in range(LEAD, KU + LEAD):
                    split_hi(act, WB, c, u)
                    if u == 4 and prev:
                        conv_tanh(c - 1)
                act.wait_ge(sem("xs_th_free"), c + 1)
                for half in range(2):
                    if half == 0:
                        act.wait_ge(acc0a_done, c + (n0[WB] + 1))
                    else:
                        act.wait_ge(unit_used, st.index(WB, c, KU))
                    act.activation(xs[:, 2 * half:2 * half + 2, TAPS - 1:], halves(acc0[:, half]), ACT.Copy)\
                       .then_inc(acc0_free[half], 1)

            qkv_chunk(0, False)
            with act.Fori(1, B_ITERS) as c:
                qkv_chunk(c, True)
            conv_tanh(B_ITERS - 1)
            act.wait_ge(sem("lat_ps"), 1)
            act.activation(cqT[:, :, 0, :], tp_pair(0), ACT.Copy).then_inc(sem("cqT_hi"), 1)
            act.activation(ckvT[:], halves(tp[:, 2]), ACT.Copy).then_inc(sem("latT"), 1)
            act.activation(kidxT[:], tp[:, 3, 0:S], ACT.Copy).then_inc(sem("latT"), 1)

            with act.Fori(0, C_ITERS) as c:
                for u in range(LEAD, KU + LEAD):
                    split_hi(act, WC, c, u)
                read_acc0(WC, c, KU, zab)

            act.wait_ge(sem("xs_th_free"), B_ITERS + 1)
            act.wait_ge(sem("lat_norm"), 3 * T)
            for p, dst, chunks in ((WQI, qidxT, QI_CHUNKS), (WUQ, qT, UQ_CHUNKS)):
                for u in range(LEAD, chunks * QU + LEAD):
                    split_hi(act, p, 0, u)
                    if u % QU == 1:
                        j = (u - 3) // QU
                        acc, free = ((acc0, acc0_free), (acc1, acc1_free))[j % 2]
                        act.wait_ge(unit_used, st.index(p, 0, (j + 1) * QU))
                        for half in range(2):
                            act.activation(dst[:, 4 * j + 2 * half:4 * j + 2 * half + 2, :], halves(acc[:, half]),
                                           ACT.Copy).then_inc(free[half], 1)
            if upto < 2:
                return
            for i in range(SCORE_ITEMS):
                n = (i % T + 1) * P
                act.wait_ge(sem("score_ps"), i + 1)
                wait(act, sem("score_acc"), 2 * (i - 1))
                act.activation(relu[:, i % 2, :, 0:n], halves(tp[:, i % 4])[:, :, 0:n], ACT.Relu)\
                   .then_inc(sem("relu"), 1)
            for h in range(AH):
                act.wait_ge(sem("qlat_ps"), h + 1)
                act.activation(qlatT[:, :, h, :], halves(tp[:, h % 4]), ACT.Copy).then_inc(sem("qlat"), 1)
            for t, prob in ((0, prob0), (1, prob1)):
                act.wait_ge(sem("att_nmax"), t + 1)
                for h in range(AH):
                    act.activation(prob[:, h], prob[:, h], ACT.Exp, scale=A_SCALE, bias=nmax[:, t, h:h + 1],
                                   accum_out=psumm[:, t, h:h + 1]).then_inc(sem("prob_exp"), 1)
            act.wait_ge(sem("pT_ps"), 1)
            act.activation(pT0[:, :, 0:P], tp[:, 0:2].rearrange("p b (h q) -> p (b h) q", h=4), ACT.Copy)\
               .then_inc(sem("pT"), 1)
            act.wait_ge(sem("pT_ps"), 3)
            act.activation(pT1[:], acc0[:].rearrange("p b (h q) -> p (b h) q", h=4), ACT.Copy)\
               .then_inc(sem("pT"), 1)
            for h in range(AH):
                act.wait_ge(sem("olat_ps"), h + 1)
                act.activation(olatT[:, :, h, :], halves((acc1[:, 0], acc1[:, 1], tp[:, 0], tp[:, 1])[h % 4]),
                               ACT.Copy).then_inc(sem("olat"), 1)
                if h > 0:
                    oT_hi(act, h - 1)
            oT_hi(act, AH - 1)
            if upto < 3:
                return

            act.wait_ge(sem("gate_in"), 2)
            act.wait_ge(sem("delta_gains"), 48)
            act.activation(sm("ex"), sm("ax"), ACT.Exp, scale=-1.0).then_inc(sem("gate_act"), 1)
            act.activation(alog[:], alog[:], ACT.Exp).then_inc(sem("gate_act"), 1)
            act.activation(sm("tb"), zab[:, :, BW + BH:BW + 2 * BH], ACT.Tanh, scale=0.5)\
               .then_inc(sem("gate_act"), 1)
            act.activation(sq[:], qkvT[:, 0:2 * BH, :], ACT.Square).then_inc(sem("sq"), 1)
            act.wait_ge(sem("gate_act"), 1)
            act.activation(sm("spl"), sm("ex"), ACT.Ln, bias=1.0).then_inc(sem("gate_act"), 1)
            act.wait_ge(sem("cum_ps"), 1)
            for n, name in enumerate(("eg", "ekd", "cd0", "cd1")):
                act.activation(sm(name).rearrange("p t h -> p (t h)"), tp[:, 0, 16 * n:16 * n + 16], ACT.Exp)\
                   .then_inc(sem("decays"), 1)
            for n, (t, hh) in enumerate(GROUPS):
                act.wait_ge(sem("dT_diff"), G8 * (n + 1))
                act.activation(group(dT, t, hh), group(dT, t, hh), ACT.Exp).then_inc(sem("dT"), 1)
            for n, (t, hh) in enumerate(GROUPS):
                act.wait_ge(sem("kbT_ps"), n + 1)
                act.activation(group(kbT, t, hh), heads4(bankF(n)), ACT.Copy).then_inc(sem("kbT"), 1)
            act.activation(thz, zab[:, :, 0:BW], ACT.Tanh, scale=0.5).then_inc(sem("thz"), 1)
            for n, (t, hh) in enumerate(GROUPS):
                act.wait_ge(sem("x0_ps"), n + 1)
                act.activation(group(xinv, t, hh), heads4(bankE(n)), ACT.Copy).then_inc(sem("x0"), 1)
            for lvl in range(1, LEVELS + 1):
                for n, (t, hh) in enumerate(GROUPS):
                    act.wait_ge(sem("t1_ps"), 4 * (lvl - 1) + n + 1)
                    act.activation(group(t1, t, hh), heads4(bankF(n)), ACT.Copy).then_inc(sem("t1"), 1)
            for n, (t, hh) in enumerate(GROUPS):
                act.wait_ge(sem("kcd_ps"), n + 1)
                act.activation(group(nkcdT, t, hh), heads4(bankF(n)), ACT.Copy, scale=-1.0)\
                   .then_inc(sem("nkcd"), 1)
            for n in range(2 * T):
                rows = slice(CHR * (n % 2), CHR * (n % 2) + CHR)
                for b in range(2):
                    act.wait_ge(sem("vn_ps"), 2 * n + b + 1)
                    act.activation(vnew[rows, 4 * b:4 * b + 4, :], heads4(tp[rows, b]), ACT.Copy)\
                       .then_inc(sem("vnew"), 1)
            junk = t1
            for t in range(T):
                act.wait_ge(sem("o_sum"), 4 * t + 4)
                for h in range(BH):
                    act.activation(junk[:, t, h], oy[:, t, h], ACT.Square, accum_out=sm("sso")[:, t, h:h + 1])\
                       .then_inc(sem("o_ss"), 1)
            for q in range(2):
                act.wait_ge(sem("yT_ps"), q + 1)
                act.activation(xT[:, AH + 4 * q:AH + 4 * q + 4, 0, :], (yT_banks(q)), ACT.Copy)\
                   .then_inc(sem("y_hi"), 1)
            if upto < 9:
                return
            with act.Fori(0, OUT_CHUNKS) as c:
                for u in range(LEAD, KU + LEAD):
                    split_hi(act, WO, c, u)
            to_xT_act(act, 2)

        CHR = P // 2
        thz = thz_sb[:]
        z_part = zab[:, :, 0:BW]

        def yT_banks(q):
            return (acc0, acc1)[q][:].rearrange("p b (k s) -> p (b k) s", k=2)

        def o_bank(h):
            return (acc0[:, 0], acc0[:, 1], tp[:, 2], tp[:, 3])[h % 4][:, 0:S]

        def oT_hi(act, h):
            act.wait_ge(sem("oT_ps"), h + 1)
            act.activation(xT[:, h, 0, :], o_bank(h), ACT.Copy).then_inc(sem("oT_hi"), 1)

        def mixer_dve(dve):
            with dve.Fori(0, A_ITERS) as c:
                for u in range(LEAD, KU + LEAD):
                    split_lo(dve, WA, c, u)
            for t in range(T):
                dve.wait_ge(acc0_free[t], n0[WB])
            key = slice(QR + KR, QR + KR + ID)
            for t in range(T):
                dve.bn_stats(kstats[:, t], lat[:, t, key]).then_inc(sem("k_stats"), 1)
            for t in range(T):
                dve.wait_ge(sem("k_stats"), t + 1)
                dve.bn_aggr(kmv[:, t], kstats[:, t]).then_inc(sem("k_mv"), 1)
            dve.tensor_scalar(widx[:], lat[:, :, QR + KR + ID:A_COLS], W_SCALE, None, ALU.mult)\
               .then_inc(sem("widx"), 1)
            dve.wait_ge(sem("lat_rs"), 4)
            dve.wait_ge(sem("latent_gains"), 64)
            for t in range(T):
                dve.scalar_tensor_tensor(out=lat[:, t, key], in0=lat[:, t, key], scalar=kmv[:, t, 0:1],
                                         in1=ki_g[:], op0=ALU.subtract, op1=ALU.mult).then_inc(sem("k_mid"), 1)
            for t in range(T):
                dve.scalar_tensor_tensor(out=lat[:, t, 0:QR], in0=lat[:, t, 0:QR], scalar=rs[:, 0, t:t + 1],
                                         in1=cq_g[:], op0=ALU.mult, op1=ALU.mult).then_inc(sem("lat_norm"), 1)
                dve.scalar_tensor_tensor(out=ckv[:, t], in0=lat[:, t, QR:QR + KR], scalar=rs[:, 1, t:t + 1],
                                         in1=ckv_g[:], op0=ALU.mult, op1=ALU.mult).then_inc(sem("lat_norm"), 1)
                dve.wait_ge(sem("k_mid"), t + 1)
                dve.scalar_tensor_tensor(out=lat[:, t, key], in0=lat[:, t, key], scalar=rs[:, 2, t:t + 1],
                                         in1=ki_b[:], op0=ALU.mult, op1=ALU.add).then_inc(sem("lat_norm"), 1)
            dve.wait_ge(sem("cw"), 1)

            def conv(c, half):
                dve.wait_ge(acc0_free[half], c + (n0[WB] + 1))
                for step in range(TAPS):
                    tap = TAPS - 1 - step
                    for j in (2 * half, 2 * half + 1):
                        dst = qkvT[:, bass.ds(4 * c + j, 1), :].rearrange("p a s -> p (a s)")
                        w = cw[:, tap, bass.ds(4 * c + j, 1)]
                        if step == 0:
                            dve.tensor_scalar(dst, xs[:, j, tap:tap + S], w, None, ALU.mult)\
                               .then_inc(sem("conv_sum"), 1)
                        else:
                            dve.wait_ge(sem("conv_sum"), c * 16 + 8 * half + 2 * (step - 1) + j % 2 + 1)
                            dve.scalar_tensor_tensor(out=dst, in0=xs[:, j, tap:tap + S], scalar=w, in1=dst,
                                                     op0=ALU.mult, op1=ALU.add).then_inc(sem("conv_sum"), 1)

            def conv_silu(c):
                dve.wait_ge(sem("qkv_tanh"), c + 1)
                dve.scalar_tensor_tensor(out=qkvT[:, bass.ds(4 * c, 4), :], in0=th[:], scalar=1.0,
                                         in1=qkvT[:, bass.ds(4 * c, 4), :], op0=ALU.add, op1=ALU.mult)\
                   .then_inc(sem("xs_th_free"), 1)

            def qkv_chunk(c, prev):
                for u in range(LEAD, KU + LEAD):
                    split_lo(dve, WB, c, u)
                    if u == 2 and prev:
                        conv(c - 1, 1)
                    if u == 5 and prev:
                        conv_silu(c - 1)
                conv(c, 0)

            qkv_chunk(0, False)
            with dve.Fori(1, B_ITERS) as c:
                qkv_chunk(c, True)
            conv(B_ITERS - 1, 1)
            conv_silu(B_ITERS - 1)
            dve.wait_ge(sem("cqT_hi"), 1)
            dve.tensor_tensor(cqT[:, :, 1, :], tp_pair(0), cqT[:, :, 0, :].bitcast(F32), ALU.subtract)\
               .then_inc(sem("cqT_lo"), 1)
            with dve.Fori(0, C_ITERS) as c:
                for u in range(LEAD, KU + LEAD):
                    split_lo(dve, WC, c, u)
            for p, chunks in ((WQI, QI_CHUNKS), (WUQ, UQ_CHUNKS)):
                for u in range(LEAD, chunks * QU + LEAD):
                    split_lo(dve, p, 0, u)
            if upto < 2:
                return
            dve.wait_ge(sem("widx"), 1)
            dve.wait_ge(sem("lat_ps"), 1)
            dve.wait_ge(sem("xs_th_free"), B_ITERS + 1)
            for i in range(SCORE_ITEMS):
                t, n = i % T, (i % T + 1) * P
                dve.wait_ge(sem("relu"), i + 1)
                for hh in range(2):
                    h = 2 * (i // T) + hh
                    src, dst, w = relu[:, i % 2, hh, 0:n], score[:, t, 0:n], widx[:, t, h:h + 1]
                    before = 2 * i if hh else 2 * (i - T) + 1
                    if h == 0:
                        dve.tensor_scalar(dst, src, w, None, ALU.mult).then_inc(sem("score_acc"), 1)
                    else:
                        dve.wait_ge(sem("score_acc"), before + 1)
                        dve.scalar_tensor_tensor(out=dst, in0=src, scalar=w, in1=dst, op0=ALU.mult, op1=ALU.add)\
                           .then_inc(sem("score_acc"), 1)
            dve.wait_ge(sem("score_masked"), T)
            for r in range(KEPT // 8):
                for t in range(T):
                    n = (t + 1) * P
                    src = (work if r else score)[:, t, 0:n]
                    wait(dve, sem("taken"), T * (r - 1) + t + 1)
                    dve.max(top8[:, t], src).then_inc(sem("top8"), 1)
                for t in range(T):
                    n = (t + 1) * P
                    src = (work if r else score)[:, t, 0:n]
                    dve.wait_ge(sem("top8"), T * r + t + 1)
                    dve.match_replace(out=work[:, t, 0:n], in_to_replace=top8[:, t], in_values=src,
                                      imm_value=TAKEN).then_inc(sem("taken"), 1)
            dve.wait_ge(sem("ndist"), 2)
            for t in range(T):
                n = (t + 1) * P
                dve.wait_ge(sem("taken"), T * (KEPT // 8 - 1) + t + 1)
                dve.tensor_tensor(sel[:, t, 0:n], work[:, t, 0:n], score[:, t, 0:n], ALU.not_equal)\
                   .then_inc(sem("sel_raw"), 1)
            for t in range(T):
                n = (t + 1) * P
                dve.wait_ge(sem("sel_raw"), t + 1)
                dve.tensor_scalar(sel[:, t, 0:n], sel[:, t, 0:n], 1.0, -NEG, ALU.subtract, ALU.mult)\
                   .then_inc(sem("sel_raw"), 1)
            for a in range(AH):
                t, hp = a // 4, a % 4
                n = (t + 1) * P
                dve.wait_ge(sem("att_ps"), a + 1)
                for hh in range(2):
                    h = 2 * hp + hh
                    slope = 2.0 ** (-8.0 * (h + 1.0) / AH)
                    dve.scalar_tensor_tensor(out=(prob0, prob1)[t][:, h, :], in0=ndist[:, t, 0:n],
                                             scalar=slope / A_SCALE, in1=halves(bankE(a % 4))[:, hh, 0:n],
                                             op0=ALU.mult, op1=ALU.add).then_inc(sem("att_z"), 1)
            dve.wait_ge(sem("sel"), T)
            for t, prob in ((0, prob0), (1, prob1)):
                n = (t + 1) * P
                dve.wait_ge(sem("att_z"), AH * (t + 1))
                dve.tensor_tensor(prob[:], prob[:], sel[:, t, 0:n].unsqueeze(1).to_broadcast([P, AH, n]), ALU.add)\
                   .then_inc(sem("att_sel"), 1)
                dve.wait_ge(sem("att_sel"), t + 1)
                dve.reduce_max(amax[:, t], prob[:], AX_X).then_inc(sem("att_max"), 1)
                dve.wait_ge(sem("att_max"), t + 1)
                dve.tensor_scalar(nmax[:, t], amax[:, t], -A_SCALE, None, ALU.mult).then_inc(sem("att_nmax"), 1)
            for t, prob in ((0, prob0), (1, prob1)):
                n = (t + 1) * P
                dve.wait_ge(sem("prob_exp"), AH * (t + 1))
                dve.reciprocal(pinv[:, t], psumm[:, t]).then_inc(sem("pinv"), 1)
                dve.wait_ge(sem("pinv"), t + 1)
                dve.tensor_tensor(prob[:], prob[:], pinv[:, t].unsqueeze(2).to_broadcast([P, AH, n]), ALU.mult)\
                   .then_inc(sem("prob"), 1)
            dve.wait_ge(sem("pT_ps"), 2)
            dve.tensor_copy(pT0[:, :, P:S], tp[:, 2:4].rearrange("p b (h q) -> p (b h) q", h=4))\
               .then_inc(sem("pT"), 1)
            for h in range(AH):
                dve.wait_ge(sem("oT_hi"), h + 1)
                dve.tensor_tensor(xT[:, h, 1, :], o_bank(h), xT[:, h, 0, :].bitcast(F32), ALU.subtract)\
                   .then_inc(sem("oT_lo"), 1)
            if upto < 3:
                return

            dve.wait_ge(sem("delta_gains"), 48)
            a_part = zab[:, :, BW:BW + BH]
            dve.tensor_tensor(sm("xa"), a_part, dtb[:].unsqueeze(1).to_broadcast([P, T, BH]), ALU.add)\
               .then_inc(sem("gate_in"), 1)
            dve.wait_ge(sem("gate_in"), 1)
            dve.scalar_tensor_tensor(out=sm("ax"), in0=sm("xa"), scalar=-1.0, in1=sm("xa"), op0=ALU.mult,
                                     op1=ALU.max).then_inc(sem("gate_in"), 1)
            dve.wait_ge(sem("gate_act"), 4)
            dve.scalar_tensor_tensor(out=sm("sp"), in0=sm("xa"), scalar=0.0, in1=sm("spl"), op0=ALU.max,
                                     op1=ALU.add).then_inc(sem("gate_mid"), 1)
            dve.wait_ge(sem("gate_mid"), 1)
            dve.scalar_tensor_tensor(out=sm("g"), in0=sm("sp"), scalar=-1.0,
                                     in1=alog[:].unsqueeze(1).to_broadcast([P, T, BH]), op0=ALU.mult,
                                     op1=ALU.mult).then_inc(sem("g"), 1)
            dve.tensor_scalar(sm("beta"), sm("tb"), 0.5, 0.5, ALU.mult, ALU.add).then_inc(sem("beta"), 1)
            dve.wait_ge(sem("ss_ps"), 1)
            dve.tensor_copy(small[:, NAMES.index("rq"):NAMES.index("rq") + 2].rearrange("p a t h -> p (a t h)"),
                            tp[:, 1, 0:2 * T * BH]).then_inc(sem("qk_ss"), 1)
            dve.wait_ge(sem("decays"), 4)
            dve.tensor_copy(sm("gc").rearrange("p t h -> p (t h)"), tp[:, 0, 0:T * BH]).then_inc(sem("gc"), 1)
            dve.wait_ge(sem("gc"), 1)
            dve.wait_ge(sem("masks"), MASKS)
            for n, (t, hh) in enumerate(GROUPS):
                dve.wait_ge(sem("gbc_ps"), n + 1)
                for k in range(G8):
                    h = G8 * hh + k
                    dve.scalar_tensor_tensor(out=dT[:, t, h], in0=bankE(n)[:, k * P:k * P + P],
                                             scalar=sm("gc")[:, t, h:h + 1], in1=not_ahead[:],
                                             op0=ALU.subtract, op1=ALU.add).then_inc(sem("dT_diff"), 1)
            dve.wait_ge(sem("qk_r"), 2)
            dve.wait_ge(sem("beta"), 1)
            dve.wait_ge(sem("decays"), 4)
            dve.tensor_tensor(sm("c1"), sm("rk"), sm("beta"), ALU.mult).then_inc(sem("factors"), 1)
            dve.tensor_tensor(sm("c3"), sm("rk"), sm("ekd"), ALU.mult).then_inc(sem("factors"), 1)
            dve.tensor_scalar(sm("vbs"), sm("beta"), 0.5, None, ALU.mult).then_inc(sem("factors"), 1)
            dve.tensor_scalar(sm("qs"), sm("rq"), BD ** -0.5, None, ALU.mult).then_inc(sem("factors"), 1)
            dve.wait_ge(sem("factors"), 1)
            dve.tensor_tensor(sm("c2"), sm("c1"), sm("eg"), ALU.mult).then_inc(sem("factors"), 1)
            dve.wait_ge(sem("factors"), 5)
            for n, (t, hh) in enumerate(GROUPS):
                dve.wait_ge(sem("k_ps"), n + 1)
                for dst, f in ((kb, "c1"), (kbeg, "c2"), (kdec, "c3")):
                    dve.tensor_tensor(group(dst, t, hh), heads4(bankF(n)), sm_group(f, t, hh), ALU.mult)\
                       .then_inc(sem("k_tok"), 1)
            for n, (t, hh) in enumerate(GROUPS):
                dve.wait_ge(sem("v_ps"), n + 1)
                dve.tensor_tensor(group(vb, t, hh), heads4(bankE(n)), sm_group("vbs", t, hh), ALU.mult)\
                   .then_inc(sem("v_tok"), 1)
            for n, (t, hh) in enumerate(GROUPS):
                for name, dst, bank in (("kk", aT, bankE(n)), ("qk", aiT, bankF(n))):
                    dve.wait_ge(sem(name + "_ps"), n + 1)
                    dve.wait_ge(sem("dT"), n + 1)
                    for k in range(G8):
                        h = G8 * hh + k
                        dve.scalar_tensor_tensor(out=dst[:, t, h], in0=bank[:, k * P:k * P + P],
                                                 scalar=sm("rk")[:, t, h:h + 1], in1=dT[:, t, h],
                                                 op0=ALU.mult, op1=ALU.mult).then_inc(sem(name + "_m"), 1)

            def mask_level(lvl, n, t, hh):
                wait(dve, sem("y_up"), 4 * lvl)
                dve.tensor_tensor(group(lev, t, hh), group(aT, t, hh),
                                  pair_mask[:, lvl].unsqueeze(1).to_broadcast([P, G8, P]), ALU.mult)\
                   .then_inc(sem("lev"), 1)

            dve.wait_ge(sem("kk_m"), T * BH)
            dve.wait_ge(sem("qk_ps"), 4)
            dve.wait_ge(sem("v_ps"), 4)
            for n, (t, hh) in enumerate(GROUPS):
                mask_level(0, n, t, hh)
            for n, (t, hh) in enumerate(GROUPS):
                dve.wait_ge(sem("lev"), n + 1)
                dve.tensor_tensor(group(yinv, t, hh), ident[:].unsqueeze(1).to_broadcast([P, G8, P]),
                                  group(lev, t, hh), ALU.subtract).then_inc(sem("y_up"), 1)
            dve.wait_ge(sem("thz"), 1)
            dve.scalar_tensor_tensor(out=z_part, in0=thz, scalar=1.0, in1=z_part, op0=ALU.add, op1=ALU.mult)\
               .then_inc(sem("z"), 1)
            dve.wait_ge(sem("z"), 1)
            for t in range(T):
                zt = zab[:, t, 0:BW].rearrange("p (h d) -> p h d", d=BD)
                dve.tensor_tensor(zt, zt, og[:].unsqueeze(1).to_broadcast([P, BH, BD]), ALU.mult)\
                   .then_inc(sem("z"), 1)
            for lvl in range(1, LEVELS + 1):
                for n, (t, hh) in enumerate(GROUPS):
                    mask_level(lvl, n, t, hh)
                for n, (t, hh) in enumerate(GROUPS):
                    dve.wait_ge(sem("xy_ps"), 4 * (lvl - 1) + n + 1)
                    if lvl == 1:
                        dve.wait_ge(sem("x0"), n + 1)
                    if lvl < LEVELS:
                        dve.tensor_tensor(group(xinv, t, hh), group(xinv, t, hh), heads4(bankE(2 * (n % 2))),
                                          ALU.subtract).then_inc(sem("x_up"), 1)
                    dve.tensor_tensor(group(yinv, t, hh), group(yinv, t, hh), heads4(bankE(2 * (n % 2) + 1)),
                                      ALU.subtract).then_inc(sem("y_up"), 1)
            dve.wait_ge(sem("state0"), 1)
            for n in range(2 * T):
                t, half = n // 2, n % 2
                if n < 2 * T - 1:
                    for h in range(BH):
                        if h % 4 == 0:
                            dve.wait_ge(sem("st_ps"), 2 * n + h // 4 + 1)
                        wait(dve, sem("state"), BH * (n - 1) + h + 1)
                        dve.scalar_tensor_tensor(out=state[:, h], in0=state[:, h],
                                                 scalar=sm(f"cd{half}")[:, t, h:h + 1],
                                                 in1=tp[:, 2 + h // 4, (h % 4) * P:(h % 4) * P + P],
                                                 op0=ALU.mult, op1=ALU.add).then_inc(sem("state"), 1)
                if half == 1:
                    dve.wait_ge(sem("o_ps"), n + 1)
                    for b in range(2):
                        dve.tensor_tensor(group(oy, t, b), heads4(acc0[:, b]), sm_group("eg", t, b), ALU.mult)\
                           .then_inc(sem("o_sum"), 1)
                    for b in range(2):
                        dve.wait_ge(sem("o_sum"), 4 * t + b + 1)
                        dve.tensor_tensor(group(oy, t, b), group(oy, t, b), heads4(acc1[:, b]), ALU.add)\
                           .then_inc(sem("o_sum"), 1)
            dve.wait_ge(sem("o_ss"), T * BH)
            dve.scalar_tensor_tensor(out=sm("a1"), in0=sm("sso"), scalar=1.0 / BD, in1=sm("qs"), op0=ALU.mult,
                                     op1=ALU.mult).then_inc(sem("o_a1"), 1)
            dve.wait_ge(sem("o_a1"), 1)
            dve.tensor_tensor(sm("a2"), sm("a1"), sm("qs"), ALU.mult).then_inc(sem("o_a2"), 1)
            dve.wait_ge(sem("o_r"), 2)
            dve.scalar_tensor_tensor(out=sm("co"), in0=sm("ro"), scalar=0.5, in1=sm("qs"), op0=ALU.mult,
                                     op1=ALU.mult).then_inc(sem("o_co"), 1)
            dve.wait_ge(sem("o_co"), 1)
            dve.wait_ge(sem("o_sum"), 8)
            for n, (t, hh) in enumerate(GROUPS):
                dve.tensor_tensor(group(oy, t, hh), group(oy, t, hh), sm_group("co", t, hh), ALU.mult)\
                   .then_inc(sem("y_mid"), 1)
            dve.wait_ge(sem("z"), 1 + T)
            for n, (t, hh) in enumerate(GROUPS):
                dve.wait_ge(sem("y_mid"), n + 1)
                zg = zab[:, t, BW // 2 * hh:BW // 2 * (hh + 1)].rearrange("p (h d) -> p h d", d=BD)
                dve.tensor_tensor(group(oy, t, hh), group(oy, t, hh), zg, ALU.mult).then_inc(sem("y"), 1)
            for q in range(2):
                dve.wait_ge(sem("y_hi"), q + 1)
                rows = xT[:, AH + 4 * q:AH + 4 * q + 4, :, :]
                dve.tensor_tensor(rows[:, :, 1, :], yT_banks(q), rows[:, :, 0, :].bitcast(F32), ALU.subtract)\
                   .then_inc(sem("y_lo"), 1)
            if upto < 9:
                return
            with dve.Fori(0, OUT_CHUNKS) as c:
                for u in range(LEAD, KU + LEAD):
                    split_lo(dve, WO, c, u)
                into_resid(dve, WO, c, 1.0 / ALPHA, 1, KU)
            norm_dve(dve, 1, True)

        def mixer_pe(pe):
            with pe.Fori(0, A_ITERS) as c:
                for u in range(KU):
                    pe.wait_ge(sem("xT_lo"), 4 + u // 2 + 1)
                    unit_mm(pe, WA, c, u, acc0, acc0_free, c + n0[WA], "w", xT, 2 * u, u == 0, u == KU - 1,
                            acc0a_done)
            with pe.Fori(0, B_ITERS) as c:
                for u in range(KU):
                    unit_mm(pe, WB, c, u, acc0, acc0_free, c + n0[WB], "x", xT, 2 * u, u == 0, u == KU - 1,
                            acc0a_done)
            pe.wait_ge(sem("lat_norm"), 3 * T)
            for t in range(T):
                for k in range(QT):
                    pe.transpose(tp_pair(0)[:, k, t * P:t * P + P], lat[:, t, k * P:k * P + P], ident[:])
                for k in range(RT):
                    pe.transpose(halves(tp[:, 2])[:, k, t * P:t * P + P], ckv[:, t, k * P:k * P + P], ident[:])
                ins = pe.transpose(tp[:, 3, t * P:t * P + P], lat[:, t, QR + KR:QR + KR + ID], ident[:])
            ins.then_inc(sem("lat_ps"), 1)
            with pe.Fori(0, C_ITERS) as c:
                for u in range(KU):
                    unit_mm(pe, WC, c, u, acc0, acc0_free, c + n0[WC], "w", xT, 2 * u, u == 0, u == KU - 1,
                            acc0a_done)
            pe.wait_ge(sem("cqT_lo"), 1)
            for p, chunks in ((WQI, QI_CHUNKS), (WUQ, UQ_CHUNKS)):
                for j in range(chunks):
                    acc, free = ((acc0, acc0_free), (acc1, acc1_free))[j % 2]
                    n = (n0, n1)[j % 2][p] + j // 2
                    for u in range(QU):
                        unit_mm(pe, p, 0, j * QU + u, acc, free, n, "x", cqT, 2 * u, u == 0, u == QU - 1,
                                acc0a_done if j % 2 == 0 else None)
            if upto < 2:
                return
            pe.wait_ge(sem("latT"), 2)
            for half in range(2):
                pe.wait_ge(acc0_free[half], n0[WO])
                pe.wait_ge(acc1_free[half], n1[F2GU])
            for i in range(SCORE_ITEMS):
                t, n = i % T, (i % T + 1) * P
                wait(pe, sem("relu"), i - 3)
                for hh in range(2):
                    h = 2 * (i // T) + hh
                    ins = pe.matmul(halves(tp[:, i % 4])[:, hh, 0:n], qidxT[:, h, t * P:t * P + P], kidxT[:, 0:n],
                                    start=True, stop=True)
                ins.then_inc(sem("score_ps"), 1)
            pe.wait_ge(sem("wuk"), 16)
            for h in range(AH):
                if h < 4:
                    pe.wait_ge(sem("relu"), SCORE_ITEMS - 3 + h)
                else:
                    pe.wait_ge(sem("qlat"), h - 3)
                for r in range(RT):
                    ins = pe.matmul(halves(tp[:, h % 4])[:, r, :], wuk[:, h, r * P:r * P + P], qT[:, h, :],
                                    start=True, stop=True)
                ins.then_inc(sem("qlat_ps"), 1)
            for a in range(AH):
                t, hp = a // 4, a % 4
                n = (t + 1) * P
                wait(pe, sem("att_z"), 2 * (a - 3))
                for hh in range(2):
                    h = 2 * hp + hh
                    if t == 0:
                        pe.wait_ge(sem("qlat"), h + 1)
                    for r in range(RT):
                        ins = pe.matmul(halves(bankE(a % 4))[:, hh, 0:n], qlatT[:, r, h, t * P:t * P + P],
                                        ckvT[:, r, 0:n], start=r == 0, stop=r == RT - 1)
                ins.then_inc(sem("att_ps"), 1)
            pe.wait_ge(sem("qlat"), AH)
            pe.wait_ge(sem("prob"), 1)
            for h in range(AH):
                ins = pe.transpose(tp[:, h // 4, (h % 4) * P:(h % 4) * P + P], prob0[:, h, :], ident[:])
            ins.then_inc(sem("pT_ps"), 1)
            pe.wait_ge(sem("prob"), 2)
            for h in range(AH):
                ins = pe.transpose(tp[:, 2 + h // 4, (h % 4) * P:(h % 4) * P + P], prob1[:, h, 0:P], ident[:])
            ins.then_inc(sem("pT_ps"), 1)
            pe.wait_ge(sem("att_z"), 2 * AH)
            for h in range(AH):
                ins = pe.transpose(acc0[:, h // 4, (h % 4) * P:(h % 4) * P + P], prob1[:, h, P:S], ident[:])
            ins.then_inc(sem("pT_ps"), 1)
            pe.wait_ge(sem("pT"), 3)
            pe.wait_ge(sem("wuv"), 16)

            def o_head(h):
                pe.wait_ge(sem("olat"), h + 1)
                wait(pe, sem("oT_lo"), h - 3)
                for r in range(RT):
                    ins = pe.matmul(o_bank(h), wuv[:, h, r, :], olatT[:, r, h, :], start=r == 0, stop=r == RT - 1)
                ins.then_inc(sem("oT_ps"), 1)

            for h in range(AH):
                wait(pe, sem("olat"), h - 3)
                bank = halves((acc1[:, 0], acc1[:, 1], tp[:, 0], tp[:, 1])[h % 4])
                for r in range(RT):
                    rc = slice(r * P, r * P + P)
                    pe.matmul(bank[:, r, 0:P], ckv[:, 0, rc], pT0[:, h, 0:P], start=True, stop=True)
                    pe.matmul(bank[:, r, P:S], ckv[:, 0, rc], pT0[:, h, P:S], start=True, stop=False)
                    ins = pe.matmul(bank[:, r, P:S], ckv[:, 1, rc], pT1[:, h, :], start=False, stop=True)
                ins.then_inc(sem("olat_ps"), 1)
                if h > 0:
                    o_head(h - 1)
            o_head(AH - 1)
            if upto < 3:
                return

            pe.wait_ge(sem("oT_lo"), AH)
            pe.wait_ge(sem("olat"), AH)
            pe.wait_ge(sem("ones"), 1)
            pe.wait_ge(sem("sq"), 1)
            for i in range(2):
                for t in range(T):
                    for h in range(BH):
                        ins = pe.matmul(tp[:, 1, (i * T + t) * BH + h:(i * T + t) * BH + h + 1],
                                        sq[:, i * BH + h, t * P:t * P + P], ones[:, 0:1], start=True, stop=True)
            ins.then_inc(sem("ss_ps"), 1)
            pe.wait_ge(sem("g"), 1)
            pe.wait_ge(sem("masks"), MASKS)
            g_all = sm("g").rearrange("p t h -> p (t h)")
            for n, m in enumerate((up_to[:], later[:], in_half[:, 0], in_half[:, 1])):
                ins = pe.matmul(tp[:, 0, 16 * n:16 * n + 16], m, g_all, start=True, stop=True)
            ins.then_inc(sem("cum_ps"), 1)
            for n, (t, hh) in enumerate(GROUPS):
                for k in range(G8):
                    h = G8 * hh + k
                    ins = pe.matmul(bankE(n)[:, k * P:k * P + P], sm("g")[:, t, h:h + 1].to_broadcast([P, P]),
                                    up_to[:], start=True, stop=True)
                ins.then_inc(sem("gbc_ps"), 1)
            for n, (t, hh) in enumerate(GROUPS):
                if n == 0:
                    pe.wait_ge(sem("decays"), 4)
                    pe.wait_ge(sem("gc"), 1)
                if n == 1:
                    pe.wait_ge(sem("qk_ss"), 1)
                for k in range(G8):
                    ins = pe.transpose(bankF(n)[:, k * P:k * P + P], kT_of(G8 * hh + k, t), ident[:])
                ins.then_inc(sem("k_ps"), 1)
            for n, (t, hh) in enumerate(GROUPS):
                pe.wait_ge(sem("dT_diff"), G8 * (n + 1))
                for k in range(G8):
                    ins = pe.transpose(bankE(n)[:, k * P:k * P + P], vT_of(G8 * hh + k, t), ident[:])
                ins.then_inc(sem("v_ps"), 1)
            for n, (t, hh) in enumerate(GROUPS):
                pe.wait_ge(sem("k_tok"), 3 * (n + 1))
                for k in range(G8):
                    ins = pe.transpose(bankF(n)[:, k * P:k * P + P], kb[:, t, G8 * hh + k], ident[:])
                ins.then_inc(sem("kbT_ps"), 1)
            for n, (t, hh) in enumerate(GROUPS):
                pe.wait_ge(sem("kbT"), n + 1)
                pe.wait_ge(sem("v_tok"), n + 1)
                for k in range(G8):
                    h = G8 * hh + k
                    ins = pe.matmul(bankE(n)[:, k * P:k * P + P], kT_of(h, t), kbT[:, t, h], start=True, stop=True)
                ins.then_inc(sem("kk_ps"), 1)
                for k in range(G8):
                    h = G8 * hh + k
                    ins = pe.matmul(bankF(n)[:, k * P:k * P + P], kT_of(h, t), qT_of(h, t), start=True, stop=True)
                ins.then_inc(sem("qk_ps"), 1)
            for n, (t, hh) in enumerate(GROUPS):
                pe.wait_ge(sem("y_up"), n + 1)
                for k in range(G8):
                    ins = pe.transpose(bankE(n)[:, k * P:k * P + P], yinv[:, t, G8 * hh + k], ident[:])
                ins.then_inc(sem("x0_ps"), 1)

            def t1_mm(lvl, n):
                t, hh = GROUPS[n]
                pe.wait_ge(sem("lev"), 4 * lvl + n + 1)
                if lvl == 1:
                    pe.wait_ge(sem("x0"), n + 1)
                    pe.wait_ge(sem("qk_m"), G8 * (n + 1))
                else:
                    pe.wait_ge(sem("x_up"), 4 * (lvl - 2) + n + 1)
                for k in range(G8):
                    h = G8 * hh + k
                    ins = pe.matmul(bankF(n)[:, k * P:k * P + P], lev[:, t, h], xinv[:, t, h],
                                    start=True, stop=True)
                ins.then_inc(sem("t1_ps"), 1)

            def xy_mm(lvl, n):
                t, hh = GROUPS[n]
                pe.wait_ge(sem("t1"), 4 * (lvl - 1) + n + 1)
                if lvl == 1 and n == 0:
                    pe.wait_ge(sem("x0"), 4)
                pe.wait_ge(sem("y_up"), 4 * lvl + n - 1 if (lvl > 1 or n > 1) else 4)
                for k in range(G8):
                    h, cols = G8 * hh + k, slice(k * P, k * P + P)
                    if lvl < LEVELS:
                        pe.matmul(bankE(2 * (n % 2))[:, cols], yinv[:, t, h], t1[:, t, h], start=True, stop=True)
                    ins = pe.matmul(bankE(2 * (n % 2) + 1)[:, cols], t1[:, t, h], yinv[:, t, h],
                                    start=True, stop=True)
                ins.then_inc(sem("xy_ps"), 1)

            for lvl in range(1, LEVELS + 1):
                t1_mm(lvl, 0)
                t1_mm(lvl, 1)
                xy_mm(lvl, 0)
                t1_mm(lvl, 2)
                xy_mm(lvl, 1)
                t1_mm(lvl, 3)
                xy_mm(lvl, 2)
                xy_mm(lvl, 3)
            for n, (t, hh) in enumerate(GROUPS):
                pe.wait_ge(sem("y_up"), 4 * LEVELS + n + 1)
                for k in range(G8):
                    h = G8 * hh + k
                    ins = pe.matmul(bankF(n)[:, k * P:k * P + P], kbeg[:, t, h], yinv[:, t, h],
                                    start=True, stop=True)
                ins.then_inc(sem("kcd_ps"), 1)
            pe.wait_ge(sem("nkcd"), 4)
            pe.wait_ge(sem("state0"), 1)
            for n in range(2 * T):
                t, half = n // 2, n % 2
                rows = slice(CHR * half, CHR * half + CHR)
                cols = slice(t * P + CHR * half, t * P + CHR * half + CHR)

                def head_cols(h):
                    return slice((h % 4) * P, (h % 4) * P + P)

                for h in range(BH):
                    wait(pe, sem("state"), BH * (n - 1) + h + 1)
                    if h % 4 == 0:
                        wait(pe, sem("vnew"), 2 * (n - 1) + h // 4 + 1)
                    o = tp[rows, h // 4, head_cols(h)]
                    pe.matmul(o, yinv[:, t, h, rows], vb[:, t, h], start=True, stop=False)
                    ins = pe.matmul(o, nkcdT[:, t, h, rows], state[:, h], start=False, stop=True)
                    if h % 4 == 3:
                        ins.then_inc(sem("vn_ps"), 1)
                if t > 0:
                    pe.wait_ge(sem("o_sum"), 4 * t)
                for h in range(BH):
                    ins = pe.matmul(acc0[rows, h // 4, head_cols(h)], qkvT[:, h, cols], state[:, h],
                                    start=True, stop=True)
                for h in range(BH):
                    if h % 4 == 0:
                        pe.wait_ge(sem("vnew"), 2 * n + h // 4 + 1)
                    if n < 2 * T - 1:
                        ins = pe.matmul(tp[:, 2 + h // 4, head_cols(h)], kdec[rows, t, h], vnew[rows, h],
                                        start=True, stop=True)
                        if h % 4 == 3:
                            ins.then_inc(sem("st_ps"), 1)
                for h in range(BH):
                    ins = pe.matmul(acc1[rows, h // 4, head_cols(h)], aiT[rows, t, h, rows], vnew[rows, h],
                                    start=True, stop=True)
                ins.then_inc(sem("o_ps"), 1)
            pe.wait_ge(sem("o_sum"), 8)
            for q in range(2):
                pe.wait_ge(sem("y"), 4)
                for k in range(4):
                    for t in range(T):
                        ins = pe.transpose(yT_banks(q)[:, k, t * P:t * P + P], oy[:, t, 4 * q + k], ident[:])
                ins.then_inc(sem("yT_ps"), 1)
            if upto < 9:
                return
            pe.wait_ge(sem("y_lo"), 2)
            with pe.Fori(0, OUT_CHUNKS) as c:
                for u in range(KU):
                    unit_mm(pe, WO, c, u, acc0, acc0_free, c + n0[WO], "w", xT, 2 * u, u == 0, u == KU - 1,
                            acc0a_done)
            to_xT_pe(pe, 2)

        block = ctx.enter_context(nc.Block())

        @block.sync
        def _(sp):
            x_v = x[0].rearrange("(t p) d -> p t d", p=P)
            for q in range(4):
                sp.dma_start(resid[:, :, q * BANK:(q + 1) * BANK], x_v[:, :, q * BANK:(q + 1) * BANK])\
                  .then_inc(sem(f"x_loaded{q}"), 16)
            ffn_loads(sp, 0, ffn1_w_gate[0], ffn1_w_up[0], ffn1_w_down[0])
            if upto < 1:
                v = w_in[0].rearrange("(k p) n -> p k n", p=P)
                for u in range(LEAD):
                    load_unit(sp, WA, 0, u, v[:, 2 * u:2 * u + 2, 0:A_W])
                return
            mixer_loads(sp)
            if upto < 9:
                return
            ffn_loads(sp, 1, ffn2_w_gate[0], ffn2_w_up[0], ffn2_w_down[0])
            out_v = out[0].rearrange("(t p) d -> p t d", p=P)
            for q in range(4):
                sp.wait_ge(sem("ln_out"), 16 + 2 * q + 2)
                sp.dma_start(out_v[:, :, q * BANK:(q + 1) * BANK], resid[:, :, q * BANK:(q + 1) * BANK])\
                  .then_inc(sem("stored"), 16)
            sp.wait_ge(sem("stored"), 64)

        @block.gpsimd
        def _(pool):
            pool.memset(ident[:], 1.0).then_inc(sem("ident"), 1)
            pool.memset(half_neg[:], -0.5).then_inc(sem("pow_ready"), 1)
            pool.wait_ge(sem("ident"), 1)
            pool.affine_select(out=ident[:], in_=ident[:], compare_op=ALU.is_equal, fill=0.0, base=0,
                               pattern=[[-1, P]], channel_multiplier=1).then_inc(sem("ident"), 1)
            pool.wait_ge(sem("pow_ready"), 1)
            pool.wait_ge(unit_used, st.index(F1D, OUT_CHUNKS - 1, KT // UNIT_KT))
            norm_gains(pool, ln1_g, ln1_b)
            norm_pool(pool, 0)
            if upto < 1:
                return
            mixer_pool(pool)
            if upto < 9:
                return
            pool.wait_ge(unit_used, st.index(F2D, OUT_CHUNKS - 1, KT // UNIT_KT))
            norm_gains(pool, ln3_g, ln3_b)
            norm_pool(pool, 2)

        @block.scalar
        def _(act):
            act.dma_start(cw_rows[:], conv_w[0].rearrange("a (t p) -> (a t) p", p=P)).then_inc(sem("cw_rows"), 16)
            to_xT_act(act, 0)
            act.wait_ge(sem("cw_ps"), 1)
            act.activation(cw[:].rearrange("p a t -> p (a t)"), acc1[:, 0, 0:TAPS * CONV_TILES], ACT.Copy)\
               .then_inc(sem("cw"), 1)
            for u in range(LEAD):
                split_hi(act, F1GU, 0, u)
            ffn_act(act, 0, False)
            to_xT_act(act, 1)
            if upto < 1:
                return
            mixer_act(act)
            if upto < 9:
                return
            ffn_act(act, 1, True)

        @block.vector
        def _(dve):
            for q in range(4):
                to_xT_dve_step(dve, 0, q)
            for u in range(LEAD):
                split_lo(dve, F1GU, 0, u)
            ffn_dve(dve, 0, False)
            norm_dve(dve, 0, True)
            if upto < 1:
                return
            mixer_dve(dve)
            if upto < 9:
                return
            ffn_dve(dve, 1, True)
            norm_dve(dve, 2, False)

        @block.tensor
        def _(pe):
            to_xT_pe(pe, 0)
            pe.wait_ge(sem("cw_rows"), 16)
            pe.transpose(acc1[:, 0, 0:TAPS * CONV_TILES], cw_rows[:], ident[0:TAPS * CONV_TILES, 0:TAPS * CONV_TILES])\
              .then_inc(sem("cw_ps"), 1)
            pe.wait_ge(sem("cw"), 1)
            ffn_pe(pe, 0)
            to_xT_pe(pe, 1)
            if upto < 1:
                return
            mixer_pe(pe)
            if upto < 9:
                return
            ffn_pe(pe, 1)

    if dump:
        dump(nc, locals())


_INS = ['x', 'ffn1_w_gate', 'ffn1_w_up', 'ffn1_w_down', 'ln1_g', 'ln1_b', 'w_in', 'q_norm_g', 'kv_norm_g',
        'w_uq', 'w_uk', 'w_uv', 'w_q_idx', 'k_idx_ln_g', 'k_idx_ln_b', 'conv_w', 'a_log', 'dt_bias', 'o_norm_g',
        'w_out', 'ln2_g', 'ln2_b', 'ffn2_w_gate', 'ffn2_w_up', 'ffn2_w_down', 'ln3_g', 'ln3_b']


def kernel(**inputs):
    import numpy as _np
    import concourse.bacc as _bacc
    from concourse import mybir as _mybir
    from concourse.bass_utils import run_bass_kernel_spmd as _run

    nc = _bacc.Bacc("TRN2", target_bir_lowering=False, num_devices=1)
    arrays, args = {}, []
    for name in _INS:
        a = _np.ascontiguousarray(inputs[name])
        arrays[f"in_{name}_dram"] = a
        args.append(nc.dram_tensor(f"in_{name}_dram", a.shape, _mybir.dt.from_np(a.dtype), kind="ExternalInput").ap())
    out = nc.dram_tensor("out_dram", arrays["in_x_dram"].shape, _mybir.dt.float32, kind="ExternalOutput").ap()
    hybrid_block(nc, *args, out)
    r = _run(nc, [arrays], core_ids=[0])
    return r.results[0]["out_dram"]
```

```python
from contextlib import ExitStack

import concourse.bass as bass
from concourse import mybir

ALU = mybir.AluOpType
ACT = mybir.ActivationFunctionType
F32 = mybir.dt.float32
F32R = mybir.dt.float32r
I32 = mybir.dt.int32
AX_X = mybir.AxisListType.X

P = 128
BANK = 512
EPS = 1e-6
ALPHA = 2.0 ** 0.25
UNIT_KT = 2
RAW_SLOTS = 8
SPLIT_SLOTS = 3
LEAD = 2
KEPT = 64
KB = 1024


class Phase:

    def __init__(self, name, iters, units, width):
        self.name, self.iters, self.units, self.width = name, iters, units, width


def ring_place(u, units, slots):
    if slots != SPLIT_SLOTS:
        return u % slots
    back = {0: 0, 1: 2, 2: 1}[units % slots]
    middle = max(1, units // 2)
    steps_back = min(max(u - middle, 0), back)
    return (u - 2 * steps_back) % slots


class Stream:

    def __init__(self, phases):
        self.phases = phases
        self.base = []
        self.loads = []
        at, loads = 0, [0] * RAW_SLOTS
        for ph in phases:
            self.base.append(at)
            self.loads.append(list(loads))
            at += ph.iters * ph.units
            for s in range(RAW_SLOTS):
                loads[s] += ph.iters * self.uses(ph, s)

    @staticmethod
    def uses(ph, s):
        return sum(ring_place(u, ph.units, RAW_SLOTS) == s for u in range(ph.units))

    def index(self, p, it, u):
        return it * self.phases[p].units + (self.base[p] + u)

    def loaded(self, p, it, u):
        n = self.phases[p].units
        if u >= n:
            it, u = it + 1, u - n
        s = ring_place(u, n, RAW_SLOTS)
        earlier = sum(ring_place(v, n, RAW_SLOTS) == s for v in range(u))
        return it * (16 * self.uses(self.phases[p], s)) + 16 * (self.loads[p][s] + earlier + 1)

    def freed(self, p, it, u, slots):
        n = self.phases[p].units
        over = u >= n
        if over:
            it, u = it + 1, u - n
        s = ring_place(u, n, slots)
        same = [v for v in range(u) if ring_place(v, n, slots) == s]
        if same:
            c = same[-1] + 1
        else:
            prev = [v for v in range(n) if ring_place(v, n, slots) == s]
            c = prev[-1] - n + 1 if prev else -n
            if not over:
                if p > 0:
                    m = self.phases[p - 1].units
                    prev = [v for v in range(m) if ring_place(v, m, slots) == s]
                    before = prev[-1] - m + 1 if prev else -m
                    c = max(c, before) if self.phases[p].iters > 1 else before
                elif isinstance(it, int) and it == 0:
                    return None
        return it * n + (self.base[p] + c)


def hybrid_block(nc, x, ffn1_w_gate, ffn1_w_up, ffn1_w_down, ln1_g, ln1_b, w_in, q_norm_g, kv_norm_g,
                 w_uq, w_uk, w_uv, w_q_idx, k_idx_ln_g, k_idx_ln_b, conv_w, a_log, dt_bias, o_norm_g,
                 w_out, ln2_g, ln2_b, ffn2_w_gate, ffn2_w_up, ffn2_w_down, ln3_g, ln3_b, out):
    T = x.shape[1] // P
    D = x.shape[2]
    KT = D // P
    FF = ffn1_w_gate.shape[2]
    FT = FF // P
    QR = q_norm_g.shape[1]
    KR = kv_norm_g.shape[1]
    AH, AD = w_uq.shape[2], w_uq.shape[3]
    ID = k_idx_ln_g.shape[1]
    IH = w_q_idx.shape[2] // ID
    BH = a_log.shape[1]
    BD = o_norm_g.shape[1]
    BW = BH * BD
    TAPS = conv_w.shape[1]
    S = T * P
    RT = KR // P
    QT = QR // P
    A_COLS = QR + KR + ID + IH
    Z_COLS = BW + 2 * BH
    CONV_TILES = 3 * BW // P
    A_SCALE = AD ** -0.5
    W_SCALE = IH ** -0.5 * ID ** -0.5
    assert T == 2 and D == 2048 and FT == 44 and AD == P and BD == P and ID == P

    GATE_CHUNKS = FF // BANK
    OUT_CHUNKS = D // BANK
    KU = KT // UNIT_KT
    DOWN_U = FT // UNIT_KT
    A_ITERS, C_ITERS = 2, 4
    A_W, C_W = A_COLS // A_ITERS, Z_COLS // C_ITERS
    B_ITERS = 3 * BW // BANK
    F1GU, F1D, WA, WB, WC, WQI, WUQ, WO, F2GU, F2D = range(10)
    QI_CHUNKS, UQ_CHUNKS, QU = IH * ID // BANK, AH * AD // BANK, QT // UNIT_KT
    st = Stream([
        Phase("ffn1 gate and up", GATE_CHUNKS, 2 * KU, BANK),
        Phase("ffn1 down", OUT_CHUNKS, DOWN_U, BANK),
        Phase("w_in: latents and index key", A_ITERS, KU, A_W),
        Phase("w_in: q k v", B_ITERS, KU, BANK),
        Phase("w_in: z a b", C_ITERS, KU, C_W),
        Phase("w_q_idx", 1, QI_CHUNKS * QU, BANK),
        Phase("w_uq", 1, UQ_CHUNKS * QU, BANK),
        Phase("w_out", OUT_CHUNKS, KU, BANK),
        Phase("ffn2 gate and up", GATE_CHUNKS, 2 * KU, BANK),
        Phase("ffn2 down", OUT_CHUNKS, DOWN_U, BANK),
    ])
    n0 = {F1GU: 0, F1D: 11, WA: 15, WB: 17, WC: 23, WQI: 27, WUQ: 29, WO: 30, F2GU: 34, F2D: 45}
    n1 = {F1GU: 0, WQI: 11, WUQ: 13, F2GU: 14}

    with ExitStack() as ctx:
        base = 16512
        MZ = base + 104 * KB

        def at(name, offset, shape, dt=F32):
            return nc.alloc_sbuf_tensor_at(name, shape, dt, offset=offset)

        def mz(name, kb, shape, dt=F32):
            return at(name, MZ + int(kb * KB), shape, dt)

        raw = at("raw", base, [P, RAW_SLOTS, UNIT_KT, BANK])
        whi = at("whi", base + 32 * KB, [P, SPLIT_SLOTS, UNIT_KT, BANK], F32R)
        wlo = at("wlo", base + 44 * KB, [P, SPLIT_SLOTS, UNIT_KT, BANK], F32R)
        xT = at("xT", base + 56 * KB, [P, KT, 2, S], F32R)
        resid = at("resid", base + 88 * KB, [P, T, D])

        hT = mz("hT", 0, [P, FT, 2, S], F32R)
        gated = mz("gated", 88, [P, T, BANK])
        ln_g = mz("ln_g", 0, [P, D])
        ln_b = mz("ln_b", 8, [P, D])

        qkvT = mz("qkvT", 0, [P, CONV_TILES, S])
        zab = mz("zab", 24, [P, T, Z_COLS])
        lat = mz("lat", 32.5, [P, T, A_COLS])
        xs = mz("xs", 40, [P, 4, S + TAPS - 1])
        up_to = mz("up_to", 45, [P, P])
        later = mz("later", 45.5, [P, P])
        in_half = mz("in_half", 46, [P, 2, P])
        not_ahead = mz("not_ahead", 47, [P, P])
        pair_mask = mz("pair_mask", 47.5, [P, 6, P])
        wuk = mz("wuk", 50.5, [P, AH, KR])
        wuv = mz("wuv", 90.5, [P, AH, RT, AD])
        qidxT = mz("qidxT", 66.5, [P, IH, S])
        th = mz("th", 66.5, [P, 4, S])
        qT = mz("qT", 82.5, [P, AH, S])
        cq_g = mz("cq_g", 82.5, [P, QR])
        ckv_g = mz("ckv_g", 84.5, [P, KR])
        ki_g = mz("ki_g", 85.5, [P, ID])
        ki_b = mz("ki_b", 86, [P, ID])
        cqT = mz("cqT", 90.5, [P, QT, 2, S], F32R)
        ckv = mz("ckv", 58.5, [P, T, KR])
        ckvT = mz("ckvT", 60.5, [P, RT, S])
        kidxT = mz("kidxT", 62.5, [P, S])
        sel = at("sel", base + 56 * KB, [P, T, S])
        ndist_i = at("ndist_i", base + 56 * KB, [P, T, S], I32)
        ndist = at("ndist", base + 58 * KB, [P, T, S])
        score = mz("score", 33, [P, T, S])
        work = mz("work", 35, [P, T, S])
        relu = mz("relu", 37, [P, 4, 2, S])
        qlatT = at("qlatT", base + 72 * KB, [P, RT, AH, S])
        prob0 = mz("prob0", 82.5, [P, AH, P])
        prob1 = mz("prob1", 50.5, [P, AH, S])
        pT0 = mz("pT0", 33, [P, AH, S])
        pT1 = mz("pT1", 41, [P, AH, P])
        olatT = mz("olatT", 66.5, [P, RT, AH, S])
        vb = mz("vb", 50.5, [P, T, BH, BD])
        kbeg = mz("kbeg", 58.5, [P, T, BH, BD])
        kdec = mz("kdec", 66.5, [P, T, BH, BD])
        aiT = mz("aiT", 74.5, [P, T, BH, P])
        aT = mz("aT", 82.5, [P, T, BH, P])
        sq = mz("sq", 70.5, [P, 2 * BH, S])
        dT = mz("dT", 90.5, [P, T, BH, P])
        xinv = mz("xinv", 90.5, [P, T, BH, P])
        kbT = mz("kbT", 33, [P, T, BH, P])
        yinv = mz("yinv", 33, [P, T, BH, P])
        kb = at("kb", base + 72 * KB, [P, T, BH, BD])
        lev = mz("lev", 8, [P, T, BH, P])
        t1 = mz("t1", 16, [P, T, BH, P])
        nkcdT = mz("nkcdT", 82.5, [P, T, BH, P])
        state = mz("state", 90.5, [P, BH, BD])
        vnew = mz("vnew", 94.5, [P, BH, BD])
        thz_sb = at("thz_sb", base + 72 * KB, [P, T, BW])
        oy = mz("oy", 8, [P, T, BH, BD])
        small = mz("small", 98.5, [P, 24, T, BH])
        ktok = at("ktok", base + 80 * KB, [P, T, BH, BD])

        cz = base + 204 * KB
        ident = at("ident", cz, [P, P])
        cw = at("cw", cz + 512, [P, TAPS, CONV_TILES])
        cw_rows = mz("cw_rows", 89, [TAPS * CONV_TILES, P])
        stats = at("stats", cz + 896, [P, T, OUT_CHUNKS, 6])
        mv = at("mv", cz + 1088, [P, T, 2])
        rstd = at("rstd", cz + 1120, [P, T])
        half_neg = at("half_neg", cz + 1152, [P, 32])
        ss = at("ss", cz + 1280, [P, 3, T])
        rs = at("rs", cz + 1312, [P, 3, T])
        kmv = at("kmv", cz + 1344, [P, T, 2])
        kstats = at("kstats", cz + 1376, [P, T, 6])
        widx = at("widx", cz + 1440, [P, T, IH])
        top8 = at("top8", cz + 1568, [P, T, 8])
        amax = at("amax", cz + 1632, [P, T, AH])
        nmax = at("nmax", cz + 1696, [P, T, AH])
        psumm = at("psumm", cz + 1760, [P, T, AH])
        pinv = at("pinv", cz + 1824, [P, T, AH])
        alog = at("alog", cz + 1888, [P, BH])
        dtb = at("dtb", cz + 1920, [P, BH])
        og = at("og", cz + 1952, [P, BD])
        ones = at("ones", cz + 2464, [P, 2])

        def psum(name, shape):
            return ctx.enter_context(nc.psum_tensor(name, shape, F32))

        acc0 = psum("acc0", [P, 2, BANK])
        acc1 = psum("acc1", [P, 2, BANK])
        tp = psum("tp", [P, 4, BANK])

        class Sems:

            def __init__(self):
                self.made = {}

            def __call__(self, name):
                if name not in self.made:
                    self.made[name] = ctx.enter_context(nc.semaphore("s_" + name))
                return self.made[name]

        sem = Sems()
        raw_loaded = [sem(f"raw_loaded{i}") for i in range(RAW_SLOTS)]
        hi_done, lo_done, unit_used = sem("hi_done"), sem("lo_done"), sem("unit_used")
        acc0a_done = sem("acc0a_done")
        acc0_free = [sem("acc0a_free"), sem("acc0b_free")]
        acc1_free = [sem("acc1a_free"), sem("acc1b_free")]

        def wait(eng, s, value):
            if not (isinstance(value, int) and value <= 0):
                eng.wait_ge(s, value)

        def load_unit(sp, p, it, u, src):
            s = ring_place(u, st.phases[p].units, RAW_SLOTS)
            free = st.freed(p, it, u, RAW_SLOTS)
            if free is not None:
                wait(sp, lo_done, free)
            sp.dma_start(raw[:, s, :, 0:src.shape[2]], src).then_inc(raw_loaded[s], 16)

        def cut_width(p, u):
            return st.phases[p].width if u < st.phases[p].units else BANK

        def split_hi(act, p, it, u):
            n, w = st.phases[p].units, cut_width(p, u)
            s, r = ring_place(u % n, n, SPLIT_SLOTS), ring_place(u % n, n, RAW_SLOTS)
            act.wait_ge(raw_loaded[r], st.loaded(p, it, u))
            free = st.freed(p, it, u, SPLIT_SLOTS)
            if free is not None:
                wait(act, unit_used, free)
            act.activation(whi[:, s, :, 0:w], raw[:, r, :, 0:w], ACT.Copy).then_inc(hi_done, 1)

        def split_lo(dve, p, it, u):
            n, w = st.phases[p].units, cut_width(p, u)
            s, r = ring_place(u % n, n, SPLIT_SLOTS), ring_place(u % n, n, RAW_SLOTS)
            dve.wait_ge(hi_done, st.index(p, it, u + 1))
            dve.tensor_tensor(wlo[:, s, :, 0:w], raw[:, r, :, 0:w], whi[:, s, :, 0:w].bitcast(F32),
                              ALU.subtract).then_inc(lo_done, 1)

        def unit_mm(pe, p, it, u, acc, free, n_chunk, moving, stat, kt0, first, last, a_done=None,
                    ready=None, width=None):
            n = st.phases[p].units
            s = ring_place(u, n, SPLIT_SLOTS)
            width = width or st.phases[p].width
            pe.wait_ge(lo_done, st.index(p, it, u + 1))
            for half in range(2):
                if first and n_chunk is not None:
                    wait(pe, free[half], n_chunk)
                if moving == "w":
                    for k in range(UNIT_KT):
                        kt = kt0 + k
                        hi = stat[:, kt, 0, half * P:half * P + P]
                        lo = stat[:, kt, 1, half * P:half * P + P]
                        o = acc[:, half, 0:width]
                        pe.matmul(o, hi, whi[:, s, k, 0:width], start=first and k == 0, stop=False)
                        pe.matmul(o, hi, wlo[:, s, k, 0:width], start=False, stop=False)
                        ins = pe.matmul(o, lo, whi[:, s, k, 0:width], start=False,
                                        stop=last and k == UNIT_KT - 1)
                else:
                    for c in range(2):
                        cols = slice((2 * half + c) * P, (2 * half + c) * P + P)
                        o = acc[:, half, c * S:c * S + S]
                        for k in range(UNIT_KT):
                            hi, lo = stat[:, kt0 + k, 0, :], stat[:, kt0 + k, 1, :]
                            end = last and k == UNIT_KT - 1
                            pe.matmul(o, whi[:, s, k, cols], hi, start=first and k == 0 and c == 0,
                                      stop=False, skip_group_check=True)
                            pe.matmul(o, whi[:, s, k, cols], lo, start=False, stop=False,
                                      skip_group_check=True)
                            ins = pe.matmul(o, wlo[:, s, k, cols], hi, start=False, stop=end,
                                            skip_group_check=True)
                if half == 0 and last and a_done is not None:
                    ins.then_inc(a_done, 1)
            ins.then_inc(unit_used, 1)

        def to_xT_pe(pe, e, q):
            if e == 0:
                pe.wait_ge(sem(f"x_loaded{q}"), 16)
            else:
                pe.wait_ge(sem("ln_out"), 8 * (e - 1) + 2 * q + 2)
            if 4 * e + q >= 2:
                pe.wait_ge(sem("xT_lo"), 4 * e + q - 1)
            for k in range(4):
                for t in range(T):
                    ins = pe.transpose(tp[:, 2 * (q % 2) + k // 2, (k % 2) * S + t * P:(k % 2) * S + t * P + P],
                                       resid[:, t, (4 * q + k) * P:(4 * q + k + 1) * P], ident[:])
            ins.then_inc(sem("xT_ps"), 1)

        def entry_pe(pe, e, u):
            if u == 0:
                to_xT_pe(pe, e, 0)
                to_xT_pe(pe, e, 1)
            elif u in (2, 4):
                to_xT_pe(pe, e, u // 2 + 1)
            pe.wait_ge(sem("xT_lo"), 4 * e + u // 2 + 1)

        def tp_pair(i):
            return tp[:, 2 * i:2 * i + 2, :].rearrange("p b (k s) -> p (b k) s", k=2)

        def to_xT_act(act, e, q):
            act.wait_ge(sem("xT_ps"), 4 * e + q + 1)
            act.activation(xT[:, 4 * q:4 * q + 4, 0, :], tp_pair(q % 2), ACT.Copy).then_inc(sem("xT_hi"), 1)

        def entry_act(act, e, u):
            for q in {LEAD - 1: (0, 1), 3: (2,), 5: (3,)}.get(u, ()):
                to_xT_act(act, e, q)

        def to_xT_dve(dve, e, q):
            dve.wait_ge(sem("xT_hi"), 4 * e + q + 1)
            dve.tensor_tensor(xT[:, 4 * q:4 * q + 4, 1, :], tp_pair(q % 2),
                              xT[:, 4 * q:4 * q + 4, 0, :].bitcast(F32), ALU.subtract).then_inc(sem("xT_lo"), 1)

        def norm_stats(dve, e):
            for t in range(T):
                dve.wait_ge(sem("stats"), T * OUT_CHUNKS * (e + 1))
                dve.bn_aggr(mv[:, t], stats[:, t]).then_inc(sem("ln_mv"), 1)
            dve.wait_ge(sem("ln_rstd"), 2 * e + 2)
            dve.wait_ge(sem("ln_gains"), 32 * (e + 1))

        def norm_quarter(eng, e, q, tiles=range(T)):
            cols = slice(q * BANK, q * BANK + BANK)
            for t in tiles:
                eng.scalar_tensor_tensor(out=resid[:, t, cols], in0=resid[:, t, cols], scalar=mv[:, t, 0:1],
                                         in1=ln_g[:, cols], op0=ALU.subtract, op1=ALU.mult)\
                   .then_inc(sem("ln_mid"), 1)
            for t in tiles:
                eng.wait_ge(sem("ln_mid"), 8 * e + 2 * q + t + 1)
                eng.scalar_tensor_tensor(out=resid[:, t, cols], in0=resid[:, t, cols], scalar=rstd[:, t:t + 1],
                                         in1=ln_b[:, cols], op0=ALU.mult, op1=ALU.add)\
                   .then_inc(sem("ln_out"), 1)

        def entry_dve(dve, e, u):
            def norm(*quarters):
                if e > 0:
                    for q in quarters:
                        norm_quarter(dve, e - 1, q)

            if u == LEAD - 1:
                if e > 0:
                    norm_stats(dve, e - 1)
                norm(0, 1)
                to_xT_dve(dve, e, 0)
                to_xT_dve(dve, e, 1)
            elif u == 2:
                norm(2)
            elif u == 3:
                to_xT_dve(dve, e, 2)
                norm(3)
            elif u == 5:
                to_xT_dve(dve, e, 3)

        def norm_gains(pool, g, b):
            for dst, src in ((ln_g, g), (ln_b, b)):
                pool.dma_start(dst[:], src.to_broadcast([P, D])).then_inc(sem("ln_gains"), 16)

        def norm_pool(pool, e):
            pool.wait_ge(sem("ln_mv"), 2 * e + 2)
            pool.tensor_scalar(rstd[:], mv[:, :, 1], EPS / ALPHA ** 2, None, ALU.add).then_inc(sem("ln_rstd"), 1)
            pool.wait_ge(sem("ln_rstd"), 2 * e + 1)
            pool.tensor_tensor(rstd[:], rstd[:], half_neg[:, 0:T], ALU.pow).then_inc(sem("ln_rstd"), 1)

        GU, DN = [F1GU, F2GU], [F1D, F2D]

        def ffn_loads(sp, f, w_gate, w_up, w_down, load_x):
            gate_v = w_gate.rearrange("(k p) n -> p k n", p=P)
            up_v = w_up.rearrange("(k p) n -> p k n", p=P)
            down_v = w_down.rearrange("(k p) n -> p k n", p=P)

            def gate_up(c, x_between=None):
                for v, view in ((0, gate_v), (KU, up_v)):
                    for u in range(KU):
                        load_unit(sp, GU[f], c, v + u, view[:, 2 * u:2 * u + 2, bass.ds(c * BANK, BANK)])
                        if x_between and v + u in (1, 3):
                            x_between(2 + (v + u) // 2)

            gate_up(0, load_x)
            with sp.Fori(1, GATE_CHUNKS) as c:
                gate_up(c)
            with sp.Fori(0, OUT_CHUNKS) as c:
                for u in range(DOWN_U):
                    load_unit(sp, DN[f], c, u, down_v[:, 2 * u:2 * u + 2, bass.ds(c * BANK, BANK)])

        def hT_pe(pe, f, c):
            for half in range(2):
                pe.wait_ge(acc1_free[half], c + n1[GU[f]])
            for k in range(4):
                for t in range(T):
                    ins = pe.transpose(tp[:, k // 2, (k % 2) * S + t * P:(k % 2) * S + t * P + P],
                                       gated[:, t, k * P:k * P + P], ident[:])
            ins.then_inc(sem("hT_ps"), 1)

        def hT_act(act, f, c):
            act.wait_ge(sem("hT_ps"), c + f * GATE_CHUNKS)
            act.activation(hT[:, bass.ds(4 * (c - 1), 4), 0, :], tp_pair(0), ACT.Copy).then_inc(sem("hT_hi"), 1)

        def hT_dve(dve, f, c):
            dve.wait_ge(sem("hT_hi"), c + f * GATE_CHUNKS)
            dve.tensor_tensor(hT[:, bass.ds(4 * (c - 1), 4), 1, :], tp_pair(0),
                              hT[:, bass.ds(4 * (c - 1), 4), 0, :].bitcast(F32), ALU.subtract)\
               .then_inc(sem("hT_lo"), 1)

        def gate_times_up(dve, f, c):
            dve.wait_ge(unit_used, st.index(GU[f], c, 0))
            for t in range(T):
                dve.wait_ge(acc0_free[t], c + n0[GU[f]])
                dve.tensor_tensor(gated[:, t], gated[:, t], acc1[:, t], ALU.mult).then_inc(acc1_free[t], 1)

        def ffn_pe(pe, f):
            def gate_up(c, prev):
                for u in range(KU):
                    if not prev:
                        entry_pe(pe, 2 * f, u)
                    unit_mm(pe, GU[f], c, u, acc0, acc0_free, c + n0[GU[f]], "w", xT, 2 * u, u == 0, u == KU - 1,
                            acc0a_done)
                    if u == 3 and prev:
                        hT_pe(pe, f, c)
                for u in range(KU):
                    unit_mm(pe, GU[f], c, KU + u, acc1, acc1_free, c + n1[GU[f]], "w", xT, 2 * u, u == 0,
                            u == KU - 1)

            gate_up(0, False)
            with pe.Fori(1, GATE_CHUNKS) as c:
                gate_up(c, True)

            def down(c, tail):
                for u in range(DOWN_U):
                    if tail and u == 0:
                        pe.wait_ge(sem("hT_lo"), (f + 1) * GATE_CHUNKS - 1)
                    if tail and 4 * (GATE_CHUNKS - 1) == 2 * u:
                        pe.wait_ge(sem("hT_lo"), (f + 1) * GATE_CHUNKS)
                    unit_mm(pe, DN[f], c, u, acc0, acc0_free, c + n0[DN[f]], "w", hT, 2 * u, u == 0,
                            u == DOWN_U - 1, acc0a_done)
                    if tail and u == 3:
                        hT_pe(pe, f, GATE_CHUNKS)

            down(0, True)
            with pe.Fori(1, OUT_CHUNKS) as c:
                down(c, False)

        def ffn_act(act, f, last):
            def gate_up(c, prev):
                if not prev:
                    entry_act(act, 2 * f, LEAD - 1)
                for u in range(LEAD, 2 * KU + LEAD):
                    split_hi(act, GU[f], c, u)
                    if not prev:
                        entry_act(act, 2 * f, u)
                    if u == 6 and prev:
                        hT_act(act, f, c)
                    if u == KU + 1:
                        act.wait_ge(unit_used, st.index(GU[f], c, KU))
                        if prev or f > 0:
                            act.wait_ge(sem("hT_ps"), c + f * GATE_CHUNKS)
                        act.activation(gated[:], acc0[:], ACT.Tanh, scale=0.5).then_inc(sem("tanh_gate"), 1)

            if f == 0:
                act.wait_ge(sem("cw_ps"), 1)
                act.activation(cw[:].rearrange("p a t -> p (a t)"), acc1[:, 0, 0:TAPS * CONV_TILES], ACT.Copy)\
                   .then_inc(sem("cw"), 1)
            gate_up(0, False)
            with act.Fori(1, GATE_CHUNKS) as c:
                gate_up(c, True)

            def down(c, tail, lead):
                for u in range(LEAD, DOWN_U + lead):
                    split_hi(act, DN[f], c, u)
                    if u == 6 and tail:
                        hT_act(act, f, GATE_CHUNKS)

            down(0, True, LEAD)
            with act.Fori(1, OUT_CHUNKS - 1) as c:
                down(c, False, LEAD)
            down(OUT_CHUNKS - 1, False, 0 if last else LEAD)

        def into_resid(dve, p, c, scale, e, in_phase):
            for t in range(T):
                if t == 0:
                    dve.wait_ge(acc0a_done, c + (n0[p] + 1))
                else:
                    dve.wait_ge(unit_used, st.index(p, c, in_phase))
                cols = bass.ds(c * BANK, BANK)
                dve.scalar_tensor_tensor(out=resid[:, t, cols], in0=acc0[:, t], scalar=scale,
                                         in1=resid[:, t, cols], op0=ALU.mult, op1=ALU.add)\
                   .then_inc(acc0_free[t], 1)
            for t in range(T):
                dve.wait_ge(acc0_free[t], c + (n0[p] + 1))
                if isinstance(c, int):
                    where = stats[:, t, c]
                else:
                    where = stats[:, t, bass.ds(c, 1), :].rearrange("p a s -> p (a s)")
                dve.bn_stats(where, resid[:, t, bass.ds(c * BANK, BANK)]).then_inc(sem("stats"), 1)

        def ffn_dve(dve, f, last):
            def gate_up(c, prev):
                if prev:
                    gate_times_up(dve, f, c)
                elif f > 0:
                    entry_dve(dve, 2 * f, LEAD - 1)
                for u in range(LEAD, 2 * KU + LEAD):
                    split_lo(dve, GU[f], c, u)
                    if not prev:
                        entry_dve(dve, 2 * f, u)
                    if u == 6 and prev:
                        hT_dve(dve, f, c)
                    if u == KU + 1:
                        dve.wait_ge(sem("tanh_gate"), c + (f * GATE_CHUNKS + 1))
                        for t in range(T):
                            dve.scalar_tensor_tensor(out=gated[:, t], in0=gated[:, t], scalar=1.0, in1=acc0[:, t],
                                                     op0=ALU.add, op1=ALU.mult).then_inc(acc0_free[t], 1)

            gate_up(0, False)
            with dve.Fori(1, GATE_CHUNKS) as c:
                gate_up(c, True)

            def down(c, tail, lead):
                if tail:
                    gate_times_up(dve, f, GATE_CHUNKS)
                for u in range(LEAD, DOWN_U + lead):
                    split_lo(dve, DN[f], c, u)
                    if u == 6 and tail:
                        hT_dve(dve, f, GATE_CHUNKS)
                into_resid(dve, DN[f], c, 0.25 / ALPHA, 2 * f, DOWN_U)

            down(0, True, LEAD)
            with dve.Fori(1, OUT_CHUNKS - 1) as c:
                down(c, False, LEAD)
            down(OUT_CHUNKS - 1, False, 0 if last else LEAD)

        NEG = -1e30
        SOFTMAX = [(0, slice(0, AH)), (1, slice(0, AH // 2)), (1, slice(AH // 2, AH))]
        CAUSAL_FILL, TAKEN = -3e38, -3.3e38
        G8 = BH // 2
        GROUPS = [(t, hh) for t in range(T) for hh in range(2)]
        LEVELS = 5
        NAMES = ["xa", "ax", "spl", "sp", "beta", "tb", "g", "eg", "ekd", "gc", "rq", "rk", "cd0", "cd1",
                 "c1", "c2", "c3", "vbs", "qs", "qs2", "sso", "ro", "co"]
        assert len(NAMES) <= 24

        def sm(name):
            return small[:, NAMES.index(name)]

        def sm_group(name, t, hh):
            return sm(name)[:, t, G8 * hh:G8 * hh + G8].unsqueeze(2).to_broadcast([P, G8, P])

        def group(tile, t, hh):
            return tile[:, t, G8 * hh:G8 * hh + G8, :]

        def bankE(i):
            return (acc0, acc0, acc1, acc1)[i][:, i % 2]

        def bankF(i):
            return tp[:, i]

        def heads4(bank):
            return bank.rearrange("p (h c) -> p h c", h=G8)

        def halves(bank):
            return bank.rearrange("p (k s) -> p k s", k=2)

        def kT_of(h, t):
            return qkvT[:, BH + h, t * P:t * P + P]

        def vT_of(h, t):
            return qkvT[:, 2 * BH + h, t * P:t * P + P]

        def qT_of(h, t):
            return qkvT[:, h, t * P:t * P + P]

        def mixer_loads(sp):
            in_v = w_in[0].rearrange("(k p) n -> p k n", p=P)
            for p, iters, width, col0 in ((WA, A_ITERS, A_W, 0), (WB, B_ITERS, BANK, A_COLS),
                                          (WC, C_ITERS, C_W, A_COLS + 3 * BW)):
                with sp.Fori(0, iters) as c:
                    for u in range(KU):
                        load_unit(sp, p, c, u, in_v[:, 2 * u:2 * u + 2, bass.ds(c * width + col0, width)])
            qi_v = w_q_idx[0].rearrange("(k p) n -> p k n", p=P)
            uq_v = w_uq[0].rearrange("(k p) h d -> p k (h d)", p=P)
            for p, view, chunks in ((WQI, qi_v, QI_CHUNKS), (WUQ, uq_v, UQ_CHUNKS)):
                for j in range(chunks):
                    for u in range(QU):
                        load_unit(sp, p, 0, j * QU + u, view[:, 2 * u:2 * u + 2, j * BANK:(j + 1) * BANK])
            out_v = w_out[0].rearrange("(k p) n -> p k n", p=P)
            with sp.Fori(0, OUT_CHUNKS) as c:
                for u in range(KU):
                    load_unit(sp, WO, c, u, out_v[:, 2 * u:2 * u + 2, bass.ds(c * BANK, BANK)])

        def mixer_pool(pool):
            pool.wait_ge(unit_used, st.index(WA, 0, 0))
            for dst, src, n in ((cq_g, q_norm_g, QR), (ckv_g, kv_norm_g, KR), (ki_g, k_idx_ln_g, ID),
                                (ki_b, k_idx_ln_b, ID)):
                pool.dma_start(dst[:], src.to_broadcast([P, n])).then_inc(sem("latent_gains"), 16)
            for dst, src, n in ((alog, a_log, BH), (dtb, dt_bias, BH), (og, o_norm_g, BD)):
                pool.dma_start(dst[:], src.to_broadcast([P, n])).then_inc(sem("delta_gains"), 16)
            pool.memset(xs[:, :, 0:TAPS - 1], 0.0).then_inc(sem("xs_th_free"), 1)
            pool.memset(ones[:], 1.0).then_inc(sem("ones"), 1)
            pool.dma_start(wuk[:], w_uk[0].rearrange("h d r -> d h r")).then_inc(sem("wuk"), 16)
            pool.wait_ge(sem("lat_ss"), 2 * T)
            pool.wait_ge(sem("k_mv"), T)
            pool.tensor_scalar(rs[:, 0], ss[:, 0], 1.0 / QR, EPS, ALU.mult, ALU.add).then_inc(sem("lat_rs"), 1)
            pool.tensor_scalar(rs[:, 1], ss[:, 1], 1.0 / KR, EPS, ALU.mult, ALU.add).then_inc(sem("lat_rs"), 1)
            pool.tensor_scalar(rs[:, 2], kmv[:, :, 1], EPS, None, ALU.add).then_inc(sem("lat_rs"), 1)
            pool.wait_ge(sem("lat_rs"), 3)
            rs_flat = rs[:].rearrange("p a t -> p (a t)")
            pool.tensor_tensor(rs_flat, rs_flat, half_neg[:, 0:3 * T], ALU.pow).then_inc(sem("lat_rs"), 1)
            CH = P // 2
            marks = [0]

            def mark(ins):
                ins.then_inc(sem("masks"), 1)
                marks[0] += 1

            def chunked(ap):
                return ap.rearrange("p (b j) -> p b j", b=2)

            mark(pool.memset(up_to[:], 1.0))
            mark(pool.memset(later[:], 1.0))
            mark(pool.memset(in_half[:], 1.0))
            mark(pool.memset(not_ahead[:], 0.0))
            mark(pool.memset(pair_mask[:], 0.0))
            pool.wait_ge(sem("masks"), marks[0])
            for i in range(6):
                m = 1 << i
                v = pair_mask[:, i].rearrange("p (b h j) -> p b h j", h=2, j=m)
                mark(pool.memset(v[:, :, 1, :], 1.0))

            def keep(ap, base_, pattern, mult, fill=0.0):
                mark(pool.affine_select(out=ap, in_=ap, compare_op=ALU.is_ge, fill=fill, base=base_,
                                        pattern=pattern, channel_multiplier=mult))

            keep(chunked(up_to[:]), 0, [[CH, 2], [1, CH]], -1)
            keep(chunked(not_ahead[:]), 0, [[CH, 2], [1, CH]], -1, NEG)
            keep(chunked(later[:]), -1, [[-CH, 2], [-1, CH]], 1)
            keep(in_half[:, 0], CH - 1, [[0, P]], -1)
            keep(in_half[:, 1], -CH, [[0, P]], 1)
            pool.wait_ge(sem("masks"), marks[0])
            keep(chunked(up_to[:]), 0, [[-CH, 2], [0, CH]], 1)
            keep(chunked(not_ahead[:]), 0, [[-CH, 2], [0, CH]], 1, NEG)
            keep(chunked(later[:]), CH - 1, [[CH, 2], [0, CH]], -1)
            views = []
            for i in range(6):
                m = 1 << i
                v = pair_mask[:, i].rearrange("p (b h j) -> p b (h j)", h=2, j=m)
                views.append((m, P // (2 * m), v))
                keep(v, 0, [[-2 * m, P // (2 * m)], [0, 2 * m]], 1)
            pool.wait_ge(sem("masks"), marks[0])
            for m, nb, v in views:
                keep(v, m - 1, [[2 * m, nb], [0, 2 * m]], -1)
            assert marks[0] == MASKS

            pool.wait_ge(unit_used, st.index(WQI, 0, 0))
            pool.iota(ndist_i[:], pattern=[[-P, T], [1, S]], base=0, channel_multiplier=-1).then_inc(sem("ndist"), 1)
            pool.wait_ge(sem("ndist"), 1)
            pool.tensor_copy(ndist[:], ndist_i[:]).then_inc(sem("ndist"), 1)

            pool.wait_ge(sem("qk_ss"), 1)
            qk = small[:, NAMES.index("rq"):NAMES.index("rq") + 2].rearrange("p a t h -> p (a t h)")
            pool.tensor_scalar(qk, qk, 4 * EPS, None, ALU.add).then_inc(sem("qk_r"), 1)
            pool.wait_ge(sem("qk_r"), 1)
            pool.tensor_tensor(qk, qk, half_neg[:, 0:2 * T * BH], ALU.pow).then_inc(sem("qk_r"), 1)
            pool.wait_ge(unit_used, st.index(WO, 0, 0))
            pool.dma_start(wuv[:], w_uv[0].rearrange("h (t r) d -> r h t d", r=P)).then_inc(sem("wuv"), 16)
            pool.wait_ge(sem("score_acc"), 2 * IH)
            for t in range(T):
                n = (t + 1) * P
                pool.affine_select(out=score[:, t, 0:n], in_=score[:, t, 0:n], compare_op=ALU.is_ge,
                                   fill=CAUSAL_FILL, base=t * P, pattern=[[-1, n]], channel_multiplier=1)\
                    .then_inc(sem("score_masked"), 1)
            for t in range(T):
                n = (t + 1) * P
                pool.wait_ge(sem("sel_raw"), 2 * T)
                pool.affine_select(out=sel[:, t, 0:n], in_=sel[:, t, 0:n], compare_op=ALU.is_ge,
                                   fill=NEG, base=t * P, pattern=[[-1, n]], channel_multiplier=1)\
                    .then_inc(sem("sel"), 1)
            pool.wait_ge(sem("factors"), 6)
            for n, (t, hh) in enumerate(GROUPS):
                pool.wait_ge(sem("ktok"), n + 1)
                pool.tensor_tensor(group(kb, t, hh), group(ktok, t, hh), sm_group("c1", t, hh), ALU.mult)\
                    .then_inc(sem("kb"), 1)
            pool.wait_ge(sem("oT_ps"), AH)
            for n, (t, hh) in enumerate(GROUPS):
                for dst, f in ((kbeg, "c2"), (kdec, "c3")):
                    pool.tensor_tensor(group(dst, t, hh), group(ktok, t, hh), sm_group(f, t, hh), ALU.mult)\
                        .then_inc(sem("k_scaled"), 1)
            pool.wait_ge(sem("qk_ps"), 4)
            for lvl in range(1, LEVELS + 1):
                for n, (t, hh) in enumerate(GROUPS):
                    if lvl == 1:
                        pool.wait_ge(sem("kk_m"), G8 * (n + 1))
                    else:
                        pool.wait_ge(sem("t1_ps"), 4 * (lvl - 2) + n + 1)
                    pool.tensor_tensor(group(lev, t, hh), group(aT, t, hh),
                                       pair_mask[:, lvl].unsqueeze(1).to_broadcast([P, G8, P]), ALU.mult)\
                        .then_inc(sem("lev"), 1)
                if lvl == 1:
                    for n, (t, hh) in enumerate(GROUPS):
                        pool.wait_ge(sem("vtok"), n + 1)
                        pool.tensor_tensor(group(vb, t, hh), group(vb, t, hh), sm_group("vbs", t, hh), ALU.mult)\
                            .then_inc(sem("v_scaled"), 1)
            pool.wait_ge(sem("t1_ps"), 4 * LEVELS)
            pool.memset(state[:], 0.0).then_inc(sem("state0"), 1)
            for t in range(T):
                ro = sm("ro")[:, t]
                pool.wait_ge(sem("o_ms"), t + 1)
                pool.tensor_scalar(ro, sm("sso")[:, t], EPS, None, ALU.add).then_inc(sem("o_r"), 1)
                pool.wait_ge(sem("o_r"), 2 * t + 1)
                pool.tensor_tensor(ro, ro, half_neg[:, 0:BH], ALU.pow).then_inc(sem("o_r"), 1)
            pool.wait_ge(sem("y_lo"), 2)
            norm_gains(pool, ln2_g, ln2_b)
            norm_pool(pool, 1)

        MASKS = 5 + 6 + 5 + 3 + 6 + 6
        SCORE_ITEMS = IH

        def mixer_act(act):
            def read_acc0(p, c, units, dst):
                for t in range(T):
                    if t == 0:
                        act.wait_ge(acc0a_done, c + (n0[p] + 1))
                    else:
                        act.wait_ge(unit_used, st.index(p, c, units))
                    w = st.phases[p].width
                    act.activation(dst[:, t, bass.ds(c * w, w)], acc0[:, t, 0:w], ACT.Copy)\
                       .then_inc(acc0_free[t], 1)

            entry_act(act, 1, LEAD - 1)
            for u in range(LEAD, KU + LEAD):
                split_hi(act, WA, 0, u)
                entry_act(act, 1, u)
            read_acc0(WA, 0, KU, lat)
            with act.Fori(1, A_ITERS) as c:
                for u in range(LEAD, KU + LEAD):
                    split_hi(act, WA, c, u)
                read_acc0(WA, c, KU, lat)
            squares = qidxT[:].rearrange("p h s -> p (h s)")

            def latent_squares(t):
                act.wait_ge(acc0_free[t], n0[WB])
                act.activation(squares[:, 1024 * t:1024 * t + QR], lat[:, t, 0:QR], ACT.Square,
                               accum_out=ss[:, 0, t:t + 1]).then_inc(sem("lat_ss"), 1)
                act.activation(squares[:, 1024 * t + QR:1024 * t + QR + KR], lat[:, t, QR:QR + KR], ACT.Square,
                               accum_out=ss[:, 1, t:t + 1]).then_inc(sem("lat_ss"), 1)

            def conv_tanh(c):
                act.wait_ge(sem("conv_sum"), c * 16 + 16)
                act.activation(th[:], qkvT[:, bass.ds(4 * c, 4), :], ACT.Tanh, scale=0.5)\
                   .then_inc(sem("qkv_tanh"), 1)

            def qkv_chunk(c, prev):
                for u in range(LEAD, KU + LEAD):
                    split_hi(act, WB, c, u)
                    if u == 4 and prev:
                        conv_tanh(c - 1)
                    if u in (2, 3) and not prev:
                        latent_squares(u - 2)
                act.wait_ge(sem("xs_th_free"), c + 1)
                for half in range(2):
                    if half == 0:
                        act.wait_ge(acc0a_done, c + (n0[WB] + 1))
                    else:
                        act.wait_ge(unit_used, st.index(WB, c, KU))
                    act.activation(xs[:, 2 * half:2 * half + 2, TAPS - 1:], halves(acc0[:, half]), ACT.Copy)\
                       .then_inc(acc0_free[half], 1)

            qkv_chunk(0, False)
            act.wait_ge(sem("lat_ss"), 2 * T)
            with act.Fori(1, B_ITERS) as c:
                qkv_chunk(c, True)

            act.wait_ge(sem("xs_th_free"), 2 * BH // 4 + 1)
            act.wait_ge(sem("lat_norm"), 3 * T)

            def zab_chunk(c, first):
                for u in range(LEAD, KU + LEAD):
                    split_hi(act, WC, c, u)
                    if u == 2 and first:
                        act.wait_ge(sem("lat_ps"), 1)
                        act.activation(cqT[:, :, 0, :], tp_pair(0), ACT.Copy).then_inc(sem("cqT_hi"), 1)
                    if u == 3 and first:
                        act.activation(ckvT[:], halves(tp[:, 2]), ACT.Copy).then_inc(sem("latT"), 1)
                        act.activation(kidxT[:], tp[:, 3, 0:S], ACT.Copy).then_inc(sem("latT"), 1)
                    if u == 4 and first:
                        conv_tanh(B_ITERS - 1)
                    if u == 6:
                        act.activation(sq[:, bass.ds(4 * c, 4), :], qkvT[:, bass.ds(4 * c, 4), :], ACT.Square)\
                           .then_inc(sem("sq"), 1)
                read_acc0(WC, c, KU, zab)

            zab_chunk(0, True)
            with act.Fori(1, C_ITERS) as c:
                zab_chunk(c, False)
            act.wait_ge(sem("xs_th_free"), B_ITERS + 1)
            act.wait_ge(sem("ss_ps"), 1)
            for p, dst, chunks in ((WQI, qidxT, QI_CHUNKS), (WUQ, qT, UQ_CHUNKS)):
                for u in range(LEAD, chunks * QU + LEAD):
                    split_hi(act, p, 0, u)
                    if p == WQI and u == 3:
                        gate_exps(act)
                    if p == WQI and u == 6:
                        act.wait_ge(sem("gate_act"), 1)
                        act.activation(sm("spl"), sm("ax"), ACT.Ln, bias=1.0).then_inc(sem("gate_act"), 1)
                    if p == WUQ and u == 4:
                        act.wait_ge(sem("cum_ps"), 1)
                        for n, name in enumerate(("eg", "ekd", "cd0", "cd1")):
                            act.activation(sm(name).rearrange("p t h -> p (t h)"), tp[:, 0, 16 * n:16 * n + 16],
                                           ACT.Exp).then_inc(sem("decays"), 1)
                    if u % QU == 1:
                        j = (u - 3) // QU
                        acc, free = ((acc0, acc0_free), (acc1, acc1_free))[j % 2]
                        act.wait_ge(unit_used, st.index(p, 0, (j + 1) * QU))
                        for half in range(2):
                            act.activation(dst[:, 4 * j + 2 * half:4 * j + 2 * half + 2, :], halves(acc[:, half]),
                                           ACT.Copy).then_inc(free[half], 1)
            for i in range(SCORE_ITEMS):
                n = (i % T + 1) * P
                act.wait_ge(sem("score_ps"), i + 1)
                if i >= 4:
                    act.wait_ge(sem("score_acc"), 4 * (i // T - 2) + i % T + 3)
                act.activation(relu[:, i % 4, :, 0:n], halves(tp[:, i % 4])[:, :, 0:n], ACT.Relu)\
                   .then_inc(sem("relu"), 1)
            for h in range(AH):
                act.wait_ge(sem("qlat_ps"), h + 1)
                act.activation(qlatT[:, :, h, :], halves(tp[:, h % 4]), ACT.Copy).then_inc(sem("qlat"), 1)
            for i, (t, heads) in enumerate(SOFTMAX):
                act.wait_ge(sem("att_nmax"), i + 1)
                prob = (prob0, prob1)[t]
                for h in range(heads.start, heads.stop):
                    act.activation(prob[:, h], prob[:, h], ACT.Exp, scale=A_SCALE, bias=nmax[:, t, h:h + 1],
                                   accum_out=psumm[:, t, h:h + 1]).then_inc(sem("prob_exp"), 1)
            act.wait_ge(sem("pT_ps"), 1)
            act.activation(pT0[:, :, 0:P], tp[:, 0:2].rearrange("p b (h q) -> p (b h) q", h=4), ACT.Copy)\
               .then_inc(sem("pT_part0"), 1)
            for i in (1, 2):
                act.wait_ge(sem("pT_ps"), i + 1)
                act.activation(pT1[:, SOFTMAX[i][1]], heads4(acc0[:, i - 1]), ACT.Copy)\
                   .then_inc(sem(f"pT_part{i}"), 1)
            for h in range(AH):
                act.wait_ge(sem("olat_ps"), h + 1)
                act.activation(olatT[:, :, h, :], olat_bank(h), ACT.Copy).then_inc(sem("olat"), 1)
                if h % 2 == 1:
                    act.wait_ge(sem("k_ps"), h // 2 + 1)
                    act.activation(group(ktok, *GROUPS[h // 2]), heads4(tp[:, 1]), ACT.Copy)\
                       .then_inc(sem("ktok"), 1)
                if h > 0:
                    oT_hi(act, h - 1)
            oT_hi(act, AH - 1)

            for n, (t, hh) in enumerate(GROUPS):
                act.wait_ge(sem("v_ps"), n + 1)
                act.activation(group(vb, t, hh), heads4(bankF(n)), ACT.Copy).then_inc(sem("vtok"), 1)
                act.wait_ge(sem("dT_diff"), G8 * (n + 1))
                act.activation(group(dT, t, hh), group(dT, t, hh), ACT.Exp).then_inc(sem("dT"), 1)
            for n, (t, hh) in enumerate(GROUPS):
                act.wait_ge(sem("kbT_ps"), n + 1)
                act.activation(group(kbT, t, hh), heads4(bankE(n)), ACT.Copy).then_inc(sem("kbT"), 1)
            for n, (t, hh) in enumerate(GROUPS):
                act.wait_ge(sem("x0_ps"), n + 1)
                act.wait_ge(sem("qk_m"), G8 * (n + 1))
                act.activation(group(xinv, t, hh), heads4(bankE(n)), ACT.Copy).then_inc(sem("x0"), 1)
            for s in range(STEPS + 2):
                if s < STEPS:
                    t, hh = GROUPS[s % 4]
                    act.wait_ge(sem("t1_ps"), s + 1)
                    act.activation(group(t1, t, hh), heads4(bankF(s % 4)), ACT.Copy).then_inc(sem("t1"), 1)
                if 0 <= s - 2 < STEPS - 4:
                    t, hh = GROUPS[(s - 2) % 4]
                    act.wait_ge(sem("x_ps"), s - 1)
                    act.activation(group(xinv, t, hh), heads4(bankF((s - 2) % 4)), ACT.Copy).then_inc(sem("x_up"), 1)
                if s < 4:
                    t, cols = s // 2, slice(BANK * (s % 2), BANK * (s % 2) + BANK)
                    act.activation(thz[:, t, cols], zab[:, t, cols], ACT.Tanh, scale=0.5).then_inc(sem("thz"), 1)
            for n, (t, hh) in enumerate(GROUPS):
                act.wait_ge(sem("kcd_ps"), n + 1)
                act.activation(group(nkcdT, t, hh), heads4(bankF(n)), ACT.Copy, scale=-1.0)\
                   .then_inc(sem("nkcd"), 1)
            for n in range(2 * T):
                rows = slice(CHR * (n % 2), CHR * (n % 2) + CHR)
                for b in range(2):
                    act.wait_ge(sem("vn_ps"), 2 * n + b + 1)
                    act.activation(vnew[rows, 4 * b:4 * b + 4, :], heads4(tp[rows, b]), ACT.Copy)\
                       .then_inc(sem("vnew"), 1)
                if n % 2 == 0 and n > 0:
                    square_o(act, n // 2 - 1)
            square_o(act, T - 1)

            for u in range(LEAD, 5):
                split_hi(act, WO, 0, u)
            for q in range(2):
                act.wait_ge(sem("yT_ps"), q + 1)
                act.activation(xT[:, AH + 4 * q:AH + 4 * q + 4, 0, :], yT_banks(q), ACT.Copy)\
                   .then_inc(sem("y_hi"), 1)
            for u in range(5, KU + LEAD):
                split_hi(act, WO, 0, u)
            with act.Fori(1, OUT_CHUNKS) as c:
                for u in range(LEAD, KU + LEAD):
                    split_hi(act, WO, c, u)

        def gate_exps(act):
            act.wait_ge(sem("gate_in"), 2)
            act.wait_ge(sem("delta_gains"), 48)
            act.activation(sm("ax"), sm("ax"), ACT.Exp, scale=-1.0).then_inc(sem("gate_act"), 1)
            act.activation(alog[:], alog[:], ACT.Exp).then_inc(sem("gate_act"), 1)
            act.activation(sm("tb"), zab[:, :, BW + BH:BW + 2 * BH], ACT.Tanh, scale=0.5)\
               .then_inc(sem("gate_act"), 1)

        def square_o(act, t):
            act.wait_ge(sem("o_sum"), 4 * t + 4)
            act.activation(t1[:, t], oy[:, t], ACT.Square).then_inc(sem("o_sq"), 1)

        STEPS = 4 * LEVELS
        CHR = P // 2
        thz = thz_sb[:]
        z_part = zab[:, :, 0:BW]

        def yT_banks(q):
            return (acc1[:], tp[:, 0:2])[q].rearrange("p b (k s) -> p (b k) s", k=2)

        def olat_bank(h):
            return halves((acc1[:, 0], acc1[:, 1], tp[:, 0])[h % 3])

        def o_bank(h):
            return (acc0[:, 0], acc0[:, 1], tp[:, 2], tp[:, 3])[h % 4][:, 0:S]

        def oT_hi(act, h):
            act.wait_ge(sem("oT_ps"), h + 1)
            act.activation(xT[:, h, 0, :], o_bank(h), ACT.Copy).then_inc(sem("oT_hi"), 1)

        def mixer_dve(dve):
            entry_dve(dve, 1, LEAD - 1)
            for u in range(LEAD, KU + LEAD):
                split_lo(dve, WA, 0, u)
                entry_dve(dve, 1, u)
            with dve.Fori(1, A_ITERS) as c:
                for u in range(LEAD, KU + LEAD):
                    split_lo(dve, WA, c, u)
            key = slice(QR + KR, QR + KR + ID)

            def key_stats():
                for t in range(T):
                    dve.wait_ge(acc0_free[t], n0[WB])
                for t in range(T):
                    dve.bn_stats(kstats[:, t], lat[:, t, key]).then_inc(sem("k_stats"), 1)
                for t in range(T):
                    dve.wait_ge(sem("k_stats"), t + 1)
                    dve.bn_aggr(kmv[:, t], kstats[:, t]).then_inc(sem("k_mv"), 1)
                dve.tensor_scalar(widx[:], lat[:, :, QR + KR + ID:A_COLS], W_SCALE, None, ALU.mult)\
                   .then_inc(sem("widx"), 1)

            def latent_norms(t):
                dve.wait_ge(sem("lat_rs"), 4)
                dve.wait_ge(sem("latent_gains"), 64)
                dve.scalar_tensor_tensor(out=lat[:, t, key], in0=lat[:, t, key], scalar=kmv[:, t, 0:1],
                                         in1=ki_g[:], op0=ALU.subtract, op1=ALU.mult).then_inc(sem("k_mid"), 1)
                dve.scalar_tensor_tensor(out=lat[:, t, 0:QR], in0=lat[:, t, 0:QR], scalar=rs[:, 0, t:t + 1],
                                         in1=cq_g[:], op0=ALU.mult, op1=ALU.mult).then_inc(sem("lat_norm"), 1)
                dve.scalar_tensor_tensor(out=ckv[:, t], in0=lat[:, t, QR:QR + KR], scalar=rs[:, 1, t:t + 1],
                                         in1=ckv_g[:], op0=ALU.mult, op1=ALU.mult).then_inc(sem("lat_norm"), 1)
                dve.wait_ge(sem("k_mid"), t + 1)
                dve.scalar_tensor_tensor(out=lat[:, t, key], in0=lat[:, t, key], scalar=rs[:, 2, t:t + 1],
                                         in1=ki_b[:], op0=ALU.mult, op1=ALU.add).then_inc(sem("lat_norm"), 1)

            dve.wait_ge(sem("cw"), 1)

            def conv(c, half):
                dve.wait_ge(acc0_free[half], c + (n0[WB] + 1))
                for step in range(TAPS):
                    tap = TAPS - 1 - step
                    for j in (2 * half, 2 * half + 1):
                        dst = qkvT[:, bass.ds(4 * c + j, 1), :].rearrange("p a s -> p (a s)")
                        w = cw[:, tap, bass.ds(4 * c + j, 1)]
                        if step == 0:
                            dve.tensor_scalar(dst, xs[:, j, tap:tap + S], w, None, ALU.mult)\
                               .then_inc(sem("conv_sum"), 1)
                        else:
                            dve.wait_ge(sem("conv_sum"), c * 16 + 8 * half + 2 * (step - 1) + j % 2 + 1)
                            dve.scalar_tensor_tensor(out=dst, in0=xs[:, j, tap:tap + S], scalar=w, in1=dst,
                                                     op0=ALU.mult, op1=ALU.add).then_inc(sem("conv_sum"), 1)

            def conv_silu(c):
                dve.wait_ge(sem("qkv_tanh"), c + 1)
                dve.scalar_tensor_tensor(out=qkvT[:, bass.ds(4 * c, 4), :], in0=th[:], scalar=1.0,
                                         in1=qkvT[:, bass.ds(4 * c, 4), :], op0=ALU.add, op1=ALU.mult)\
                   .then_inc(sem("xs_th_free"), 1)

            def qkv_chunk(c, prev):
                for u in range(LEAD, KU + LEAD):
                    split_lo(dve, WB, c, u)
                    if u == 2 and prev:
                        conv(c - 1, 1)
                    if u == 5 and prev:
                        conv_silu(c - 1)
                    if u == 2 and not prev:
                        key_stats()
                    if u in (6, 7) and not prev:
                        latent_norms(u - 6)
                conv(c, 0)

            qkv_chunk(0, False)
            with dve.Fori(1, B_ITERS) as c:
                qkv_chunk(c, True)
            for u in range(LEAD, KU + LEAD):
                split_lo(dve, WC, 0, u)
                if u == 2:
                    conv(B_ITERS - 1, 1)
                if u == 3:
                    dve.wait_ge(sem("cqT_hi"), 1)
                    dve.tensor_tensor(cqT[:, :, 1, :], tp_pair(0), cqT[:, :, 0, :].bitcast(F32), ALU.subtract)\
                       .then_inc(sem("cqT_lo"), 1)
                if u == 5:
                    conv_silu(B_ITERS - 1)
            with dve.Fori(1, C_ITERS) as c:
                for u in range(LEAD, KU + LEAD):
                    split_lo(dve, WC, c, u)
            for t in range(T):
                dve.wait_ge(acc0_free[t], n0[WQI])
            dve.wait_ge(sem("delta_gains"), 48)
            dve.tensor_tensor(sm("xa"), zab[:, :, BW:BW + BH], dtb[:].unsqueeze(1).to_broadcast([P, T, BH]), ALU.add)\
               .then_inc(sem("gate_in"), 1)
            dve.wait_ge(sem("gate_in"), 1)
            dve.scalar_tensor_tensor(out=sm("ax"), in0=sm("xa"), scalar=-1.0, in1=sm("xa"), op0=ALU.mult,
                                     op1=ALU.max).then_inc(sem("gate_in"), 1)
            for p, chunks in ((WQI, QI_CHUNKS), (WUQ, UQ_CHUNKS)):
                for u in range(LEAD, chunks * QU + LEAD):
                    split_lo(dve, p, 0, u)
                    if p == WQI and u == 3:
                        dve.wait_ge(sem("ss_ps"), 1)
                        dve.tensor_copy(
                            small[:, NAMES.index("rq"):NAMES.index("rq") + 2].rearrange("p a t h -> p (a t h)"),
                            tp[:, 1, 0:2 * T * BH]).then_inc(sem("qk_ss"), 1)
                    if p == WQI and u == 7:
                        dve.wait_ge(sem("gate_act"), 4)
                        dve.scalar_tensor_tensor(out=sm("sp"), in0=sm("xa"), scalar=0.0, in1=sm("spl"), op0=ALU.max,
                                                 op1=ALU.add).then_inc(sem("gate_mid"), 1)
                        dve.wait_ge(sem("gate_mid"), 1)
                        dve.scalar_tensor_tensor(out=sm("g"), in0=sm("sp"), scalar=-1.0,
                                                 in1=alog[:].unsqueeze(1).to_broadcast([P, T, BH]), op0=ALU.mult,
                                                 op1=ALU.mult).then_inc(sem("g"), 1)
                        dve.tensor_scalar(sm("beta"), sm("tb"), 0.5, 0.5, ALU.mult, ALU.add).then_inc(sem("beta"), 1)
            dve.wait_ge(sem("decays"), 4)
            dve.tensor_copy(sm("gc").rearrange("p t h -> p (t h)"), tp[:, 0, 0:T * BH]).then_inc(sem("gc"), 1)
            dve.wait_ge(sem("qk_r"), 2)
            dve.wait_ge(sem("beta"), 1)
            dve.tensor_tensor(sm("c1"), sm("rk"), sm("beta"), ALU.mult).then_inc(sem("factors"), 1)
            dve.tensor_tensor(sm("c3"), sm("rk"), sm("ekd"), ALU.mult).then_inc(sem("factors"), 1)
            dve.tensor_scalar(sm("vbs"), sm("beta"), 0.5, None, ALU.mult).then_inc(sem("factors"), 1)
            dve.tensor_scalar(sm("qs"), sm("rq"), BD ** -0.5, None, ALU.mult).then_inc(sem("factors"), 1)
            dve.wait_ge(sem("factors"), 4)
            dve.tensor_tensor(sm("c2"), sm("c1"), sm("eg"), ALU.mult).then_inc(sem("factors"), 1)
            dve.scalar_tensor_tensor(out=sm("qs2"), in0=sm("qs"), scalar=1.0 / BD, in1=sm("qs"), op0=ALU.mult,
                                     op1=ALU.mult).then_inc(sem("factors"), 1)
            dve.wait_ge(sem("widx"), 1)
            dve.wait_ge(sem("lat_ps"), 1)
            dve.wait_ge(sem("xs_th_free"), B_ITERS + 1)
            for pair in range(SCORE_ITEMS // T):
                for hh in range(2):
                    for t in range(T):
                        i, n, h = T * pair + t, (t + 1) * P, 2 * pair + hh
                        dve.wait_ge(sem("relu"), i + 1)
                        src, dst, w = relu[:, i % 4, hh, 0:n], score[:, t, 0:n], widx[:, t, h:h + 1]
                        if h == 0:
                            dve.tensor_scalar(dst, src, w, None, ALU.mult).then_inc(sem("score_acc"), 1)
                        else:
                            dve.wait_ge(sem("score_acc"), T * (h - 1) + t + 1)
                            dve.scalar_tensor_tensor(out=dst, in0=src, scalar=w, in1=dst, op0=ALU.mult, op1=ALU.add)\
                               .then_inc(sem("score_acc"), 1)
            dve.wait_ge(sem("score_masked"), T)
            for r in range(KEPT // 8):
                for t in range(T):
                    n = (t + 1) * P
                    src = (work if r else score)[:, t, 0:n]
                    wait(dve, sem("taken"), T * (r - 1) + t + 1)
                    dve.max(top8[:, t], src).then_inc(sem("top8"), 1)
                for t in range(T):
                    n = (t + 1) * P
                    src = (work if r else score)[:, t, 0:n]
                    dve.wait_ge(sem("top8"), T * r + t + 1)
                    dve.match_replace(out=work[:, t, 0:n], in_to_replace=top8[:, t], in_values=src,
                                      imm_value=TAKEN).then_inc(sem("taken"), 1)
            dve.wait_ge(sem("ndist"), 2)
            for t in range(T):
                n = (t + 1) * P
                dve.wait_ge(sem("taken"), T * (KEPT // 8 - 1) + t + 1)
                dve.tensor_tensor(sel[:, t, 0:n], work[:, t, 0:n], score[:, t, 0:n], ALU.not_equal)\
                   .then_inc(sem("sel_raw"), 1)
            for t in range(T):
                n = (t + 1) * P
                dve.wait_ge(sem("sel_raw"), t + 1)
                dve.tensor_scalar(sel[:, t, 0:n], sel[:, t, 0:n], 1.0, -NEG, ALU.subtract, ALU.mult)\
                   .then_inc(sem("sel_raw"), 1)
            def logits(a):
                t, hp = a // 4, a % 4
                n = (t + 1) * P
                dve.wait_ge(sem("att_ps"), a + 1)
                for hh in range(2):
                    h = 2 * hp + hh
                    slope = 2.0 ** (-8.0 * (h + 1.0) / AH)
                    dve.scalar_tensor_tensor(out=(prob0, prob1)[t][:, h, :], in0=ndist[:, t, 0:n],
                                             scalar=slope / A_SCALE, in1=halves(bankE(a % 4))[:, hh, 0:n],
                                             op0=ALU.mult, op1=ALU.add).then_inc(sem("att_z"), 1)

            def select(i):
                t, heads = SOFTMAX[i]
                n, m = (t + 1) * P, heads.stop - heads.start
                prob = (prob0, prob1)[t][:, heads]
                dve.wait_ge(sem("sel"), T)
                dve.wait_ge(sem("att_z"), AH * t + heads.stop)
                dve.tensor_tensor(prob, prob, sel[:, t, 0:n].unsqueeze(1).to_broadcast([P, m, n]), ALU.add)\
                   .then_inc(sem("att_sel"), 1)
                dve.wait_ge(sem("att_sel"), i + 1)
                dve.reduce_max(amax[:, t, heads], prob, AX_X).then_inc(sem("att_max"), 1)
                dve.wait_ge(sem("att_max"), i + 1)
                dve.tensor_scalar(nmax[:, t, heads], amax[:, t, heads], -A_SCALE, None, ALU.mult)\
                   .then_inc(sem("att_nmax"), 1)

            def normalise(i):
                t, heads = SOFTMAX[i]
                n, m = (t + 1) * P, heads.stop - heads.start
                prob = (prob0, prob1)[t][:, heads]
                dve.wait_ge(sem("prob_exp"), AH * t + heads.stop)
                dve.reciprocal(pinv[:, t, heads], psumm[:, t, heads]).then_inc(sem("pinv"), 1)
                dve.wait_ge(sem("pinv"), i + 1)
                dve.tensor_tensor(prob, prob, pinv[:, t, heads].unsqueeze(2).to_broadcast([P, m, n]), ALU.mult)\
                   .then_inc(sem("prob"), 1)

            for a in range(4):
                logits(a)
            select(0)
            logits(4)
            logits(5)
            select(1)
            logits(6)
            logits(7)
            select(2)
            for i in range(3):
                normalise(i)
            for i in (1, 2):
                heads = SOFTMAX[i][1]
                dve.wait_ge(sem("pT_ps"), i + 1)
                dve.tensor_copy(pT0[:, heads, P:S], heads4(tp[:, 1 + i])).then_inc(sem(f"pT_part{i}"), 1)
            for h in range(AH):
                dve.wait_ge(sem("oT_hi"), h + 1)
                dve.tensor_tensor(xT[:, h, 1, :], o_bank(h), xT[:, h, 0, :].bitcast(F32), ALU.subtract)\
                   .then_inc(sem("oT_lo"), 1)

            dve.wait_ge(sem("gc"), 1)
            dve.wait_ge(sem("factors"), 6)
            dve.wait_ge(sem("masks"), MASKS)
            for n, (t, hh) in enumerate(GROUPS):
                dve.wait_ge(sem("gbc_ps"), n + 1)
                for k in range(G8):
                    h = G8 * hh + k
                    dve.scalar_tensor_tensor(out=dT[:, t, h], in0=bankE(n)[:, k * P:k * P + P],
                                             scalar=sm("gc")[:, t, h:h + 1], in1=not_ahead[:],
                                             op0=ALU.subtract, op1=ALU.add).then_inc(sem("dT_diff"), 1)

            def times_decay(name, dst, bank, n, t, hh):
                dve.wait_ge(sem(name + "_ps"), n + 1)
                dve.wait_ge(sem("dT"), n + 1)
                for k in range(G8):
                    h = G8 * hh + k
                    dve.scalar_tensor_tensor(out=dst[:, t, h], in0=bank[:, k * P:k * P + P],
                                             scalar=sm("rk")[:, t, h:h + 1], in1=dT[:, t, h],
                                             op0=ALU.mult, op1=ALU.mult).then_inc(sem(name + "_m"), 1)

            for n, (t, hh) in enumerate(GROUPS):
                times_decay("kk", aT, bankE(n), n, t, hh)
                dve.wait_ge(sem("kk_m"), G8 * (n + 1))
                dve.tensor_tensor(group(yinv, t, hh), group(aT, t, hh),
                                  pair_mask[:, 0].unsqueeze(1).to_broadcast([P, G8, P]), ALU.mult)\
                   .then_inc(sem("pairs"), 1)
                dve.wait_ge(sem("pairs"), n + 1)
                dve.tensor_tensor(group(yinv, t, hh), ident[:].unsqueeze(1).to_broadcast([P, G8, P]),
                                  group(yinv, t, hh), ALU.subtract).then_inc(sem("y_up"), 1)
                if n > 0:
                    times_decay("qk", aiT, bankF(n - 1), n - 1, *GROUPS[n - 1])
            times_decay("qk", aiT, bankF(3), 3, *GROUPS[3])

            for s in range(STEPS):
                t, hh = GROUPS[s % 4]
                dve.wait_ge(sem("y_ps"), s + 1)
                dve.tensor_tensor(group(yinv, t, hh), group(yinv, t, hh), heads4(bankE(s % 4)),
                                  ALU.subtract).then_inc(sem("y_up"), 1)
                if 4 <= s < 12:
                    i = s % 4
                    t, cols = i // 2, slice(BANK * (i % 2), BANK * (i % 2) + BANK)
                    if s < 8:
                        dve.wait_ge(sem("thz"), i + 1)
                        dve.scalar_tensor_tensor(out=zab[:, t, cols], in0=thz[:, t, cols], scalar=1.0,
                                                 in1=zab[:, t, cols], op0=ALU.add, op1=ALU.mult)\
                           .then_inc(sem("z"), 1)
                    else:
                        dve.wait_ge(sem("z"), i + 1)
                        zt = zab[:, t, cols].rearrange("p (h d) -> p h d", d=BD)
                        dve.tensor_tensor(zt, zt, og[:].unsqueeze(1).to_broadcast([P, G8, BD]), ALU.mult)\
                           .then_inc(sem("z"), 1)

            def o_tile(t):
                for b in range(2):
                    dve.tensor_tensor(group(oy, t, b), heads4(acc0[:, b]), sm_group("eg", t, b), ALU.mult)\
                       .then_inc(sem("o_sum"), 1)
                for b in range(2):
                    dve.wait_ge(sem("o_sum"), 4 * t + b + 1)
                    dve.tensor_tensor(group(oy, t, b), group(oy, t, b), heads4(acc1[:, b]), ALU.add)\
                       .then_inc(sem("o_sum"), 1)

            def z_tile(t):
                dve.wait_ge(sem("o_sum"), 4 * t + 4)
                dve.tensor_tensor(zab[:, t, 0:BW].rearrange("p (h d) -> p h d", d=BD), oy[:, t],
                                  zab[:, t, 0:BW].rearrange("p (h d) -> p h d", d=BD), ALU.mult)\
                   .then_inc(sem("zo"), 1)

            def o_mean_square(t):
                dve.wait_ge(sem("o_sq"), t + 1)
                dve.reduce_sum(sm("co")[:, t], t1[:, t], AX_X).then_inc(sem("o_red"), 1)
                dve.wait_ge(sem("o_red"), t + 1)
                dve.tensor_tensor(sm("sso")[:, t], sm("co")[:, t], sm("qs2")[:, t], ALU.mult)\
                   .then_inc(sem("o_ms"), 1)

            def y_tile(t):
                dve.wait_ge(sem("o_r"), 2 * t + 2)
                dve.wait_ge(sem("o_ms"), t + 1)
                dve.scalar_tensor_tensor(out=sm("co")[:, t], in0=sm("ro")[:, t], scalar=0.5, in1=sm("qs")[:, t],
                                         op0=ALU.mult, op1=ALU.mult).then_inc(sem("o_co"), 1)
                dve.wait_ge(sem("o_co"), t + 1)
                dve.wait_ge(sem("zo"), t + 1)
                dve.tensor_tensor(oy[:, t], zab[:, t, 0:BW].rearrange("p (h d) -> p h d", d=BD),
                                  sm("co")[:, t].unsqueeze(2).to_broadcast([P, BH, BD]), ALU.mult)\
                   .then_inc(sem("y"), 1)

            dve.wait_ge(sem("z"), 8)
            dve.wait_ge(sem("state0"), 1)
            for n in range(2 * T):
                t, half = n // 2, n % 2
                if n < 2 * T - 1:
                    for h in range(BH):
                        if h % 4 == 0:
                            dve.wait_ge(sem("st_ps"), 2 * n + h // 4 + 1)
                        wait(dve, sem("state"), BH * (n - 1) + h + 1)
                        dve.scalar_tensor_tensor(out=state[:, h], in0=state[:, h],
                                                 scalar=sm(f"cd{half}")[:, t, h:h + 1],
                                                 in1=tp[:, 2 + h // 4, (h % 4) * P:(h % 4) * P + P],
                                                 op0=ALU.mult, op1=ALU.add).then_inc(sem("state"), 1)
                if half == 0 and t > 0:
                    z_tile(t - 1)
                    o_mean_square(t - 1)
                if half == 1:
                    if t > 0:
                        y_tile(t - 1)
                    dve.wait_ge(sem("o_ps"), n + 1)
                    o_tile(t)
            split_lo(dve, WO, 0, 2)
            o_mean_square(T - 1)
            z_tile(T - 1)
            split_lo(dve, WO, 0, 3)
            y_tile(T - 1)
            split_lo(dve, WO, 0, 4)
            for q in range(2):
                dve.wait_ge(sem("y_hi"), q + 1)
                rows = xT[:, AH + 4 * q:AH + 4 * q + 4, :, :]
                dve.tensor_tensor(rows[:, :, 1, :], yT_banks(q), rows[:, :, 0, :].bitcast(F32), ALU.subtract)\
                   .then_inc(sem("y_lo"), 1)
            for u in range(5, KU + LEAD):
                split_lo(dve, WO, 0, u)
            into_resid(dve, WO, 0, 1.0 / ALPHA, 1, KU)
            with dve.Fori(1, OUT_CHUNKS) as c:
                for u in range(LEAD, KU + LEAD):
                    split_lo(dve, WO, c, u)
                into_resid(dve, WO, c, 1.0 / ALPHA, 1, KU)

        def mixer_pe(pe):
            def latent_unit(c, u):
                unit_mm(pe, WA, c, u, acc0, acc0_free, c + n0[WA], "w", xT, 2 * u, u == 0, u == KU - 1, acc0a_done)

            for u in range(KU):
                entry_pe(pe, 1, u)
                latent_unit(0, u)
            with pe.Fori(1, A_ITERS) as c:
                for u in range(KU):
                    latent_unit(c, u)
            with pe.Fori(0, B_ITERS) as c:
                for u in range(KU):
                    unit_mm(pe, WB, c, u, acc0, acc0_free, c + n0[WB], "x", xT, 2 * u, u == 0, u == KU - 1,
                            acc0a_done)
            pe.wait_ge(sem("lat_norm"), 3 * T)
            for t in range(T):
                for k in range(QT):
                    pe.transpose(tp_pair(0)[:, k, t * P:t * P + P], lat[:, t, k * P:k * P + P], ident[:])
                for k in range(RT):
                    pe.transpose(halves(tp[:, 2])[:, k, t * P:t * P + P], ckv[:, t, k * P:k * P + P], ident[:])
                ins = pe.transpose(tp[:, 3, t * P:t * P + P], lat[:, t, QR + KR:QR + KR + ID], ident[:])
            ins.then_inc(sem("lat_ps"), 1)
            with pe.Fori(0, C_ITERS) as c:
                for u in range(KU):
                    unit_mm(pe, WC, c, u, acc0, acc0_free, c + n0[WC], "w", xT, 2 * u, u == 0, u == KU - 1,
                            acc0a_done)
            pe.wait_ge(sem("cqT_lo"), 1)
            pe.wait_ge(sem("latT"), 2)
            pe.wait_ge(sem("ones"), 1)
            pe.wait_ge(sem("sq"), 4)
            for i in range(2):
                for t in range(T):
                    for h in range(BH):
                        ins = pe.matmul(tp[:, 1, (i * T + t) * BH + h:(i * T + t) * BH + h + 1],
                                        sq[:, i * BH + h, t * P:t * P + P], ones[:, 0:1], start=True, stop=True)
            ins.then_inc(sem("ss_ps"), 1)
            for p, chunks in ((WQI, QI_CHUNKS), (WUQ, UQ_CHUNKS)):
                if p == WUQ:
                    pe.wait_ge(sem("g"), 1)
                    pe.wait_ge(sem("masks"), MASKS)
                    g_all = sm("g").rearrange("p t h -> p (t h)")
                    for n, m in enumerate((up_to[:], later[:], in_half[:, 0], in_half[:, 1])):
                        ins = pe.matmul(tp[:, 0, 16 * n:16 * n + 16], m, g_all, start=True, stop=True)
                    ins.then_inc(sem("cum_ps"), 1)
                for j in range(chunks):
                    acc, free = ((acc0, acc0_free), (acc1, acc1_free))[j % 2]
                    n = (n0, n1)[j % 2][p] + j // 2
                    for u in range(QU):
                        unit_mm(pe, p, 0, j * QU + u, acc, free, n, "x", cqT, 2 * u, u == 0, u == QU - 1,
                                acc0a_done if j % 2 == 0 else None)
            pe.wait_ge(sem("gc"), 1)
            pe.wait_ge(sem("qk_ss"), 1)
            for half in range(2):
                pe.wait_ge(acc0_free[half], n0[WO])
                pe.wait_ge(acc1_free[half], n1[F2GU])
            for i in range(SCORE_ITEMS):
                t, n = i % T, (i % T + 1) * P
                wait(pe, sem("relu"), i - 3)
                for hh in range(2):
                    h = 2 * (i // T) + hh
                    ins = pe.matmul(halves(tp[:, i % 4])[:, hh, 0:n], qidxT[:, h, t * P:t * P + P], kidxT[:, 0:n],
                                    start=True, stop=True)
                ins.then_inc(sem("score_ps"), 1)
            pe.wait_ge(sem("wuk"), 16)
            for h in range(AH):
                if h < 4:
                    pe.wait_ge(sem("relu"), SCORE_ITEMS - 3 + h)
                else:
                    pe.wait_ge(sem("qlat"), h - 3)
                for r in range(RT):
                    ins = pe.matmul(halves(tp[:, h % 4])[:, r, :], wuk[:, h, r * P:r * P + P], qT[:, h, :],
                                    start=True, stop=True)
                ins.then_inc(sem("qlat_ps"), 1)
            for a in range(AH):
                t, hp = a // 4, a % 4
                n = (t + 1) * P
                wait(pe, sem("att_z"), 2 * (a - 3))
                for hh in range(2):
                    h = 2 * hp + hh
                    if t == 0:
                        pe.wait_ge(sem("qlat"), h + 1)
                    for r in range(RT):
                        ins = pe.matmul(halves(bankE(a % 4))[:, hh, 0:n], qlatT[:, r, h, t * P:t * P + P],
                                        ckvT[:, r, 0:n], start=r == 0, stop=r == RT - 1)
                ins.then_inc(sem("att_ps"), 1)
            pe.wait_ge(sem("qlat"), AH)
            pe.wait_ge(sem("prob"), 1)
            for h in range(AH):
                ins = pe.transpose(tp[:, h // 4, (h % 4) * P:(h % 4) * P + P], prob0[:, h, :], ident[:])
            ins.then_inc(sem("pT_ps"), 1)
            pe.wait_ge(sem("att_z"), 2 * AH)
            for i in (1, 2):
                pe.wait_ge(sem("prob"), i + 1)
                heads = SOFTMAX[i][1]
                for k, h in enumerate(range(heads.start, heads.stop)):
                    cols = slice(k * P, k * P + P)
                    pe.transpose(tp[:, 1 + i, cols], prob1[:, h, 0:P], ident[:])
                    ins = pe.transpose(acc0[:, i - 1, cols], prob1[:, h, P:S], ident[:])
                ins.then_inc(sem("pT_ps"), 1)
            pe.wait_ge(sem("pT_part0"), 1)
            pe.wait_ge(sem("pT_part1"), 2)
            pe.wait_ge(sem("wuv"), 16)

            def o_head(h):
                pe.wait_ge(sem("olat"), h + 1)
                wait(pe, sem("oT_lo"), h - 3)
                for r in range(RT):
                    ins = pe.matmul(o_bank(h), wuv[:, h, r, :], olatT[:, r, h, :], start=r == 0, stop=r == RT - 1)
                ins.then_inc(sem("oT_ps"), 1)

            for h in range(AH):
                if h == 2:
                    pe.wait_ge(sem("pT_part2"), 2)
                wait(pe, sem("olat"), h - 2)
                bank = olat_bank(h)
                for r in range(RT):
                    rc = slice(r * P, r * P + P)
                    pe.matmul(bank[:, r, 0:P], ckv[:, 0, rc], pT0[:, h, 0:P], start=True, stop=True)
                    pe.matmul(bank[:, r, P:S], ckv[:, 0, rc], pT0[:, h, P:S], start=True, stop=False)
                    ins = pe.matmul(bank[:, r, P:S], ckv[:, 1, rc], pT1[:, h, :], start=False, stop=True)
                ins.then_inc(sem("olat_ps"), 1)
                if h % 2 == 1:
                    n = h // 2
                    t, hh = GROUPS[n]
                    wait(pe, sem("ktok"), n)
                    for k in range(G8):
                        ins = pe.transpose(tp[:, 1, k * P:k * P + P], kT_of(G8 * hh + k, t), ident[:])
                    ins.then_inc(sem("k_ps"), 1)
                if h > 0:
                    o_head(h - 1)
            o_head(AH - 1)

            pe.wait_ge(sem("oT_lo"), AH)
            pe.wait_ge(sem("olat"), AH)
            pe.wait_ge(sem("ktok"), 4)
            for n, (t, hh) in enumerate(GROUPS):
                for k in range(G8):
                    ins = pe.transpose(bankF(n)[:, k * P:k * P + P], vT_of(G8 * hh + k, t), ident[:])
                ins.then_inc(sem("v_ps"), 1)
                for k in range(G8):
                    h = G8 * hh + k
                    ins = pe.matmul(bankE(n)[:, k * P:k * P + P], sm("g")[:, t, h:h + 1].to_broadcast([P, P]),
                                    up_to[:], start=True, stop=True)
                ins.then_inc(sem("gbc_ps"), 1)
            for n, (t, hh) in enumerate(GROUPS):
                pe.wait_ge(sem("dT_diff"), G8 * (n + 1))
                pe.wait_ge(sem("kb"), n + 1)
                for k in range(G8):
                    ins = pe.transpose(bankE(n)[:, k * P:k * P + P], kb[:, t, G8 * hh + k], ident[:])
                ins.then_inc(sem("kbT_ps"), 1)
            for n, (t, hh) in enumerate(GROUPS):
                pe.wait_ge(sem("kbT"), n + 1)
                for k in range(G8):
                    h = G8 * hh + k
                    ins = pe.matmul(bankE(n)[:, k * P:k * P + P], kT_of(h, t), kbT[:, t, h], start=True, stop=True)
                ins.then_inc(sem("kk_ps"), 1)
            for n, (t, hh) in enumerate(GROUPS):
                pe.wait_ge(sem("vtok"), n + 1)
                for k in range(G8):
                    h = G8 * hh + k
                    ins = pe.matmul(bankF(n)[:, k * P:k * P + P], kT_of(h, t), qT_of(h, t), start=True, stop=True)
                ins.then_inc(sem("qk_ps"), 1)
            for n, (t, hh) in enumerate(GROUPS):
                pe.wait_ge(sem("y_up"), n + 1)
                for k in range(G8):
                    ins = pe.transpose(bankE(n)[:, k * P:k * P + P], yinv[:, t, G8 * hh + k], ident[:])
                ins.then_inc(sem("x0_ps"), 1)

            for s in range(STEPS + 2):
                if s < STEPS:
                    t, hh = GROUPS[s % 4]
                    pe.wait_ge(sem("lev"), s + 1)
                    if s < 4:
                        pe.wait_ge(sem("x0"), s + 1)
                        pe.wait_ge(sem("qk_m"), G8 * (s + 1))
                    else:
                        pe.wait_ge(sem("x_up"), s - 3)
                    for k in range(G8):
                        h = G8 * hh + k
                        ins = pe.matmul(bankF(s % 4)[:, k * P:k * P + P], lev[:, t, h], xinv[:, t, h],
                                        start=True, stop=True)
                    ins.then_inc(sem("t1_ps"), 1)
                if 0 <= s - 1 < STEPS:
                    n = (s - 1) % 4
                    t, hh = GROUPS[n]
                    pe.wait_ge(sem("t1"), s)
                    for k in range(G8):
                        h = G8 * hh + k
                        ins = pe.matmul(bankE(n)[:, k * P:k * P + P], t1[:, t, h], yinv[:, t, h],
                                        start=True, stop=True)
                    ins.then_inc(sem("y_ps"), 1)
                if 0 <= s - 2 < STEPS - 4:
                    n = (s - 2) % 4
                    t, hh = GROUPS[n]
                    pe.wait_ge(sem("y_up"), 4 + s - 1)
                    for k in range(G8):
                        ins = pe.transpose(bankF(n)[:, k * P:k * P + P], yinv[:, t, G8 * hh + k], ident[:])
                    ins.then_inc(sem("x_ps"), 1)
            pe.wait_ge(sem("k_scaled"), 8)
            for n, (t, hh) in enumerate(GROUPS):
                pe.wait_ge(sem("y_up"), 4 * LEVELS + n + 1)
                for k in range(G8):
                    h = G8 * hh + k
                    ins = pe.matmul(bankF(n)[:, k * P:k * P + P], kbeg[:, t, h], yinv[:, t, h],
                                    start=True, stop=True)
                ins.then_inc(sem("kcd_ps"), 1)
            pe.wait_ge(sem("v_scaled"), 4)
            pe.wait_ge(sem("nkcd"), 4)
            pe.wait_ge(sem("state0"), 1)
            for n in range(2 * T):
                t, half = n // 2, n % 2
                rows = slice(CHR * half, CHR * half + CHR)
                cols = slice(t * P + CHR * half, t * P + CHR * half + CHR)

                def head_cols(h):
                    return slice((h % 4) * P, (h % 4) * P + P)

                for h in range(BH):
                    wait(pe, sem("state"), BH * (n - 1) + h + 1)
                    if h % 4 == 0:
                        wait(pe, sem("vnew"), 2 * (n - 1) + h // 4 + 1)
                    o = tp[rows, h // 4, head_cols(h)]
                    pe.matmul(o, yinv[:, t, h, rows], vb[:, t, h], start=True, stop=False)
                    ins = pe.matmul(o, nkcdT[:, t, h, rows], state[:, h], start=False, stop=True)
                    if h % 4 == 3:
                        ins.then_inc(sem("vn_ps"), 1)
                if t > 0:
                    pe.wait_ge(sem("o_sum"), 4 * t)
                for h in range(BH):
                    ins = pe.matmul(acc0[rows, h // 4, head_cols(h)], qkvT[:, h, cols], state[:, h],
                                    start=True, stop=True)
                for h in range(BH):
                    if h % 4 == 0:
                        pe.wait_ge(sem("vnew"), 2 * n + h // 4 + 1)
                    if n < 2 * T - 1:
                        ins = pe.matmul(tp[:, 2 + h // 4, head_cols(h)], kdec[rows, t, h], vnew[rows, h],
                                        start=True, stop=True)
                        if h % 4 == 3:
                            ins.then_inc(sem("st_ps"), 1)
                for h in range(BH):
                    ins = pe.matmul(acc1[rows, h // 4, head_cols(h)], aiT[rows, t, h, rows], vnew[rows, h],
                                    start=True, stop=True)
                ins.then_inc(sem("o_ps"), 1)
            def out_unit(c, u):
                unit_mm(pe, WO, c, u, acc0, acc0_free, c + n0[WO], "w", xT, 2 * u, u == 0, u == KU - 1, acc0a_done)

            pe.wait_ge(sem("o_sum"), 4 * (T - 1) + 2)
            for u in range(3):
                out_unit(0, u)
            pe.wait_ge(sem("o_sum"), 4 * T)
            pe.wait_ge(sem("y"), T)
            for q in range(2):
                for k in range(4):
                    for t in range(T):
                        ins = pe.transpose(yT_banks(q)[:, k, t * P:t * P + P], oy[:, t, 4 * q + k], ident[:])
                ins.then_inc(sem("yT_ps"), 1)
            out_unit(0, 3)
            for u in range(4, KU):
                pe.wait_ge(sem("y_lo"), (2 * u - AH) // 4 + 1)
                out_unit(0, u)
            with pe.Fori(1, OUT_CHUNKS) as c:
                for u in range(KU):
                    out_unit(c, u)

        block = ctx.enter_context(nc.Block())

        @block.sync
        def _(sp):
            x_v = x[0].rearrange("(t p) d -> p t d", p=P)

            def load_x(q):
                sp.dma_start(resid[:, :, q * BANK:(q + 1) * BANK], x_v[:, :, q * BANK:(q + 1) * BANK])\
                  .then_inc(sem(f"x_loaded{q}"), 16)

            load_x(0)
            load_x(1)
            ffn_loads(sp, 0, ffn1_w_gate[0], ffn1_w_up[0], ffn1_w_down[0], load_x)
            mixer_loads(sp)
            ffn_loads(sp, 1, ffn2_w_gate[0], ffn2_w_up[0], ffn2_w_down[0], None)
            out_v = out[0].rearrange("(t p) d -> p t d", p=P)
            for q in range(4):
                sp.wait_ge(sem("ln_out"), 16 + 2 * q + 2)
                sp.dma_start(out_v[:, :, q * BANK:(q + 1) * BANK], resid[:, :, q * BANK:(q + 1) * BANK])\
                  .then_inc(sem("stored"), 16)
            sp.wait_ge(sem("stored"), 64)

        @block.gpsimd
        def _(pool):
            pool.memset(ident[:], 1.0).then_inc(sem("ident"), 1)
            pool.memset(half_neg[:], -0.5).then_inc(sem("pow_ready"), 1)
            pool.wait_ge(sem("ident"), 1)
            pool.affine_select(out=ident[:], in_=ident[:], compare_op=ALU.is_equal, fill=0.0, base=0,
                               pattern=[[-1, P]], channel_multiplier=1).then_inc(sem("ident"), 1)
            pool.wait_ge(sem("pow_ready"), 1)
            pool.wait_ge(unit_used, st.index(F1D, OUT_CHUNKS - 1, KT // UNIT_KT))
            norm_gains(pool, ln1_g, ln1_b)
            norm_pool(pool, 0)
            mixer_pool(pool)
            pool.wait_ge(unit_used, st.index(F2D, OUT_CHUNKS - 1, KT // UNIT_KT))
            norm_gains(pool, ln3_g, ln3_b)
            norm_pool(pool, 2)

        @block.scalar
        def _(act):
            act.dma_start(cw_rows[:], conv_w[0].rearrange("a (t p) -> (a t) p", p=P)).then_inc(sem("cw_rows"), 16)
            for u in range(LEAD):
                split_hi(act, F1GU, 0, u)
            ffn_act(act, 0, False)
            mixer_act(act)
            ffn_act(act, 1, True)

        @block.vector
        def _(dve):
            for u in range(LEAD):
                to_xT_dve(dve, 0, u)
                split_lo(dve, F1GU, 0, u)
            ffn_dve(dve, 0, False)
            mixer_dve(dve)
            ffn_dve(dve, 1, True)
            norm_stats(dve, 2)
            for q in range(OUT_CHUNKS):
                norm_quarter(dve, 2, q)

        @block.tensor
        def _(pe):
            pe.wait_ge(sem("ident"), 2)
            pe.wait_ge(sem("cw_rows"), 16)
            pe.transpose(acc1[:, 0, 0:TAPS * CONV_TILES], cw_rows[:], ident[0:TAPS * CONV_TILES, 0:TAPS * CONV_TILES])\
              .then_inc(sem("cw_ps"), 1)
            pe.wait_ge(sem("cw"), 1)
            ffn_pe(pe, 0)
            mixer_pe(pe)
            ffn_pe(pe, 1)


_INS = ['x', 'ffn1_w_gate', 'ffn1_w_up', 'ffn1_w_down', 'ln1_g', 'ln1_b', 'w_in', 'q_norm_g', 'kv_norm_g',
        'w_uq', 'w_uk', 'w_uv', 'w_q_idx', 'k_idx_ln_g', 'k_idx_ln_b', 'conv_w', 'a_log', 'dt_bias', 'o_norm_g',
        'w_out', 'ln2_g', 'ln2_b', 'ffn2_w_gate', 'ffn2_w_up', 'ffn2_w_down', 'ln3_g', 'ln3_b']


def kernel(**inputs):
    import numpy as _np
    import concourse.bacc as _bacc
    from concourse import mybir as _mybir
    from concourse.bass_utils import run_bass_kernel_spmd as _run

    nc = _bacc.Bacc("TRN2", target_bir_lowering=False, num_devices=1)
    arrays, args = {}, []
    for name in _INS:
        a = _np.ascontiguousarray(inputs[name])
        arrays[f"in_{name}_dram"] = a
        args.append(nc.dram_tensor(f"in_{name}_dram", a.shape, _mybir.dt.from_np(a.dtype), kind="ExternalInput").ap())
    out = nc.dram_tensor("out_dram", arrays["in_x_dram"].shape, _mybir.dt.float32, kind="ExternalOutput").ap()
    hybrid_block(nc, *args, out)
    r = _run(nc, [arrays], core_ids=[0])
    return r.results[0]["out_dram"]
```

```python
from contextlib import ExitStack

import concourse.bass as bass
from concourse import mybir

ALU = mybir.AluOpType
ACT = mybir.ActivationFunctionType
F32 = mybir.dt.float32
F32R = mybir.dt.float32r
I32 = mybir.dt.int32
AX_X = mybir.AxisListType.X

P = 128
BANK = 512
EPS = 1e-6
ALPHA = 2.0 ** 0.25
UNIT_KT = 2
RAW_SLOTS = 8
SPLIT_SLOTS = 3
LEAD = 2
KEPT = 64
KB = 1024
START_WAIT, NORM_WAIT, SOFTMAX_WAIT = 6, 22, 24


class Phase:

    def __init__(self, name, iters, units, width):
        self.name, self.iters, self.units, self.width = name, iters, units, width


def ring_place(u, units, slots):
    if slots != SPLIT_SLOTS:
        return u % slots
    back = {0: 0, 1: 2, 2: 1}[units % slots]
    middle = max(1, units // 2)
    steps_back = min(max(u - middle, 0), back)
    return (u - 2 * steps_back) % slots


class Stream:

    def __init__(self, phases):
        self.phases = phases
        self.base = []
        self.loads = []
        at, loads = 0, [0] * RAW_SLOTS
        for ph in phases:
            self.base.append(at)
            self.loads.append(list(loads))
            at += ph.iters * ph.units
            for s in range(RAW_SLOTS):
                loads[s] += ph.iters * self.uses(ph, s)

    @staticmethod
    def uses(ph, s):
        return sum(ring_place(u, ph.units, RAW_SLOTS) == s for u in range(ph.units))

    def index(self, p, it, u):
        return it * self.phases[p].units + (self.base[p] + u)

    def loaded(self, p, it, u):
        n = self.phases[p].units
        if u >= n:
            it, u = it + 1, u - n
        s = ring_place(u, n, RAW_SLOTS)
        earlier = sum(ring_place(v, n, RAW_SLOTS) == s for v in range(u))
        return it * (16 * self.uses(self.phases[p], s)) + 16 * (self.loads[p][s] + earlier + 1)

    def freed(self, p, it, u, slots):
        n = self.phases[p].units
        over = u >= n
        if over:
            it, u = it + 1, u - n
        s = ring_place(u, n, slots)
        same = [v for v in range(u) if ring_place(v, n, slots) == s]
        if same:
            c = same[-1] + 1
        else:
            prev = [v for v in range(n) if ring_place(v, n, slots) == s]
            c = prev[-1] - n + 1 if prev else -n
            if not over:
                if p > 0:
                    m = self.phases[p - 1].units
                    prev = [v for v in range(m) if ring_place(v, m, slots) == s]
                    before = prev[-1] - m + 1 if prev else -m
                    c = max(c, before) if self.phases[p].iters > 1 else before
                elif isinstance(it, int) and it == 0:
                    return None
        return it * n + (self.base[p] + c)


def hybrid_block(nc, x, ffn1_w_gate, ffn1_w_up, ffn1_w_down, ln1_g, ln1_b, w_in, q_norm_g, kv_norm_g,
                 w_uq, w_uk, w_uv, w_q_idx, k_idx_ln_g, k_idx_ln_b, conv_w, a_log, dt_bias, o_norm_g,
                 w_out, ln2_g, ln2_b, ffn2_w_gate, ffn2_w_up, ffn2_w_down, ln3_g, ln3_b, out):
    T = x.shape[1] // P
    D = x.shape[2]
    KT = D // P
    FF = ffn1_w_gate.shape[2]
    FT = FF // P
    QR = q_norm_g.shape[1]
    KR = kv_norm_g.shape[1]
    AH, AD = w_uq.shape[2], w_uq.shape[3]
    ID = k_idx_ln_g.shape[1]
    IH = w_q_idx.shape[2] // ID
    BH = a_log.shape[1]
    BD = o_norm_g.shape[1]
    BW = BH * BD
    TAPS = conv_w.shape[1]
    S = T * P
    RT = KR // P
    QT = QR // P
    A_COLS = QR + KR + ID + IH
    Z_COLS = BW + 2 * BH
    CONV_TILES = 3 * BW // P
    A_SCALE = AD ** -0.5
    W_SCALE = IH ** -0.5 * ID ** -0.5
    assert T == 2 and D == 2048 and FT == 44 and AD == P and BD == P and ID == P

    GATE_CHUNKS = FF // BANK
    OUT_CHUNKS = D // BANK
    KU = KT // UNIT_KT
    DOWN_U = FT // UNIT_KT
    A_ITERS, C_ITERS = 2, 4
    A_W, C_W = A_COLS // A_ITERS, Z_COLS // C_ITERS
    B_ITERS = 3 * BW // BANK
    F1GU, F1D, WA, WB, WC, WQI, WUQ, WO, F2GU, F2D = range(10)
    QI_CHUNKS, UQ_CHUNKS, QU = IH * ID // BANK, AH * AD // BANK, QT // UNIT_KT
    st = Stream([
        Phase("ffn1 gate and up", GATE_CHUNKS, 2 * KU, BANK),
        Phase("ffn1 down", OUT_CHUNKS, DOWN_U, BANK),
        Phase("w_in: latents and index key", A_ITERS, KU, A_W),
        Phase("w_in: q k v", B_ITERS, KU, BANK),
        Phase("w_in: z a b", C_ITERS, KU, C_W),
        Phase("w_q_idx", 1, QI_CHUNKS * QU, BANK),
        Phase("w_uq", 1, UQ_CHUNKS * QU, BANK),
        Phase("w_out", OUT_CHUNKS, KU, BANK),
        Phase("ffn2 gate and up", GATE_CHUNKS, 2 * KU, BANK),
        Phase("ffn2 down", OUT_CHUNKS, DOWN_U, BANK),
    ])
    n0 = {F1GU: 0, F1D: 11, WA: 15, WB: 17, WC: 23, WQI: 27, WUQ: 29, WO: 30, F2GU: 34, F2D: 45}
    n1 = {F1GU: 0, WQI: 11, WUQ: 13, F2GU: 14}

    with ExitStack() as ctx:
        base = 16512
        MZ = base + 104 * KB

        def at(name, offset, shape, dt=F32):
            return nc.alloc_sbuf_tensor_at(name, shape, dt, offset=offset)

        def mz(name, kb, shape, dt=F32):
            return at(name, MZ + int(kb * KB), shape, dt)

        raw = at("raw", base, [P, RAW_SLOTS, UNIT_KT, BANK])
        whi = at("whi", base + 32 * KB, [P, SPLIT_SLOTS, UNIT_KT, BANK], F32R)
        wlo = at("wlo", base + 44 * KB, [P, SPLIT_SLOTS, UNIT_KT, BANK], F32R)
        xT = at("xT", base + 56 * KB, [P, KT, 2, S], F32R)
        resid = at("resid", base + 88 * KB, [P, T, D])

        hT = mz("hT", 0, [P, FT, 2, S], F32R)
        gated = mz("gated", 88, [P, T, BANK])
        ln_g = mz("ln_g", 0, [P, D])
        ln_b = mz("ln_b", 8, [P, D])

        qkvT = mz("qkvT", 0, [P, CONV_TILES, S])
        zab = mz("zab", 24, [P, T, Z_COLS])
        lat = mz("lat", 32.5, [P, T, A_COLS])
        xs = mz("xs", 40, [P, 4, S + TAPS - 1])
        up_to = mz("up_to", 45, [P, P])
        later = mz("later", 45.5, [P, P])
        in_half = mz("in_half", 46, [P, 2, P])
        not_ahead = mz("not_ahead", 47, [P, P])
        pair_mask = mz("pair_mask", 47.5, [P, 6, P])
        wuk = mz("wuk", 50.5, [P, AH, KR])
        wuv = mz("wuv", 90.5, [P, AH, RT, AD])
        qidxT = mz("qidxT", 66.5, [P, IH, S])
        th = mz("th", 66.5, [P, 4, S])
        qT = mz("qT", 82.5, [P, AH, S])
        cq_g = mz("cq_g", 82.5, [P, QR])
        ckv_g = mz("ckv_g", 84.5, [P, KR])
        ki_g = mz("ki_g", 85.5, [P, ID])
        ki_b = mz("ki_b", 86, [P, ID])
        cqT = mz("cqT", 90.5, [P, QT, 2, S], F32R)
        ckv = mz("ckv", 58.5, [P, T, KR])
        ckvT = mz("ckvT", 60.5, [P, RT, S])
        kidxT = mz("kidxT", 62.5, [P, S])
        sel = at("sel", base + 56 * KB, [P, T, S])
        ndist_i = at("ndist_i", base + 56 * KB, [P, T, S], I32)
        ndist = at("ndist", base + 58 * KB, [P, T, S])
        score = mz("score", 33, [P, T, S])
        work = mz("work", 35, [P, T, S])
        relu = mz("relu", 37, [P, 4, 2, S])
        qlatT = at("qlatT", base + 72 * KB, [P, RT, AH, S])
        prob0 = mz("prob0", 82.5, [P, AH, P])
        prob1 = mz("prob1", 50.5, [P, AH, S])
        pT0 = mz("pT0", 33, [P, AH, S])
        pT1 = mz("pT1", 41, [P, AH, P])
        olatT = mz("olatT", 66.5, [P, RT, AH, S])
        vb = mz("vb", 50.5, [P, T, BH, BD])
        kbeg = mz("kbeg", 58.5, [P, T, BH, BD])
        kdec = mz("kdec", 66.5, [P, T, BH, BD])
        aiT = mz("aiT", 74.5, [P, T, BH, P])
        aT = mz("aT", 82.5, [P, T, BH, P])
        sq = mz("sq", 70.5, [P, 2 * BH, S])
        dT = mz("dT", 90.5, [P, T, BH, P])
        xinv = mz("xinv", 90.5, [P, T, BH, P])
        kbT = mz("kbT", 33, [P, T, BH, P])
        yinv = mz("yinv", 33, [P, T, BH, P])
        kb = at("kb", base + 72 * KB, [P, T, BH, BD])
        lev = at("lev", base + 80 * KB, [P, T, BH, P])
        t1 = mz("t1", 16, [P, T, BH, P])
        nkcdT = mz("nkcdT", 82.5, [P, T, BH, P])
        state = mz("state", 90.5, [P, BH, BD])
        vnew = mz("vnew", 94.5, [P, BH, BD])
        thz_sb = at("thz_sb", base + 72 * KB, [P, T, BW])
        oy = mz("oy", 8, [P, T, BH, BD])
        small = mz("small", 98.5, [P, 24, T, BH])
        ktok = at("ktok", base + 80 * KB, [P, T, BH, BD])

        cz = base + 204 * KB
        ident = at("ident", cz, [P, P])
        cw = at("cw", cz + 512, [P, TAPS, CONV_TILES])
        cw_rows = mz("cw_rows", 89, [TAPS * CONV_TILES, P])
        stats = at("stats", cz + 896, [P, T, OUT_CHUNKS, 6])
        mv = at("mv", cz + 1088, [P, T, 2])
        rstd = at("rstd", cz + 1120, [P, T])
        shift = at("shift", cz + 2496, [P, T])
        half_neg = at("half_neg", cz + 1152, [P, 32])
        ss = at("ss", cz + 1280, [P, 3, T])
        rs = at("rs", cz + 1312, [P, 3, T])
        kmv = at("kmv", cz + 1344, [P, T, 2])
        kstats = at("kstats", cz + 1376, [P, T, 6])
        widx = at("widx", cz + 1440, [P, T, IH])
        top8 = at("top8", cz + 1568, [P, T, 8])
        amax = at("amax", cz + 1632, [P, T, AH])
        nmax = at("nmax", cz + 1696, [P, T, AH])
        psumm = at("psumm", cz + 1760, [P, T, AH])
        pinv = at("pinv", cz + 1824, [P, T, AH])
        alog = at("alog", cz + 1888, [P, BH])
        dtb = at("dtb", cz + 1920, [P, BH])
        og = at("og", cz + 1952, [P, BD])
        ones = at("ones", cz + 2464, [P, 2])

        def psum(name, shape):
            return ctx.enter_context(nc.psum_tensor(name, shape, F32))

        acc0 = psum("acc0", [P, 2, BANK])
        acc1 = psum("acc1", [P, 2, BANK])
        tp = psum("tp", [P, 4, BANK])

        class Sems:

            def __init__(self):
                self.made = {}

            def __call__(self, name):
                if name not in self.made:
                    self.made[name] = ctx.enter_context(nc.semaphore("s_" + name))
                return self.made[name]

        sem = Sems()
        raw_loaded = [sem(f"raw_loaded{i}") for i in range(RAW_SLOTS)]
        hi_done, lo_done, unit_used = sem("hi_done"), sem("lo_done"), sem("unit_used")
        acc0a_done = sem("acc0a_done")
        acc0_free = [sem("acc0a_free"), sem("acc0b_free")]
        acc1_free = [sem("acc1a_free"), sem("acc1b_free")]

        def wait(eng, s, value):
            if not (isinstance(value, int) and value <= 0):
                eng.wait_ge(s, value)

        def load_unit(sp, p, it, u, src):
            s = ring_place(u, st.phases[p].units, RAW_SLOTS)
            free = st.freed(p, it, u, RAW_SLOTS)
            if free is not None:
                wait(sp, lo_done, free)
            sp.dma_start(raw[:, s, :, 0:src.shape[2]], src).then_inc(raw_loaded[s], 16)

        def cut_width(p, u):
            return st.phases[p].width if u < st.phases[p].units else BANK

        def split_hi(act, p, it, u):
            n, w = st.phases[p].units, cut_width(p, u)
            s, r = ring_place(u % n, n, SPLIT_SLOTS), ring_place(u % n, n, RAW_SLOTS)
            act.wait_ge(raw_loaded[r], st.loaded(p, it, u))
            free = st.freed(p, it, u, SPLIT_SLOTS)
            if free is not None:
                wait(act, unit_used, free)
            act.activation(whi[:, s, :, 0:w], raw[:, r, :, 0:w], ACT.Copy).then_inc(hi_done, 1)

        def split_lo(dve, p, it, u):
            n, w = st.phases[p].units, cut_width(p, u)
            s, r = ring_place(u % n, n, SPLIT_SLOTS), ring_place(u % n, n, RAW_SLOTS)
            dve.wait_ge(hi_done, st.index(p, it, u + 1))
            dve.tensor_tensor(wlo[:, s, :, 0:w], raw[:, r, :, 0:w], whi[:, s, :, 0:w].bitcast(F32),
                              ALU.subtract).then_inc(lo_done, 1)

        def unit_mm(pe, p, it, u, acc, free, n_chunk, moving, stat, kt0, first, last, a_done=None):
            n = st.phases[p].units
            s = ring_place(u, n, SPLIT_SLOTS)
            width = st.phases[p].width
            pe.wait_ge(lo_done, st.index(p, it, u + 1))
            for half in range(2):
                if first and n_chunk is not None:
                    wait(pe, free[half], n_chunk)
                if moving == "w":
                    for k in range(UNIT_KT):
                        kt = kt0 + k
                        hi = stat[:, kt, 0, half * P:half * P + P]
                        lo = stat[:, kt, 1, half * P:half * P + P]
                        o = acc[:, half, 0:width]
                        pe.matmul(o, hi, whi[:, s, k, 0:width], start=first and k == 0, stop=False)
                        pe.matmul(o, hi, wlo[:, s, k, 0:width], start=False, stop=False)
                        ins = pe.matmul(o, lo, whi[:, s, k, 0:width], start=False,
                                        stop=last and k == UNIT_KT - 1)
                else:
                    for c in range(2):
                        cols = slice((2 * half + c) * P, (2 * half + c) * P + P)
                        o = acc[:, half, c * S:c * S + S]
                        for k in range(UNIT_KT):
                            hi, lo = stat[:, kt0 + k, 0, :], stat[:, kt0 + k, 1, :]
                            end = last and k == UNIT_KT - 1
                            pe.matmul(o, whi[:, s, k, cols], hi, start=first and k == 0 and c == 0,
                                      stop=False, skip_group_check=True)
                            pe.matmul(o, whi[:, s, k, cols], lo, start=False, stop=False,
                                      skip_group_check=True)
                            ins = pe.matmul(o, wlo[:, s, k, cols], hi, start=False, stop=end,
                                            skip_group_check=True)
                if half == 0 and last and a_done is not None:
                    ins.then_inc(a_done, 1)
            ins.then_inc(unit_used, 1)

        def halves(bank):
            return bank.rearrange("p (k s) -> p k s", k=2)

        def to_xT_pe(pe, e, q):
            if e == 0:
                pe.wait_ge(sem(f"x_loaded{q}"), 16)
            if 4 * e + q >= 2:
                pe.wait_ge(sem("xT_lo"), 4 * e + q - 1)
            for t in range(T):
                if e > 0 and q == 0:
                    pe.wait_ge(sem("ln_out"), 5 * (e - 1) + t + 1)
                elif e > 0:
                    normed(pe, e - 1, q)
                for k in range(4):
                    ins = pe.transpose(tp[:, 2 * (q % 2) + k // 2, (k % 2) * S + t * P:(k % 2) * S + t * P + P],
                                       resid[:, t, (4 * q + k) * P:(4 * q + k + 1) * P], ident[:])
            ins.then_inc(sem("xT_ps"), 1)

        def keep_warm(pe, p, bank, times):
            s = ring_place(0, st.phases[p].units, SPLIT_SLOTS)
            pe.wait_ge(lo_done, st.index(p, 0, 1))
            for _ in range(times):
                pe.matmul(bank, whi[:, s, 0, 0:P], whi[:, s, 1, :], start=True, stop=True)

        def entry_pe(pe, e, u):
            if u == 0 and e > 0:
                keep_warm(pe, (WA, F2GU)[e - 1], tp[:, 0], NORM_WAIT)
            if u == 0:
                to_xT_pe(pe, e, 0)
            elif u in (1, 3, 5):
                to_xT_pe(pe, e, (u + 1) // 2)
            if u == 0:
                pe.wait_ge(sem("xT_lo_first"), e + 1)
            else:
                pe.wait_ge(sem("xT_lo"), 4 * e + u // 2 + 1)

        def tp_pair(i):
            return tp[:, 2 * i:2 * i + 2, :].rearrange("p b (k s) -> p (b k) s", k=2)

        def to_xT_act(act, e, q):
            act.wait_ge(sem("xT_ps"), 4 * e + q + 1)
            if q == 0:
                act.activation(xT[:, 0:UNIT_KT, 0, :], halves(tp[:, 0]), ACT.Copy).then_inc(sem("xT_hi_first"), 1)
                act.activation(xT[:, UNIT_KT:4, 0, :], halves(tp[:, 1]), ACT.Copy).then_inc(sem("xT_hi"), 1)
                return
            act.activation(xT[:, 4 * q:4 * q + 4, 0, :], tp_pair(q % 2), ACT.Copy).then_inc(sem("xT_hi"), 1)

        def entry_act(act, e, u):
            if u == LEAD - 1:
                norm_act(act, e - 1)
            q = {LEAD - 1: 0, 2: 1, 4: 2, 6: 3}.get(u)
            if q is not None:
                to_xT_act(act, e, q)

        def to_xT_dve(dve, e, q):
            if q == 0:
                dve.wait_ge(sem("xT_hi_first"), e + 1)
                dve.tensor_tensor(xT[:, 0:UNIT_KT, 1, :], halves(tp[:, 0]), xT[:, 0:UNIT_KT, 0, :].bitcast(F32),
                                  ALU.subtract).then_inc(sem("xT_lo_first"), 1)
                dve.wait_ge(sem("xT_hi"), 4 * e + 1)
                dve.tensor_tensor(xT[:, UNIT_KT:4, 1, :], halves(tp[:, 1]), xT[:, UNIT_KT:4, 0, :].bitcast(F32),
                                  ALU.subtract).then_inc(sem("xT_lo"), 1)
                return
            dve.wait_ge(sem("xT_hi"), 4 * e + q + 1)
            dve.tensor_tensor(xT[:, 4 * q:4 * q + 4, 1, :], tp_pair(q % 2),
                              xT[:, 4 * q:4 * q + 4, 0, :].bitcast(F32), ALU.subtract).then_inc(sem("xT_lo"), 1)

        def norm_stats(dve, e, p=None):
            for t in range(T):
                dve.wait_ge(sem("stats"), T * OUT_CHUNKS * (e + 1))
                dve.bn_aggr(mv[:, t], stats[:, t]).then_inc(sem("ln_mv"), 1)
            if p is not None:
                split_lo(dve, p, st.phases[p].iters - 1, st.phases[p].units + LEAD - 1)
            dve.wait_ge(sem("ln_rstd"), 2 * e + 2)
            dve.scalar_tensor_tensor(out=shift[:], in0=mv[:, :, 0], scalar=-1.0, in1=rstd[:], op0=ALU.mult,
                                     op1=ALU.mult).then_inc(sem("ln_shift"), 1)
            dve.wait_ge(sem("ln_gains"), 32 * (e + 1))

        NORM_STEPS = [2, 3, 4, 5]

        def normed(eng, e, q):
            eng.wait_ge(sem("ln_out"), 5 * e + NORM_STEPS[q])
            if q >= 1:
                eng.wait_ge(sem("ln_out_pool"), 3 * e + q)

        def norm_quarter(dve, e, q):
            cols = slice(q * BANK, q * BANK + BANK)
            tiles = range(T) if q == 0 else range(1)
            for t in tiles:
                dve.scalar_tensor_tensor(out=resid[:, t, cols], in0=resid[:, t, cols], scalar=mv[:, t, 0:1],
                                         in1=ln_g[:, cols], op0=ALU.subtract, op1=ALU.mult)\
                   .then_inc(sem("ln_mid"), 1)
            for t in tiles:
                dve.wait_ge(sem("ln_mid"), 5 * e + NORM_STEPS[q] - len(tiles) + t + 1)
                dve.scalar_tensor_tensor(out=resid[:, t, cols], in0=resid[:, t, cols], scalar=rstd[:, t:t + 1],
                                         in1=ln_b[:, cols], op0=ALU.mult, op1=ALU.add)\
                   .then_inc(sem("ln_out"), 1)

        def entry_dve(dve, e, u):
            if u == LEAD - 1:
                norm_stats(dve, e - 1, (F1D, WO)[e - 1])
                norm_quarter(dve, e - 1, 0)
                norm_quarter(dve, e - 1, 1)
                to_xT_dve(dve, e, 0)
            elif u == 2:
                to_xT_dve(dve, e, 1)
                if e > 0:
                    norm_quarter(dve, e - 1, 2)
            elif u == 4:
                to_xT_dve(dve, e, 2)
                if e > 0:
                    norm_quarter(dve, e - 1, 3)
            elif u == 6:
                to_xT_dve(dve, e, 3)

        def norm_gains(pool, g, b):
            for dst, src in ((ln_g, g), (ln_b, b)):
                pool.dma_start(dst[:], src.to_broadcast([P, D])).then_inc(sem("ln_gains"), 16)

        def norm_pool(pool, e):
            pool.wait_ge(sem("ln_mv"), 2 * e + 2)
            pool.tensor_scalar(rstd[:], mv[:, :, 1], EPS / ALPHA ** 2, None, ALU.add).then_inc(sem("ln_rstd"), 1)
            pool.wait_ge(sem("ln_rstd"), 2 * e + 1)
            pool.tensor_tensor(rstd[:], rstd[:], half_neg[:, 0:T], ALU.pow).then_inc(sem("ln_rstd"), 1)
            pool.wait_ge(sem("ln_rstd"), 2 * e + 2)
            pool.wait_ge(sem("ln_gains"), 32 * (e + 1))
            for q in range(1, 4):
                part, step = resid[:, T - 1, q * BANK:q * BANK + BANK], 3 * e + q
                pool.wait_ge(sem("ln_centred"), step)
                pool.tensor_tensor(part, part, ln_g[:, q * BANK:q * BANK + BANK], ALU.mult)\
                    .then_inc(sem("ln_mid_pool"), 1)
                pool.wait_ge(sem("ln_mid_pool"), step)
                pool.tensor_tensor(part, part, ln_b[:, q * BANK:q * BANK + BANK], ALU.add)\
                    .then_inc(sem("ln_out_pool"), 1)

        def norm_act(act, e):
            act.wait_ge(sem("ln_shift"), e + 1)
            for q in range(1, 4):
                part = resid[:, T - 1, q * BANK:q * BANK + BANK]
                act.activation(part, part, ACT.Identity, scale=rstd[:, T - 1:T], bias=shift[:, T - 1:T])\
                   .then_inc(sem("ln_centred"), 1)

        GU, DN = [F1GU, F2GU], [F1D, F2D]

        def ffn_loads(sp, f, w_gate, w_up, w_down, load_x):
            gate_v = w_gate.rearrange("(k p) n -> p k n", p=P)
            up_v = w_up.rearrange("(k p) n -> p k n", p=P)
            down_v = w_down.rearrange("(k p) n -> p k n", p=P)

            def gate_up(c, x_between=None):
                for v, view in ((0, gate_v), (KU, up_v)):
                    for u in range(KU):
                        load_unit(sp, GU[f], c, v + u, view[:, 2 * u:2 * u + 2, bass.ds(c * BANK, BANK)])
                        if x_between and v + u in (1, 3, 5):
                            x_between((v + u + 1) // 2)

            gate_up(0, load_x)
            with sp.Fori(1, GATE_CHUNKS) as c:
                gate_up(c)
            with sp.Fori(0, OUT_CHUNKS) as c:
                for u in range(DOWN_U):
                    load_unit(sp, DN[f], c, u, down_v[:, 2 * u:2 * u + 2, bass.ds(c * BANK, BANK)])

        def hT_pe(pe, f, c):
            for half in range(2):
                pe.wait_ge(acc1_free[half], c + n1[GU[f]])
            for k in range(4):
                for t in range(T):
                    ins = pe.transpose(tp[:, k // 2, (k % 2) * S + t * P:(k % 2) * S + t * P + P],
                                       gated[:, t, k * P:k * P + P], ident[:])
            ins.then_inc(sem("hT_ps"), 1)

        def hT_act(act, f, c):
            act.wait_ge(sem("hT_ps"), c + f * GATE_CHUNKS)
            act.activation(hT[:, bass.ds(4 * (c - 1), 4), 0, :], tp_pair(0), ACT.Copy).then_inc(sem("hT_hi"), 1)

        def hT_dve(dve, f, c):
            dve.wait_ge(sem("hT_hi"), c + f * GATE_CHUNKS)
            dve.tensor_tensor(hT[:, bass.ds(4 * (c - 1), 4), 1, :], tp_pair(0),
                              hT[:, bass.ds(4 * (c - 1), 4), 0, :].bitcast(F32), ALU.subtract)\
               .then_inc(sem("hT_lo"), 1)

        def gate_times_up(dve, f, c):
            dve.wait_ge(unit_used, st.index(GU[f], c, 0))
            for t in range(T):
                dve.wait_ge(acc0_free[t], c + n0[GU[f]])
                dve.tensor_tensor(gated[:, t], gated[:, t], acc1[:, t], ALU.mult).then_inc(acc1_free[t], 1)

        def ffn_pe(pe, f):
            def gate_up(c, prev):
                for u in range(KU):
                    if not prev:
                        entry_pe(pe, 2 * f, u)
                    unit_mm(pe, GU[f], c, u, acc0, acc0_free, c + n0[GU[f]], "w", xT, 2 * u, u == 0, u == KU - 1,
                            acc0a_done)
                    if u == 3 and prev:
                        hT_pe(pe, f, c)
                if not prev and f == 0:
                    pe.wait_ge(sem("cw"), 1)
                for u in range(KU):
                    unit_mm(pe, GU[f], c, KU + u, acc1, acc1_free, c + n1[GU[f]], "w", xT, 2 * u, u == 0,
                            u == KU - 1)

            gate_up(0, False)
            with pe.Fori(1, GATE_CHUNKS) as c:
                gate_up(c, True)

            def down(c, tail):
                for u in range(DOWN_U):
                    if tail and u == 0:
                        pe.wait_ge(sem("hT_lo"), (f + 1) * GATE_CHUNKS - 1)
                    if tail and 4 * (GATE_CHUNKS - 1) == 2 * u:
                        pe.wait_ge(sem("hT_lo"), (f + 1) * GATE_CHUNKS)
                    unit_mm(pe, DN[f], c, u, acc0, acc0_free, c + n0[DN[f]], "w", hT, 2 * u, u == 0,
                            u == DOWN_U - 1, acc0a_done)
                    if tail and u == 3:
                        hT_pe(pe, f, GATE_CHUNKS)

            down(0, True)
            with pe.Fori(1, OUT_CHUNKS) as c:
                down(c, False)

        def ffn_act(act, f, last):
            def gate_up(c, prev):
                if not prev and f > 0:
                    entry_act(act, 2 * f, LEAD - 1)
                for u in range(LEAD, 2 * KU + LEAD):
                    split_hi(act, GU[f], c, u)
                    if not prev:
                        entry_act(act, 2 * f, u)
                    if not prev and f == 0 and u == 3:
                        act.wait_ge(sem("cw_ps"), 1)
                        act.activation(cw[:].rearrange("p a t -> p (a t)"), acc1[:, 0, 0:TAPS * CONV_TILES],
                                       ACT.Copy).then_inc(sem("cw"), 1)
                    if u == 6 and prev:
                        hT_act(act, f, c)
                    if u == KU + 1:
                        act.wait_ge(unit_used, st.index(GU[f], c, KU))
                        if prev or f > 0:
                            act.wait_ge(sem("hT_ps"), c + f * GATE_CHUNKS)
                        act.activation(gated[:], acc0[:], ACT.Tanh, scale=0.5).then_inc(sem("tanh_gate"), 1)

            gate_up(0, False)
            with act.Fori(1, GATE_CHUNKS) as c:
                gate_up(c, True)

            def down(c, tail, lead):
                for u in range(LEAD, DOWN_U + lead):
                    split_hi(act, DN[f], c, u)
                    if u == 6 and tail:
                        hT_act(act, f, GATE_CHUNKS)

            down(0, True, LEAD)
            with act.Fori(1, OUT_CHUNKS - 1) as c:
                down(c, False, LEAD)
            down(OUT_CHUNKS - 1, False, 0 if last else LEAD)

        def into_resid(dve, p, c, scale, in_phase):
            cols = bass.ds(c * BANK, BANK)
            for t in range(T):
                if t == 0:
                    dve.wait_ge(acc0a_done, c + (n0[p] + 1))
                else:
                    dve.wait_ge(unit_used, st.index(p, c, in_phase))
                dve.scalar_tensor_tensor(out=resid[:, t, cols], in0=acc0[:, t], scalar=scale,
                                         in1=resid[:, t, cols], op0=ALU.mult, op1=ALU.add)\
                   .then_inc(acc0_free[t], 1)
                dve.wait_ge(acc0_free[t], c + (n0[p] + 1))
                if isinstance(c, int):
                    where = stats[:, t, c]
                else:
                    where = stats[:, t, bass.ds(c, 1), :].rearrange("p a s -> p (a s)")
                dve.bn_stats(where, resid[:, t, cols]).then_inc(sem("stats"), 1)

        def ffn_dve(dve, f, last):
            def gate_up(c, prev):
                if prev:
                    gate_times_up(dve, f, c)
                elif f > 0:
                    entry_dve(dve, 2 * f, LEAD - 1)
                for u in range(LEAD, 2 * KU + LEAD):
                    split_lo(dve, GU[f], c, u)
                    if not prev:
                        entry_dve(dve, 2 * f, u)
                    if u == 6 and prev:
                        hT_dve(dve, f, c)
                    if u == KU + 1:
                        dve.wait_ge(sem("tanh_gate"), c + (f * GATE_CHUNKS + 1))
                        for t in range(T):
                            dve.scalar_tensor_tensor(out=gated[:, t], in0=gated[:, t], scalar=1.0, in1=acc0[:, t],
                                                     op0=ALU.add, op1=ALU.mult).then_inc(acc0_free[t], 1)

            gate_up(0, False)
            with dve.Fori(1, GATE_CHUNKS) as c:
                gate_up(c, True)

            def down(c, tail, lead):
                if tail:
                    gate_times_up(dve, f, GATE_CHUNKS)
                for u in range(LEAD, DOWN_U + lead):
                    split_lo(dve, DN[f], c, u)
                    if u == 6 and tail:
                        hT_dve(dve, f, GATE_CHUNKS)
                into_resid(dve, DN[f], c, 0.25 / ALPHA, DOWN_U)

            down(0, True, LEAD)
            with dve.Fori(1, OUT_CHUNKS - 1) as c:
                down(c, False, LEAD)
            down(OUT_CHUNKS - 1, False, 0 if last else LEAD - 1)

        NEG = -1e30
        SOFTMAX = [(0, slice(0, AH)), (1, slice(0, AH // 2)), (1, slice(AH // 2, AH))]
        PART_ORDER = (1, 0, 2)
        RANK = {1: 1, 0: 2, 2: 3}
        EXPS = {1: AH // 2, 0: AH // 2 + AH, 2: 2 * AH}
        CAUSAL_FILL, TAKEN = -3e38, -3.3e38
        G8 = BH // 2
        GROUPS = [(t, hh) for t in range(T) for hh in range(2)]
        LEVELS = 5
        NAMES = ["xa", "ax", "spl", "sp", "beta", "tb", "g", "eg", "ekd", "gc", "rq", "rk", "cd0", "cd1",
                 "c1", "c2", "c3", "vbs", "qs", "qs2", "sso", "ro", "co", "lk"]
        assert len(NAMES) <= 24

        def sm(name):
            return small[:, NAMES.index(name)]

        def sm_group(name, t, hh):
            return sm(name)[:, t, G8 * hh:G8 * hh + G8].unsqueeze(2).to_broadcast([P, G8, P])

        def group(tile, t, hh):
            return tile[:, t, G8 * hh:G8 * hh + G8, :]

        def bankE(i):
            return (acc0, acc0, acc1, acc1)[i][:, i % 2]

        def bankF(i):
            return tp[:, i]

        def heads4(bank):
            return bank.rearrange("p (h c) -> p h c", h=G8)

        def kT_of(h, t):
            return qkvT[:, BH + h, t * P:t * P + P]

        def vT_of(h, t):
            return qkvT[:, 2 * BH + h, t * P:t * P + P]

        def qT_of(h, t):
            return qkvT[:, h, t * P:t * P + P]

        def mixer_loads(sp):
            in_v = w_in[0].rearrange("(k p) n -> p k n", p=P)
            for p, iters, width, col0 in ((WA, A_ITERS, A_W, 0), (WB, B_ITERS, BANK, A_COLS),
                                          (WC, C_ITERS, C_W, A_COLS + 3 * BW)):
                with sp.Fori(0, iters) as c:
                    for u in range(KU):
                        load_unit(sp, p, c, u, in_v[:, 2 * u:2 * u + 2, bass.ds(c * width + col0, width)])
            qi_v = w_q_idx[0].rearrange("(k p) n -> p k n", p=P)
            uq_v = w_uq[0].rearrange("(k p) h d -> p k (h d)", p=P)
            for p, view, chunks in ((WQI, qi_v, QI_CHUNKS), (WUQ, uq_v, UQ_CHUNKS)):
                for j in range(chunks):
                    for u in range(QU):
                        load_unit(sp, p, 0, j * QU + u, view[:, 2 * u:2 * u + 2, j * BANK:(j + 1) * BANK])
            out_v = w_out[0].rearrange("(k p) n -> p k n", p=P)
            with sp.Fori(0, OUT_CHUNKS) as c:
                for u in range(KU):
                    load_unit(sp, WO, c, u, out_v[:, 2 * u:2 * u + 2, bass.ds(c * BANK, BANK)])

        def mixer_pool(pool):
            pool.wait_ge(unit_used, st.index(WA, 0, 0))
            for dst, src, n in ((cq_g, q_norm_g, QR), (ckv_g, kv_norm_g, KR), (ki_g, k_idx_ln_g, ID),
                                (ki_b, k_idx_ln_b, ID)):
                pool.dma_start(dst[:], src.to_broadcast([P, n])).then_inc(sem("latent_gains"), 16)
            for dst, src, n in ((alog, a_log, BH), (dtb, dt_bias, BH), (og, o_norm_g, BD)):
                pool.dma_start(dst[:], src.to_broadcast([P, n])).then_inc(sem("delta_gains"), 16)
            pool.memset(xs[:, :, 0:TAPS - 1], 0.0).then_inc(sem("xs_th_free"), 1)
            pool.memset(ones[:], 1.0).then_inc(sem("ones"), 1)
            pool.dma_start(wuk[:], w_uk[0].rearrange("h d r -> d h r")).then_inc(sem("wuk"), 16)
            pool.wait_ge(sem("lat_ss"), 2 * T)
            pool.wait_ge(sem("k_mv"), T)
            pool.tensor_scalar(rs[:, 0], ss[:, 0], 1.0 / QR, EPS, ALU.mult, ALU.add).then_inc(sem("lat_rs"), 1)
            pool.tensor_scalar(rs[:, 1], ss[:, 1], 1.0 / KR, EPS, ALU.mult, ALU.add).then_inc(sem("lat_rs"), 1)
            pool.tensor_scalar(rs[:, 2], kmv[:, :, 1], EPS, None, ALU.add).then_inc(sem("lat_rs"), 1)
            pool.wait_ge(sem("lat_rs"), 3)
            rs_flat = rs[:].rearrange("p a t -> p (a t)")
            pool.tensor_tensor(rs_flat, rs_flat, half_neg[:, 0:3 * T], ALU.pow).then_inc(sem("lat_rs"), 1)
            CH = P // 2
            marks = [0]

            def mark(ins):
                ins.then_inc(sem("masks"), 1)
                marks[0] += 1

            def chunked(ap):
                return ap.rearrange("p (b j) -> p b j", b=2)

            mark(pool.memset(up_to[:], 1.0))
            mark(pool.memset(later[:], 1.0))
            mark(pool.memset(in_half[:], 1.0))
            mark(pool.memset(not_ahead[:], 0.0))
            mark(pool.memset(pair_mask[:], 0.0))
            pool.wait_ge(sem("masks"), marks[0])
            for i in range(6):
                m = 1 << i
                v = pair_mask[:, i].rearrange("p (b h j) -> p b h j", h=2, j=m)
                mark(pool.memset(v[:, :, 1, :], 1.0))

            def keep(ap, base_, pattern, mult, fill=0.0):
                mark(pool.affine_select(out=ap, in_=ap, compare_op=ALU.is_ge, fill=fill, base=base_,
                                        pattern=pattern, channel_multiplier=mult))

            keep(chunked(up_to[:]), 0, [[CH, 2], [1, CH]], -1)
            keep(chunked(not_ahead[:]), 0, [[CH, 2], [1, CH]], -1, NEG)
            keep(chunked(later[:]), -1, [[-CH, 2], [-1, CH]], 1)
            keep(in_half[:, 0], CH - 1, [[0, P]], -1)
            keep(in_half[:, 1], -CH, [[0, P]], 1)
            pool.wait_ge(sem("masks"), marks[0])
            keep(chunked(up_to[:]), 0, [[-CH, 2], [0, CH]], 1)
            keep(chunked(not_ahead[:]), 0, [[-CH, 2], [0, CH]], 1, NEG)
            keep(chunked(later[:]), CH - 1, [[CH, 2], [0, CH]], -1)
            views = []
            for i in range(6):
                m = 1 << i
                v = pair_mask[:, i].rearrange("p (b h j) -> p b (h j)", h=2, j=m)
                views.append((m, P // (2 * m), v))
                keep(v, 0, [[-2 * m, P // (2 * m)], [0, 2 * m]], 1)
            pool.wait_ge(sem("masks"), marks[0])
            for m, nb, v in views:
                keep(v, m - 1, [[2 * m, nb], [0, 2 * m]], -1)
            assert marks[0] == MASKS

            pool.wait_ge(unit_used, st.index(WQI, 0, 0))
            pool.iota(ndist_i[:], pattern=[[-P, T], [1, S]], base=0, channel_multiplier=-1).then_inc(sem("ndist"), 1)
            pool.wait_ge(sem("ndist"), 1)
            pool.tensor_copy(ndist[:], ndist_i[:]).then_inc(sem("ndist"), 1)

            pool.wait_ge(sem("qk_ss"), 1)
            qk = small[:, NAMES.index("rq"):NAMES.index("rq") + 2].rearrange("p a t h -> p (a t h)")
            pool.tensor_scalar(qk, qk, 4 * EPS, None, ALU.add).then_inc(sem("qk_r"), 1)
            pool.wait_ge(sem("qk_r"), 1)
            pool.wait_ge(sem("log_k"), 1)
            pool.tensor_tensor(qk, qk, half_neg[:, 0:2 * T * BH], ALU.pow).then_inc(sem("qk_r"), 1)
            pool.wait_ge(unit_used, st.index(WO, 0, 0))
            pool.dma_start(wuv[:], w_uv[0].rearrange("h (t r) d -> r h t d", r=P)).then_inc(sem("wuv"), 16)
            pool.wait_ge(sem("score_acc"), 2 * IH)
            for t in range(T):
                n = (t + 1) * P
                pool.affine_select(out=score[:, t, 0:n], in_=score[:, t, 0:n], compare_op=ALU.is_ge,
                                   fill=CAUSAL_FILL, base=t * P, pattern=[[-1, n]], channel_multiplier=1)\
                    .then_inc(sem("score_masked"), 1)
            for t in range(T):
                n = (t + 1) * P
                pool.wait_ge(sem("sel_raw"), 2 * T)
                pool.affine_select(out=sel[:, t, 0:n], in_=sel[:, t, 0:n], compare_op=ALU.is_ge,
                                   fill=NEG, base=t * P, pattern=[[-1, n]], channel_multiplier=1)\
                    .then_inc(sem("sel"), 1)
            pool.wait_ge(sem("att_z"), AH)
            pool.wait_ge(sem("sel"), T)
            pool.tensor_tensor(prob0[:], prob0[:], sel[:, 0, 0:P].unsqueeze(1).to_broadcast([P, AH, P]), ALU.add)\
                .then_inc(sem("att_sel0"), 1)
            pool.wait_ge(sem("factors"), 6)
            for n, (t, hh) in enumerate(GROUPS):
                pool.wait_ge(sem("ktok"), n + 1)
                pool.tensor_tensor(group(kb, t, hh), group(ktok, t, hh), sm_group("c1", t, hh), ALU.mult)\
                    .then_inc(sem("kb"), 1)
            pool.wait_ge(sem("pinv"), 1)
            pool.tensor_tensor(prob0[:], prob0[:], pinv[:, 0].unsqueeze(2).to_broadcast([P, AH, P]), ALU.mult)\
                .then_inc(sem("prob0"), 1)
            pool.wait_ge(sem("oT_ps"), AH)
            for n, (t, hh) in enumerate(GROUPS):
                for dst, f in ((kbeg, "c2"), (kdec, "c3")):
                    pool.tensor_tensor(group(dst, t, hh), group(ktok, t, hh), sm_group(f, t, hh), ALU.mult)\
                        .then_inc(sem("k_scaled"), 1)
            pool.wait_ge(sem("k_scaled"), 8)
            for lvl in range(1, LEVELS + 1):
                for n, (t, hh) in enumerate(GROUPS):
                    if lvl == 1:
                        pool.wait_ge(sem("kk_m"), n + 1)
                    else:
                        pool.wait_ge(sem("t1_ps"), 4 * (lvl - 2) + n + 1)
                    pool.tensor_tensor(group(lev, t, hh), group(aT, t, hh),
                                       pair_mask[:, lvl].unsqueeze(1).to_broadcast([P, G8, P]), ALU.mult)\
                        .then_inc(sem("lev"), 1)
                if lvl == 1:
                    for n, (t, hh) in enumerate(GROUPS):
                        pool.wait_ge(sem("vtok"), n + 1)
                        pool.tensor_tensor(group(vb, t, hh), group(vb, t, hh), sm_group("vbs", t, hh), ALU.mult)\
                            .then_inc(sem("v_scaled"), 1)
            for t in range(T):
                ro = sm("ro")[:, t]
                if t == T - 1:
                    z_tile(pool, t)
                pool.wait_ge(sem("o_ms"), t + 1)
                pool.tensor_scalar(ro, sm("sso")[:, t], EPS, None, ALU.add).then_inc(sem("o_r"), 1)
                pool.wait_ge(sem("o_r"), 2 * t + 1)
                pool.tensor_tensor(ro, ro, half_neg[:, 0:BH], ALU.pow).then_inc(sem("o_r"), 1)
            pool.wait_ge(sem("y_lo"), 2)
            pool.wait_ge(unit_used, st.index(WO, 2, 0))
            norm_gains(pool, ln2_g, ln2_b)
            norm_pool(pool, 1)

        MASKS = 5 + 6 + 5 + 3 + 6 + 6
        SCORE_ITEMS = IH

        def mixer_act(act):
            def read_acc0(p, c, units, dst):
                for t in range(T):
                    if t == 0:
                        act.wait_ge(acc0a_done, c + (n0[p] + 1))
                    else:
                        act.wait_ge(unit_used, st.index(p, c, units))
                    w = st.phases[p].width
                    act.activation(dst[:, t, bass.ds(c * w, w)], acc0[:, t, 0:w], ACT.Copy)\
                       .then_inc(acc0_free[t], 1)

            entry_act(act, 1, LEAD - 1)
            for u in range(LEAD, KU + LEAD):
                split_hi(act, WA, 0, u)
                entry_act(act, 1, u)
            read_acc0(WA, 0, KU, lat)
            with act.Fori(1, A_ITERS) as c:
                for u in range(LEAD, KU + LEAD):
                    split_hi(act, WA, c, u)
                read_acc0(WA, c, KU, lat)
            squares = qidxT[:].rearrange("p h s -> p (h s)")

            def latent_squares(t):
                act.wait_ge(acc0_free[t], n0[WB])
                act.activation(squares[:, 1024 * t:1024 * t + QR], lat[:, t, 0:QR], ACT.Square,
                               accum_out=ss[:, 0, t:t + 1]).then_inc(sem("lat_ss"), 1)
                act.activation(squares[:, 1024 * t + QR:1024 * t + QR + KR], lat[:, t, QR:QR + KR], ACT.Square,
                               accum_out=ss[:, 1, t:t + 1]).then_inc(sem("lat_ss"), 1)

            def conv_tanh(c):
                act.wait_ge(sem("conv_sum"), c * 16 + 16)
                act.activation(th[:], qkvT[:, bass.ds(4 * c, 4), :], ACT.Tanh, scale=0.5)\
                   .then_inc(sem("qkv_tanh"), 1)

            def qkv_chunk(c, prev):
                for u in range(LEAD, KU + LEAD):
                    split_hi(act, WB, c, u)
                    if u == 4 and prev:
                        conv_tanh(c - 1)
                    if u in (2, 3) and not prev:
                        latent_squares(u - 2)
                act.wait_ge(sem("xs_th_free"), c + 1)
                for half in range(2):
                    if half == 0:
                        act.wait_ge(acc0a_done, c + (n0[WB] + 1))
                    else:
                        act.wait_ge(unit_used, st.index(WB, c, KU))
                    act.activation(xs[:, 2 * half:2 * half + 2, TAPS - 1:], halves(acc0[:, half]), ACT.Copy)\
                       .then_inc(acc0_free[half], 1)

            qkv_chunk(0, False)
            act.wait_ge(sem("lat_ss"), 2 * T)
            with act.Fori(1, B_ITERS) as c:
                qkv_chunk(c, True)

            act.wait_ge(sem("xs_th_free"), 2 * BH // 4 + 1)
            act.wait_ge(sem("lat_norm"), 3 * T)

            def zab_chunk(c, first):
                for u in range(LEAD, KU + LEAD):
                    split_hi(act, WC, c, u)
                    if u == 2 and first:
                        act.wait_ge(sem("lat_ps"), 1)
                        act.activation(cqT[:, :, 0, :], tp_pair(0), ACT.Copy).then_inc(sem("cqT_hi"), 1)
                    if u == 3 and first:
                        act.activation(ckvT[:], halves(tp[:, 2]), ACT.Copy).then_inc(sem("latT"), 1)
                        act.activation(kidxT[:], tp[:, 3, 0:S], ACT.Copy).then_inc(sem("latT"), 1)
                    if u == 4 and first:
                        conv_tanh(B_ITERS - 1)
                    if u == 6:
                        act.activation(sq[:, bass.ds(4 * c, 4), :], qkvT[:, bass.ds(4 * c, 4), :], ACT.Square)\
                           .then_inc(sem("sq"), 1)
                read_acc0(WC, c, KU, zab)

            zab_chunk(0, True)
            with act.Fori(1, C_ITERS) as c:
                zab_chunk(c, False)
            act.wait_ge(sem("xs_th_free"), B_ITERS + 1)
            act.wait_ge(sem("ss_ps"), 1)
            for p, dst, chunks in ((WQI, qidxT, QI_CHUNKS), (WUQ, qT, UQ_CHUNKS)):
                for u in range(LEAD, chunks * QU + LEAD):
                    split_hi(act, p, 0, u)
                    if p == WQI and u == 3:
                        gate_exps(act)
                    if p == WQI and u == 6:
                        act.wait_ge(sem("gate_act"), 1)
                        act.activation(sm("spl"), sm("ax"), ACT.Ln, bias=1.0).then_inc(sem("gate_act"), 1)
                        act.wait_ge(sem("qk_r"), 1)
                        act.activation(sm("lk"), sm("rk"), ACT.Ln).then_inc(sem("log_k"), 1)
                    if p == WUQ and u == 4:
                        act.wait_ge(sem("cum_ps"), 1)
                        for n, name in enumerate(("eg", "ekd", "cd0", "cd1")):
                            act.activation(sm(name).rearrange("p t h -> p (t h)"), tp[:, 0, 16 * n:16 * n + 16],
                                           ACT.Exp).then_inc(sem("decays"), 1)
                    if u % QU == 1:
                        j = (u - 3) // QU
                        acc, free = ((acc0, acc0_free), (acc1, acc1_free))[j % 2]
                        act.wait_ge(unit_used, st.index(p, 0, (j + 1) * QU))
                        for half in range(2):
                            act.activation(dst[:, 4 * j + 2 * half:4 * j + 2 * half + 2, :], halves(acc[:, half]),
                                           ACT.Copy).then_inc(free[half], 1)
            for i in range(SCORE_ITEMS):
                n = (i % T + 1) * P
                act.wait_ge(sem("score_ps"), i + 1)
                if i >= 4:
                    act.wait_ge(sem("score_acc"), 4 * (i // T - 2) + i % T + 3)
                act.activation(relu[:, i % 4, :, 0:n], halves(tp[:, i % 4])[:, :, 0:n], ACT.Relu)\
                   .then_inc(sem("relu"), 1)
            for h in range(AH):
                act.wait_ge(sem("qlat_ps"), h + 1)
                act.activation(qlatT[:, :, h, :], halves(tp[:, h % 4]), ACT.Copy).then_inc(sem("qlat"), 1)
            for n, (t, hh) in enumerate(GROUPS):
                act.wait_ge(sem("k_ps"), n + 1)
                act.activation(group(ktok, t, hh), heads4(bankE(n)), ACT.Copy).then_inc(sem("ktok"), 1)
            for i in PART_ORDER:
                t, heads = SOFTMAX[i]
                act.wait_ge(sem("att_nmax"), RANK[i])
                prob = (prob0, prob1)[t]
                for h in range(heads.start, heads.stop):
                    act.activation(prob[:, h], prob[:, h], ACT.Exp, scale=A_SCALE, bias=nmax[:, t, h:h + 1],
                                   accum_out=psumm[:, t, h:h + 1]).then_inc(sem("prob_exp"), 1)
            for i in PART_ORDER:
                act.wait_ge(sem("pT_ps"), RANK[i])
                if i == 0:
                    act.activation(pT0[:, :, 0:P], tp[:, 0:2].rearrange("p b (h q) -> p (b h) q", h=4), ACT.Copy)\
                       .then_inc(sem("pT_part0"), 1)
                else:
                    act.activation(pT1[:, SOFTMAX[i][1]], heads4(acc0[:, i - 1]), ACT.Copy)\
                       .then_inc(sem(f"pT_part{i}"), 1)
            for h in range(AH):
                act.wait_ge(sem("olat_ps"), h + 1)
                act.activation(olatT[:, :, h, :], olat_bank(h), ACT.Copy).then_inc(sem("olat"), 1)
                if h > 0:
                    oT_hi(act, h - 1)
            oT_hi(act, AH - 1)

            for n, (t, hh) in enumerate(GROUPS):
                act.wait_ge(sem("v_ps"), n + 1)
                act.activation(group(vb, t, hh), heads4(bankF(n)), ACT.Copy).then_inc(sem("vtok"), 1)
                act.wait_ge(sem("dT_diff"), G8 * (n + 1))
                act.activation(group(dT, t, hh), group(dT, t, hh), ACT.Exp).then_inc(sem("dT"), 1)
            for n, (t, hh) in enumerate(GROUPS):
                act.wait_ge(sem("kbT_ps"), n + 1)
                act.activation(group(kbT, t, hh), heads4(bankE(n)), ACT.Copy).then_inc(sem("kbT"), 1)
            for s in range(STEPS + 2):
                if s < 4:
                    t, hh = GROUPS[s]
                    act.wait_ge(sem("x0_ps"), s + 1)
                    act.wait_ge(sem("qk_m"), s + 1)
                    act.activation(group(xinv, t, hh), heads4(bankE(s)), ACT.Copy).then_inc(sem("x0"), 1)
                if s < STEPS:
                    t, hh = GROUPS[s % 4]
                    act.wait_ge(sem("t1_ps"), s + 1)
                    act.activation(group(t1, t, hh), heads4(bankF(s % 4)), ACT.Copy).then_inc(sem("t1"), 1)
                if 0 <= s - 2 < STEPS - 4:
                    t, hh = GROUPS[(s - 2) % 4]
                    act.wait_ge(sem("x_ps"), s - 1)
                    act.activation(group(xinv, t, hh), heads4(bankF((s - 2) % 4)), ACT.Copy).then_inc(sem("x_up"), 1)
                if 4 <= s < 8:
                    t, cols = (s - 4) // 2, slice(BANK * (s % 2), BANK * (s % 2) + BANK)
                    act.activation(thz[:, t, cols], zab[:, t, cols], ACT.Tanh, scale=0.5).then_inc(sem("thz"), 1)
            for n, (t, hh) in enumerate(GROUPS):
                act.wait_ge(sem("kcd_ps"), n + 1)
                act.activation(group(nkcdT, t, hh), heads4(bankF(n)), ACT.Copy, scale=-1.0)\
                   .then_inc(sem("nkcd"), 1)
            for n in range(2 * T):
                rows = slice(CHR * (n % 2), CHR * (n % 2) + CHR)
                for b in range(2):
                    act.wait_ge(sem("vn_ps"), 2 * n + b + 1)
                    act.activation(vnew[rows, 4 * b:4 * b + 4, :], heads4(tp[rows, b]), ACT.Copy)\
                       .then_inc(sem("vnew"), 1)
                    if n % 2 == 0 and n > 0 and b == 0:
                        square_o(act, n // 2 - 1)
            square_o(act, T - 1)

            for u in range(LEAD, 5):
                split_hi(act, WO, 0, u)
            for q in range(2):
                act.wait_ge(sem("yT_ps"), q + 1)
                act.activation(xT[:, AH + 4 * q:AH + 4 * q + 4, 0, :], yT_banks(q), ACT.Copy)\
                   .then_inc(sem("y_hi"), 1)
            for u in range(5, KU + LEAD):
                split_hi(act, WO, 0, u)
            with act.Fori(1, OUT_CHUNKS) as c:
                for u in range(LEAD, KU + LEAD):
                    split_hi(act, WO, c, u)

        def gate_exps(act):
            act.wait_ge(sem("gate_in"), 2)
            act.wait_ge(sem("delta_gains"), 48)
            act.activation(sm("ax"), sm("ax"), ACT.Exp, scale=-1.0).then_inc(sem("gate_act"), 1)
            act.activation(alog[:], alog[:], ACT.Exp).then_inc(sem("gate_act"), 1)
            act.activation(sm("tb"), zab[:, :, BW + BH:BW + 2 * BH], ACT.Tanh, scale=0.5)\
               .then_inc(sem("gate_act"), 1)

        def square_o(act, t):
            act.wait_ge(sem("o_sum"), O_SUMS[t])
            act.activation(t1[:, t], oy[:, t], ACT.Square).then_inc(sem("o_sq"), 1)

        def z_tile(eng, t):
            eng.wait_ge(sem("o_sum"), O_SUMS[t])
            eng.wait_ge(sem("z"), 8)
            z = zab[:, t, 0:BW].rearrange("p (h d) -> p h d", d=BD)
            eng.tensor_tensor(z, oy[:, t], z, ALU.mult).then_inc(sem("zo"), 1)

        O_SUMS = [6, 10]

        def state_count(n, h):
            return h // 4 + 1 if n == 0 else 2 + BH * (n - 1) + h + 1

        STEPS = 4 * LEVELS
        CHR = P // 2
        thz = thz_sb[:]

        def yT_banks(q):
            return (acc1[:], tp[:, 0:2])[q].rearrange("p b (k s) -> p (b k) s", k=2)

        def att_bank(a):
            return halves((bankE, bankF)[a // 4](a % 4))

        def olat_bank(h):
            return halves((acc1[:, 0], acc1[:, 1], tp[:, 0])[h % 3])

        def o_bank(h):
            return (acc0[:, 0], acc0[:, 1], tp[:, 2], tp[:, 3])[h % 4][:, 0:S]

        def oT_hi(act, h):
            act.wait_ge(sem("oT_ps"), h + 1)
            act.activation(xT[:, h, 0, :], o_bank(h), ACT.Copy).then_inc(sem("oT_hi"), 1)

        def mixer_dve(dve):
            entry_dve(dve, 1, LEAD - 1)
            for u in range(LEAD, KU + LEAD):
                split_lo(dve, WA, 0, u)
                entry_dve(dve, 1, u)
            with dve.Fori(1, A_ITERS) as c:
                for u in range(LEAD, KU + LEAD):
                    split_lo(dve, WA, c, u)
            key = slice(QR + KR, QR + KR + ID)

            def key_stats():
                for t in range(T):
                    dve.wait_ge(acc0_free[t], n0[WB])
                for t in range(T):
                    dve.bn_stats(kstats[:, t], lat[:, t, key]).then_inc(sem("k_stats"), 1)
                for t in range(T):
                    dve.wait_ge(sem("k_stats"), t + 1)
                    dve.bn_aggr(kmv[:, t], kstats[:, t]).then_inc(sem("k_mv"), 1)
                dve.tensor_scalar(widx[:], lat[:, :, QR + KR + ID:A_COLS], W_SCALE, None, ALU.mult)\
                   .then_inc(sem("widx"), 1)

            def latent_norms(t):
                dve.wait_ge(sem("lat_rs"), 4)
                dve.wait_ge(sem("latent_gains"), 64)
                dve.scalar_tensor_tensor(out=lat[:, t, key], in0=lat[:, t, key], scalar=kmv[:, t, 0:1],
                                         in1=ki_g[:], op0=ALU.subtract, op1=ALU.mult).then_inc(sem("k_mid"), 1)
                dve.scalar_tensor_tensor(out=lat[:, t, 0:QR], in0=lat[:, t, 0:QR], scalar=rs[:, 0, t:t + 1],
                                         in1=cq_g[:], op0=ALU.mult, op1=ALU.mult).then_inc(sem("lat_norm"), 1)
                dve.scalar_tensor_tensor(out=ckv[:, t], in0=lat[:, t, QR:QR + KR], scalar=rs[:, 1, t:t + 1],
                                         in1=ckv_g[:], op0=ALU.mult, op1=ALU.mult).then_inc(sem("lat_norm"), 1)
                dve.wait_ge(sem("k_mid"), t + 1)
                dve.scalar_tensor_tensor(out=lat[:, t, key], in0=lat[:, t, key], scalar=rs[:, 2, t:t + 1],
                                         in1=ki_b[:], op0=ALU.mult, op1=ALU.add).then_inc(sem("lat_norm"), 1)

            dve.wait_ge(sem("cw"), 1)

            def conv(c, half):
                dve.wait_ge(acc0_free[half], c + (n0[WB] + 1))
                for step in range(TAPS):
                    tap = TAPS - 1 - step
                    for j in (2 * half, 2 * half + 1):
                        dst = qkvT[:, bass.ds(4 * c + j, 1), :].rearrange("p a s -> p (a s)")
                        w = cw[:, tap, bass.ds(4 * c + j, 1)]
                        if step == 0:
                            dve.tensor_scalar(dst, xs[:, j, tap:tap + S], w, None, ALU.mult)\
                               .then_inc(sem("conv_sum"), 1)
                        else:
                            dve.wait_ge(sem("conv_sum"), c * 16 + 8 * half + 2 * (step - 1) + j % 2 + 1)
                            dve.scalar_tensor_tensor(out=dst, in0=xs[:, j, tap:tap + S], scalar=w, in1=dst,
                                                     op0=ALU.mult, op1=ALU.add).then_inc(sem("conv_sum"), 1)

            def conv_silu(c):
                dve.wait_ge(sem("qkv_tanh"), c + 1)
                dve.scalar_tensor_tensor(out=qkvT[:, bass.ds(4 * c, 4), :], in0=th[:], scalar=1.0,
                                         in1=qkvT[:, bass.ds(4 * c, 4), :], op0=ALU.add, op1=ALU.mult)\
                   .then_inc(sem("xs_th_free"), 1)

            def qkv_chunk(c, prev):
                for u in range(LEAD, KU + LEAD):
                    split_lo(dve, WB, c, u)
                    if u == 2 and prev:
                        conv(c - 1, 1)
                    if u == 5 and prev:
                        conv_silu(c - 1)
                    if u == 2 and not prev:
                        key_stats()
                    if u in (6, 7) and not prev:
                        latent_norms(u - 6)
                conv(c, 0)

            qkv_chunk(0, False)
            with dve.Fori(1, B_ITERS) as c:
                qkv_chunk(c, True)
            for u in range(LEAD, KU + LEAD):
                split_lo(dve, WC, 0, u)
                if u == 2:
                    conv(B_ITERS - 1, 1)
                if u == 3:
                    dve.wait_ge(sem("cqT_hi"), 1)
                    dve.tensor_tensor(cqT[:, :, 1, :], tp_pair(0), cqT[:, :, 0, :].bitcast(F32), ALU.subtract)\
                       .then_inc(sem("cqT_lo"), 1)
                if u == 5:
                    conv_silu(B_ITERS - 1)
            with dve.Fori(1, C_ITERS) as c:
                for u in range(LEAD, KU + LEAD):
                    split_lo(dve, WC, c, u)
            for t in range(T):
                dve.wait_ge(acc0_free[t], n0[WQI])
            dve.wait_ge(sem("delta_gains"), 48)
            dve.tensor_tensor(sm("xa"), zab[:, :, BW:BW + BH], dtb[:].unsqueeze(1).to_broadcast([P, T, BH]), ALU.add)\
               .then_inc(sem("gate_in"), 1)
            dve.wait_ge(sem("gate_in"), 1)
            dve.scalar_tensor_tensor(out=sm("ax"), in0=sm("xa"), scalar=-1.0, in1=sm("xa"), op0=ALU.mult,
                                     op1=ALU.max).then_inc(sem("gate_in"), 1)
            for p, chunks in ((WQI, QI_CHUNKS), (WUQ, UQ_CHUNKS)):
                for u in range(LEAD, chunks * QU + LEAD):
                    split_lo(dve, p, 0, u)
                    if p == WQI and u == 3:
                        dve.wait_ge(sem("ss_ps"), 1)
                        dve.tensor_copy(
                            small[:, NAMES.index("rq"):NAMES.index("rq") + 2].rearrange("p a t h -> p (a t h)"),
                            tp[:, 1, 0:2 * T * BH]).then_inc(sem("qk_ss"), 1)
                    if p == WQI and u == 7:
                        dve.wait_ge(sem("gate_act"), 4)
                        dve.scalar_tensor_tensor(out=sm("sp"), in0=sm("xa"), scalar=0.0, in1=sm("spl"), op0=ALU.max,
                                                 op1=ALU.add).then_inc(sem("gate_mid"), 1)
                        dve.wait_ge(sem("gate_mid"), 1)
                        dve.scalar_tensor_tensor(out=sm("g"), in0=sm("sp"), scalar=-1.0,
                                                 in1=alog[:].unsqueeze(1).to_broadcast([P, T, BH]), op0=ALU.mult,
                                                 op1=ALU.mult).then_inc(sem("g"), 1)
                        dve.tensor_scalar(sm("beta"), sm("tb"), 0.5, 0.5, ALU.mult, ALU.add).then_inc(sem("beta"), 1)
                    if p == WUQ and u == 4:
                        dve.wait_ge(sem("decays"), 4)
                        dve.tensor_copy(sm("gc").rearrange("p t h -> p (t h)"), tp[:, 0, 0:T * BH])\
                           .then_inc(sem("gc"), 1)
                        dve.wait_ge(sem("gc"), 1)
                        dve.wait_ge(sem("log_k"), 1)
                        dve.scalar_tensor_tensor(out=sm("lk"), in0=sm("lk"), scalar=0.5, in1=sm("gc"), op0=ALU.mult,
                                                 op1=ALU.add).then_inc(sem("gc"), 1)
            dve.wait_ge(sem("qk_r"), 2)
            dve.wait_ge(sem("beta"), 1)
            dve.tensor_tensor(sm("c1"), sm("rk"), sm("beta"), ALU.mult).then_inc(sem("factors"), 1)
            dve.tensor_tensor(sm("c3"), sm("rk"), sm("ekd"), ALU.mult).then_inc(sem("factors"), 1)
            dve.tensor_scalar(sm("vbs"), sm("beta"), 0.5, None, ALU.mult).then_inc(sem("factors"), 1)
            dve.tensor_scalar(sm("qs"), sm("rq"), BD ** -0.5, None, ALU.mult).then_inc(sem("factors"), 1)
            dve.wait_ge(sem("factors"), 4)
            dve.tensor_tensor(sm("c2"), sm("c1"), sm("eg"), ALU.mult).then_inc(sem("factors"), 1)
            dve.scalar_tensor_tensor(out=sm("qs2"), in0=sm("qs"), scalar=1.0 / BD, in1=sm("qs"), op0=ALU.mult,
                                     op1=ALU.mult).then_inc(sem("factors"), 1)
            dve.wait_ge(sem("widx"), 1)
            dve.wait_ge(sem("lat_ps"), 1)
            dve.wait_ge(sem("xs_th_free"), B_ITERS + 1)
            for pair in range(SCORE_ITEMS // T):
                for hh in range(2):
                    for t in range(T):
                        i, n, h = T * pair + t, (t + 1) * P, 2 * pair + hh
                        dve.wait_ge(sem("relu"), i + 1)
                        src, dst, w = relu[:, i % 4, hh, 0:n], score[:, t, 0:n], widx[:, t, h:h + 1]
                        if h == 0:
                            dve.tensor_scalar(dst, src, w, None, ALU.mult).then_inc(sem("score_acc"), 1)
                        else:
                            dve.wait_ge(sem("score_acc"), T * (h - 1) + t + 1)
                            dve.scalar_tensor_tensor(out=dst, in0=src, scalar=w, in1=dst, op0=ALU.mult, op1=ALU.add)\
                               .then_inc(sem("score_acc"), 1)
            dve.wait_ge(sem("score_masked"), T)
            for r in range(KEPT // 8):
                for t in range(T):
                    n = (t + 1) * P
                    src = (work if r else score)[:, t, 0:n]
                    wait(dve, sem("taken"), T * (r - 1) + t + 1)
                    dve.max(top8[:, t], src).then_inc(sem("top8"), 1)
                for t in range(T):
                    n = (t + 1) * P
                    src = (work if r else score)[:, t, 0:n]
                    dve.wait_ge(sem("top8"), T * r + t + 1)
                    dve.match_replace(out=work[:, t, 0:n], in_to_replace=top8[:, t], in_values=src,
                                      imm_value=TAKEN).then_inc(sem("taken"), 1)
            dve.wait_ge(sem("ndist"), 2)
            for t in range(T):
                n = (t + 1) * P
                dve.wait_ge(sem("taken"), T * (KEPT // 8 - 1) + t + 1)
                dve.tensor_tensor(sel[:, t, 0:n], work[:, t, 0:n], score[:, t, 0:n], ALU.not_equal)\
                   .then_inc(sem("sel_raw"), 1)
            for t in range(T):
                n = (t + 1) * P
                dve.wait_ge(sem("sel_raw"), t + 1)
                dve.tensor_scalar(sel[:, t, 0:n], sel[:, t, 0:n], 1.0, -NEG, ALU.subtract, ALU.mult)\
                   .then_inc(sem("sel_raw"), 1)
            def logits(a):
                t, hp = a // 4, a % 4
                n = (t + 1) * P
                dve.wait_ge(sem("att_ps"), a + 1)
                for hh in range(2):
                    h = 2 * hp + hh
                    slope = 2.0 ** (-8.0 * (h + 1.0) / AH)
                    dve.scalar_tensor_tensor(out=(prob0, prob1)[t][:, h, :], in0=ndist[:, t, 0:n],
                                             scalar=slope / A_SCALE, in1=att_bank(a)[:, hh, 0:n],
                                             op0=ALU.mult, op1=ALU.add).then_inc(sem("att_z"), 1)

            def select(i):
                t, heads = SOFTMAX[i]
                n, m = (t + 1) * P, heads.stop - heads.start
                prob = (prob0, prob1)[t][:, heads]
                dve.wait_ge(sem("sel"), T)
                dve.wait_ge(sem("att_z"), AH * t + heads.stop)
                if i > 0:
                    dve.tensor_tensor(prob, prob, sel[:, t, 0:n].unsqueeze(1).to_broadcast([P, m, n]), ALU.add)\
                       .then_inc(sem("att_sel"), 1)
                    dve.wait_ge(sem("att_sel"), i)
                else:
                    dve.wait_ge(sem("att_sel0"), 1)
                dve.reduce_max(amax[:, t, heads], prob, AX_X).then_inc(sem("att_max"), 1)
                dve.wait_ge(sem("att_max"), RANK[i])
                dve.tensor_scalar(nmax[:, t, heads], amax[:, t, heads], -A_SCALE, None, ALU.mult)\
                   .then_inc(sem("att_nmax"), 1)

            def normalise(i):
                t, heads = SOFTMAX[i]
                n, m = (t + 1) * P, heads.stop - heads.start
                prob = (prob0, prob1)[t][:, heads]
                dve.wait_ge(sem("prob_exp"), EXPS[i])
                dve.reciprocal(pinv[:, t, heads], psumm[:, t, heads]).then_inc(sem("pinv"), 1)
                if i > 0:
                    dve.wait_ge(sem("pinv"), i + 1)
                    dve.tensor_tensor(prob, prob, pinv[:, t, heads].unsqueeze(2).to_broadcast([P, m, n]), ALU.mult)\
                       .then_inc(sem("prob"), 1)

            for a in range(4):
                logits(a)
            logits(4)
            logits(5)
            select(1)
            select(0)
            logits(6)
            logits(7)
            select(2)
            normalise(0)
            normalise(1)
            normalise(2)
            for i in (1, 2):
                heads = SOFTMAX[i][1]
                dve.wait_ge(sem("pT_ps"), RANK[i])
                dve.tensor_copy(pT0[:, heads, P:S], heads4(tp[:, 1 + i])).then_inc(sem(f"pT_part{i}"), 1)
            for h in range(AH):
                dve.wait_ge(sem("oT_hi"), h + 1)
                dve.tensor_tensor(xT[:, h, 1, :], o_bank(h), xT[:, h, 0, :].bitcast(F32), ALU.subtract)\
                   .then_inc(sem("oT_lo"), 1)

            dve.wait_ge(sem("gc"), 2)
            dve.wait_ge(sem("factors"), 6)
            dve.wait_ge(sem("masks"), MASKS)
            for n, (t, hh) in enumerate(GROUPS):
                dve.wait_ge(sem("gbc_ps"), n + 1)
                for k in range(G8):
                    h = G8 * hh + k
                    dve.scalar_tensor_tensor(out=dT[:, t, h], in0=bankE(n)[:, k * P:k * P + P],
                                             scalar=sm("lk")[:, t, h:h + 1], in1=not_ahead[:],
                                             op0=ALU.subtract, op1=ALU.add).then_inc(sem("dT_diff"), 1)

            def times_decay(name, dst, bank, n, t, hh):
                dve.wait_ge(sem(name + "_ps"), n + 1)
                dve.wait_ge(sem("dT"), n + 1)
                dve.tensor_tensor(group(dst, t, hh), heads4(bank), group(dT, t, hh), ALU.mult)\
                   .then_inc(sem(name + "_m"), 1)

            for n, (t, hh) in enumerate(GROUPS):
                times_decay("kk", aT, bankE(n), n, t, hh)
                dve.wait_ge(sem("kk_m"), n + 1)
                dve.tensor_tensor(group(yinv, t, hh), group(aT, t, hh),
                                  pair_mask[:, 0].unsqueeze(1).to_broadcast([P, G8, P]), ALU.mult)\
                   .then_inc(sem("pairs"), 1)
                dve.wait_ge(sem("pairs"), n + 1)
                dve.tensor_tensor(group(yinv, t, hh), ident[:].unsqueeze(1).to_broadcast([P, G8, P]),
                                  group(yinv, t, hh), ALU.subtract).then_inc(sem("y0"), 1)
                if n > 0:
                    times_decay("qk", aiT, bankF(n - 1), n - 1, *GROUPS[n - 1])

            for s in range(STEPS):
                t, hh = GROUPS[s % 4]
                if s == 1:
                    times_decay("qk", aiT, bankF(3), 3, *GROUPS[3])
                dve.wait_ge(sem("y_ps"), s + 1)
                dve.tensor_tensor(group(yinv, t, hh), group(yinv, t, hh), heads4(bankE(s % 4)),
                                  ALU.subtract).then_inc(sem("y_up"), 1)
                if 8 <= s < 16:
                    i = s % 4
                    t, cols = i // 2, slice(BANK * (i % 2), BANK * (i % 2) + BANK)
                    if s < 12:
                        dve.wait_ge(sem("thz"), i + 1)
                        dve.scalar_tensor_tensor(out=zab[:, t, cols], in0=thz[:, t, cols], scalar=1.0,
                                                 in1=zab[:, t, cols], op0=ALU.add, op1=ALU.mult)\
                           .then_inc(sem("z"), 1)
                    else:
                        dve.wait_ge(sem("z"), i + 1)
                        zt = zab[:, t, cols].rearrange("p (h d) -> p h d", d=BD)
                        dve.tensor_tensor(zt, zt, og[:].unsqueeze(1).to_broadcast([P, G8, BD]), ALU.mult)\
                           .then_inc(sem("z"), 1)

            def o_tile(t):
                rows = slice(CHR if t == 0 else 0, P)
                eg = sm("eg")[rows, t]
                for b in range(2):
                    dve.tensor_tensor(oy[rows, t, G8 * b:G8 * b + G8], heads4(acc0[rows, b]),
                                      eg[:, G8 * b:G8 * b + G8].unsqueeze(2).to_broadcast([P - rows.start, G8, P]),
                                      ALU.mult).then_inc(sem("o_sum"), 1)
                for b in range(2):
                    dve.wait_ge(sem("o_sum"), (O_SUMS[t - 1] if t else 0) + b + 1)
                    part = oy[rows, t, G8 * b:G8 * b + G8]
                    dve.tensor_tensor(part, part, heads4(acc1[rows, b]), ALU.add).then_inc(sem("o_sum"), 1)
                    if t == 0:
                        dve.tensor_copy(oy[0:CHR, t, G8 * b:G8 * b + G8], heads4(acc1[0:CHR, b]))\
                           .then_inc(sem("o_sum"), 1)

            def o_mean_square(t):
                dve.wait_ge(sem("o_sq"), t + 1)
                dve.reduce_sum(sm("co")[:, t], t1[:, t], AX_X).then_inc(sem("o_red"), 1)
                dve.wait_ge(sem("o_red"), t + 1)
                dve.tensor_tensor(sm("sso")[:, t], sm("co")[:, t], sm("qs2")[:, t], ALU.mult)\
                   .then_inc(sem("o_ms"), 1)

            def y_tile(t):
                dve.wait_ge(sem("o_r"), 2 * t + 2)
                dve.wait_ge(sem("o_ms"), t + 1)
                dve.scalar_tensor_tensor(out=sm("co")[:, t], in0=sm("ro")[:, t], scalar=0.5, in1=sm("qs")[:, t],
                                         op0=ALU.mult, op1=ALU.mult).then_inc(sem("o_co"), 1)
                dve.wait_ge(sem("o_co"), t + 1)
                dve.wait_ge(sem("zo"), t + 1)
                dve.tensor_tensor(oy[:, t], zab[:, t, 0:BW].rearrange("p (h d) -> p h d", d=BD),
                                  sm("co")[:, t].unsqueeze(2).to_broadcast([P, BH, BD]), ALU.mult)\
                   .then_inc(sem("y"), 1)

            dve.wait_ge(sem("z"), 8)
            for n in range(2 * T):
                t, half = n // 2, n % 2
                if half == 0 and t > 0:
                    z_tile(dve, t - 1)
                    o_mean_square(t - 1)
                if n == 0:
                    for b in range(2):
                        dve.wait_ge(sem("st_ps"), b + 1)
                        dve.tensor_copy(state[:, 4 * b:4 * b + 4], heads4(tp[:, 2 + b])).then_inc(sem("state"), 1)
                elif n < 2 * T - 1:
                    for h in range(BH):
                        if h % 4 == 0:
                            dve.wait_ge(sem("st_ps"), 2 * n + h // 4 + 1)
                        dve.wait_ge(sem("state"), state_count(n - 1, h))
                        dve.scalar_tensor_tensor(out=state[:, h], in0=state[:, h],
                                                 scalar=sm(f"cd{half}")[:, t, h:h + 1],
                                                 in1=tp[:, 2 + h // 4, (h % 4) * P:(h % 4) * P + P],
                                                 op0=ALU.mult, op1=ALU.add).then_inc(sem("state"), 1)
                if half == 1:
                    if t > 0:
                        y_tile(t - 1)
                    dve.wait_ge(sem("o_ps"), t + 1)
                    o_tile(t)
            split_lo(dve, WO, 0, 2)
            o_mean_square(T - 1)
            split_lo(dve, WO, 0, 3)
            y_tile(T - 1)
            split_lo(dve, WO, 0, 4)
            for q in range(2):
                dve.wait_ge(sem("y_hi"), q + 1)
                rows = xT[:, AH + 4 * q:AH + 4 * q + 4, :, :]
                dve.tensor_tensor(rows[:, :, 1, :], yT_banks(q), rows[:, :, 0, :].bitcast(F32), ALU.subtract)\
                   .then_inc(sem("y_lo"), 1)
            for u in range(5, KU + LEAD):
                split_lo(dve, WO, 0, u)
            into_resid(dve, WO, 0, 1.0 / ALPHA, KU)
            with dve.Fori(1, OUT_CHUNKS - 1) as c:
                for u in range(LEAD, KU + LEAD):
                    split_lo(dve, WO, c, u)
                into_resid(dve, WO, c, 1.0 / ALPHA, KU)
            for u in range(LEAD, KU + LEAD - 1):
                split_lo(dve, WO, OUT_CHUNKS - 1, u)
            into_resid(dve, WO, OUT_CHUNKS - 1, 1.0 / ALPHA, KU)

        def mixer_pe(pe):
            def latent_unit(c, u):
                unit_mm(pe, WA, c, u, acc0, acc0_free, c + n0[WA], "w", xT, 2 * u, u == 0, u == KU - 1, acc0a_done)

            for u in range(KU):
                entry_pe(pe, 1, u)
                latent_unit(0, u)
            with pe.Fori(1, A_ITERS) as c:
                for u in range(KU):
                    latent_unit(c, u)
            with pe.Fori(0, B_ITERS) as c:
                for u in range(KU):
                    unit_mm(pe, WB, c, u, acc0, acc0_free, c + n0[WB], "x", xT, 2 * u, u == 0, u == KU - 1,
                            acc0a_done)
            pe.wait_ge(sem("lat_norm"), 3 * T)
            for t in range(T):
                for k in range(QT):
                    pe.transpose(tp_pair(0)[:, k, t * P:t * P + P], lat[:, t, k * P:k * P + P], ident[:])
                for k in range(RT):
                    pe.transpose(halves(tp[:, 2])[:, k, t * P:t * P + P], ckv[:, t, k * P:k * P + P], ident[:])
                ins = pe.transpose(tp[:, 3, t * P:t * P + P], lat[:, t, QR + KR:QR + KR + ID], ident[:])
            ins.then_inc(sem("lat_ps"), 1)
            with pe.Fori(0, C_ITERS) as c:
                for u in range(KU):
                    unit_mm(pe, WC, c, u, acc0, acc0_free, c + n0[WC], "w", xT, 2 * u, u == 0, u == KU - 1,
                            acc0a_done)
            pe.wait_ge(sem("cqT_lo"), 1)
            pe.wait_ge(sem("latT"), 2)
            pe.wait_ge(sem("ones"), 1)
            pe.wait_ge(sem("sq"), 4)
            for i in range(2):
                for t in range(T):
                    for h in range(BH):
                        ins = pe.matmul(tp[:, 1, (i * T + t) * BH + h:(i * T + t) * BH + h + 1],
                                        sq[:, i * BH + h, t * P:t * P + P], ones[:, 0:1], start=True, stop=True)
            ins.then_inc(sem("ss_ps"), 1)
            for p, chunks in ((WQI, QI_CHUNKS), (WUQ, UQ_CHUNKS)):
                if p == WUQ:
                    pe.wait_ge(sem("g"), 1)
                    pe.wait_ge(sem("masks"), MASKS)
                    g_all = sm("g").rearrange("p t h -> p (t h)")
                    for n, m in enumerate((up_to[:], later[:], in_half[:, 0], in_half[:, 1])):
                        ins = pe.matmul(tp[:, 0, 16 * n:16 * n + 16], m, g_all, start=True, stop=True)
                    ins.then_inc(sem("cum_ps"), 1)
                for j in range(chunks):
                    acc, free = ((acc0, acc0_free), (acc1, acc1_free))[j % 2]
                    n = (n0, n1)[j % 2][p] + j // 2
                    for u in range(QU):
                        unit_mm(pe, p, 0, j * QU + u, acc, free, n, "x", cqT, 2 * u, u == 0, u == QU - 1,
                                acc0a_done if j % 2 == 0 else None)
            pe.wait_ge(sem("gc"), 1)
            pe.wait_ge(sem("qk_ss"), 1)
            for i in range(SCORE_ITEMS):
                t, n = i % T, (i % T + 1) * P
                wait(pe, sem("relu"), i - 3)
                for hh in range(2):
                    h = 2 * (i // T) + hh
                    ins = pe.matmul(halves(tp[:, i % 4])[:, hh, 0:n], qidxT[:, h, t * P:t * P + P], kidxT[:, 0:n],
                                    start=True, stop=True)
                ins.then_inc(sem("score_ps"), 1)
            pe.wait_ge(sem("wuk"), 16)
            for half in range(2):
                pe.wait_ge(acc0_free[half], n0[WO])
                pe.wait_ge(acc1_free[half], n1[F2GU])
            for h in range(AH):
                if h < 4:
                    pe.wait_ge(sem("relu"), SCORE_ITEMS - 3 + h)
                else:
                    pe.wait_ge(sem("qlat"), h - 3)
                for r in range(RT):
                    ins = pe.matmul(halves(tp[:, h % 4])[:, r, :], wuk[:, h, r * P:r * P + P], qT[:, h, :],
                                    start=True, stop=True)
                ins.then_inc(sem("qlat_ps"), 1)
            for a in range(AH):
                t, hp = a // 4, a % 4
                n = (t + 1) * P
                for hh in range(2):
                    h = 2 * hp + hh
                    if t == 0:
                        pe.wait_ge(sem("qlat"), h + 1)
                    for r in range(RT):
                        ins = pe.matmul(att_bank(a)[:, hh, 0:n], qlatT[:, r, h, t * P:t * P + P],
                                        ckvT[:, r, 0:n], start=r == 0, stop=r == RT - 1)
                ins.then_inc(sem("att_ps"), 1)
            for n, (t, hh) in enumerate(GROUPS):
                pe.wait_ge(sem("att_z"), 2 * (n + 1))
                for k in range(G8):
                    ins = pe.transpose(bankE(n)[:, k * P:k * P + P], kT_of(G8 * hh + k, t), ident[:])
                ins.then_inc(sem("k_ps"), 1)
            pe.wait_ge(sem("qlat"), AH)
            pe.wait_ge(sem("att_z"), 2 * AH)
            pe.wait_ge(sem("ktok"), 4)
            keep_warm(pe, WO, acc1[:, 1], SOFTMAX_WAIT)
            for i in PART_ORDER:
                pe.wait_ge(sem("prob" if i else "prob0"), max(i, 1))
                for k, h in enumerate(range(*SOFTMAX[i][1].indices(AH))):
                    cols = slice((k % 4) * P, (k % 4) * P + P)
                    if i == 0:
                        ins = pe.transpose(tp[:, k // 4, cols], prob0[:, h, :], ident[:])
                    else:
                        pe.transpose(tp[:, 1 + i, cols], prob1[:, h, 0:P], ident[:])
                        ins = pe.transpose(acc0[:, i - 1, cols], prob1[:, h, P:S], ident[:])
                ins.then_inc(sem("pT_ps"), 1)
            pe.wait_ge(sem("pT_part0"), 1)
            pe.wait_ge(sem("pT_part1"), 2)
            pe.wait_ge(sem("wuv"), 16)

            def o_head(h):
                pe.wait_ge(sem("olat"), h + 1)
                wait(pe, sem("oT_lo"), h - 3)
                for r in range(RT):
                    ins = pe.matmul(o_bank(h), wuv[:, h, r, :], olatT[:, r, h, :], start=r == 0, stop=r == RT - 1)
                ins.then_inc(sem("oT_ps"), 1)

            for h in range(AH):
                if h == 2:
                    pe.wait_ge(sem("pT_part2"), 2)
                wait(pe, sem("olat"), h - 2)
                bank = olat_bank(h)
                for r in range(RT):
                    rc = slice(r * P, r * P + P)
                    pe.matmul(bank[:, r, 0:P], ckv[:, 0, rc], pT0[:, h, 0:P], start=True, stop=True)
                    pe.matmul(bank[:, r, P:S], ckv[:, 0, rc], pT0[:, h, P:S], start=True, stop=False)
                    ins = pe.matmul(bank[:, r, P:S], ckv[:, 1, rc], pT1[:, h, :], start=False, stop=True)
                ins.then_inc(sem("olat_ps"), 1)
                if h > 0:
                    o_head(h - 1)
            o_head(AH - 1)

            pe.wait_ge(sem("oT_lo"), AH)
            pe.wait_ge(sem("olat"), AH)
            for n, (t, hh) in enumerate(GROUPS):
                for k in range(G8):
                    ins = pe.transpose(bankF(n)[:, k * P:k * P + P], vT_of(G8 * hh + k, t), ident[:])
                ins.then_inc(sem("v_ps"), 1)
                for k in range(G8):
                    h = G8 * hh + k
                    ins = pe.matmul(bankE(n)[:, k * P:k * P + P], sm("g")[:, t, h:h + 1].to_broadcast([P, P]),
                                    up_to[:], start=True, stop=True)
                ins.then_inc(sem("gbc_ps"), 1)
            for n, (t, hh) in enumerate(GROUPS):
                pe.wait_ge(sem("dT_diff"), G8 * (n + 1))
                pe.wait_ge(sem("kb"), n + 1)
                for k in range(G8):
                    ins = pe.transpose(bankE(n)[:, k * P:k * P + P], kb[:, t, G8 * hh + k], ident[:])
                ins.then_inc(sem("kbT_ps"), 1)
            def kk_mm(n, t, hh):
                pe.wait_ge(sem("kbT"), n + 1)
                for k in range(G8):
                    h = G8 * hh + k
                    ins = pe.matmul(bankE(n)[:, k * P:k * P + P], kT_of(h, t), kbT[:, t, h], start=True, stop=True)
                ins.then_inc(sem("kk_ps"), 1)
            def qk_mm(n, t, hh):
                pe.wait_ge(sem("vtok"), n + 1)
                for k in range(G8):
                    h = G8 * hh + k
                    ins = pe.matmul(bankF(n)[:, k * P:k * P + P], kT_of(h, t), qT_of(h, t), start=True, stop=True)
                ins.then_inc(sem("qk_ps"), 1)

            for n, (t, hh) in enumerate(GROUPS):
                kk_mm(n, t, hh)
                if n > 0:
                    qk_mm(n - 1, *GROUPS[n - 1])
            qk_mm(3, *GROUPS[3])

            for s in range(STEPS + 2):
                if s < STEPS:
                    t, hh = GROUPS[s % 4]
                    if s < 4:
                        pe.wait_ge(sem("y0"), s + 1)
                        for k in range(G8):
                            ins = pe.transpose(bankE(s)[:, k * P:k * P + P], yinv[:, t, G8 * hh + k], ident[:])
                        ins.then_inc(sem("x0_ps"), 1)
                    pe.wait_ge(sem("lev"), s + 1)
                    if s < 4:
                        pe.wait_ge(sem("x0"), s + 1)
                        pe.wait_ge(sem("qk_m"), s + 1)
                    else:
                        pe.wait_ge(sem("x_up"), s - 3)
                    for k in range(G8):
                        h = G8 * hh + k
                        ins = pe.matmul(bankF(s % 4)[:, k * P:k * P + P], lev[:, t, h], xinv[:, t, h],
                                        start=True, stop=True)
                    ins.then_inc(sem("t1_ps"), 1)
                if 0 <= s - 1 < STEPS:
                    n = (s - 1) % 4
                    t, hh = GROUPS[n]
                    pe.wait_ge(sem("t1"), s)
                    for k in range(G8):
                        h = G8 * hh + k
                        ins = pe.matmul(bankE(n)[:, k * P:k * P + P], t1[:, t, h], yinv[:, t, h],
                                        start=True, stop=True)
                    ins.then_inc(sem("y_ps"), 1)
                if 0 <= s - 2 < STEPS - 4:
                    n = (s - 2) % 4
                    t, hh = GROUPS[n]
                    pe.wait_ge(sem("y_up"), s - 1)
                    for k in range(G8):
                        ins = pe.transpose(bankF(n)[:, k * P:k * P + P], yinv[:, t, G8 * hh + k], ident[:])
                    ins.then_inc(sem("x_ps"), 1)
            pe.wait_ge(sem("k_scaled"), 8)
            for n, (t, hh) in enumerate(GROUPS):
                pe.wait_ge(sem("y_up"), 4 * (LEVELS - 1) + n + 1)
                for k in range(G8):
                    h = G8 * hh + k
                    ins = pe.matmul(bankF(n)[:, k * P:k * P + P], kbeg[:, t, h], yinv[:, t, h],
                                    start=True, stop=True)
                ins.then_inc(sem("kcd_ps"), 1)
            pe.wait_ge(sem("v_scaled"), 4)
            pe.wait_ge(sem("nkcd"), 4)
            for n in range(2 * T):
                t, half = n // 2, n % 2
                rows = slice(CHR * half, CHR * half + CHR)
                cols = slice(t * P + CHR * half, t * P + CHR * half + CHR)

                def head_cols(h):
                    return slice((h % 4) * P, (h % 4) * P + P)

                if half == 0:
                    wait(pe, sem("vnew"), 2 * n)
                    for h in range(BH):
                        ins = pe.matmul(tp[:, h // 4, head_cols(h)], yinv[:, t, h], vb[:, t, h],
                                        start=h % 4 == 0, stop=True, skip_group_check=True)
                        if n == 0 and h % 4 == 3:
                            ins.then_inc(sem("vn_ps"), 1)
                if n > 0:
                    for h in range(BH):
                        pe.wait_ge(sem("state"), state_count(n - 1, h))
                        ins = pe.matmul(tp[rows, h // 4, head_cols(h)], nkcdT[:, t, h, rows], state[:, h],
                                        start=False, stop=True, skip_group_check=True)
                        if h % 4 == 3:
                            ins.then_inc(sem("vn_ps"), 1)
                    if t > 0 and half == 0:
                        pe.wait_ge(sem("o_sum"), O_SUMS[t - 1])
                    for h in range(BH):
                        pe.matmul(acc0[rows, h // 4, head_cols(h)], qkvT[:, h, cols], state[:, h],
                                  start=True, stop=True)
                if n < 2 * T - 1:
                    for h in range(BH):
                        if h % 4 == 0:
                            pe.wait_ge(sem("vnew"), 2 * n + h // 4 + 1)
                        ins = pe.matmul(tp[:, 2 + h // 4, head_cols(h)], kdec[rows, t, h], vnew[rows, h],
                                        start=True, stop=True)
                        if h % 4 == 3:
                            ins.then_inc(sem("st_ps"), 1)
                if half == 1:
                    pe.wait_ge(sem("vnew"), 2 * n + 2)
                    for h in range(BH):
                        ins = pe.matmul(acc1[:, h // 4, head_cols(h)], aiT[:, t, h], vnew[:, h],
                                        start=True, stop=True)
                    ins.then_inc(sem("o_ps"), 1)

            def out_unit(c, u):
                unit_mm(pe, WO, c, u, acc0, acc0_free, c + n0[WO], "w", xT, 2 * u, u == 0, u == KU - 1, acc0a_done)

            pe.wait_ge(sem("o_sum"), O_SUMS[T - 2] + 2)
            for u in range(3):
                out_unit(0, u)
            pe.wait_ge(sem("o_sum"), O_SUMS[T - 1])
            pe.wait_ge(sem("y"), T)
            for q in range(2):
                for k in range(4):
                    for t in range(T):
                        ins = pe.transpose(yT_banks(q)[:, k, t * P:t * P + P], oy[:, t, 4 * q + k], ident[:])
                ins.then_inc(sem("yT_ps"), 1)
            out_unit(0, 3)
            for u in range(4, KU):
                pe.wait_ge(sem("y_lo"), (2 * u - AH) // 4 + 1)
                out_unit(0, u)
            with pe.Fori(1, OUT_CHUNKS) as c:
                for u in range(KU):
                    out_unit(c, u)

        block = ctx.enter_context(nc.Block())

        @block.sync
        def _(sp):
            x_v = x[0].rearrange("(t p) d -> p t d", p=P)

            def load_x(q):
                sp.dma_start(resid[:, :, q * BANK:(q + 1) * BANK], x_v[:, :, q * BANK:(q + 1) * BANK])\
                  .then_inc(sem(f"x_loaded{q}"), 16)

            load_x(0)
            ffn_loads(sp, 0, ffn1_w_gate[0], ffn1_w_up[0], ffn1_w_down[0], load_x)
            mixer_loads(sp)
            ffn_loads(sp, 1, ffn2_w_gate[0], ffn2_w_up[0], ffn2_w_down[0], None)
            out_v = out[0].rearrange("(t p) d -> p t d", p=P)
            stores = 0
            for q in range(4):
                for t in range(T):
                    if t == 0 or q == 0:
                        sp.wait_ge(sem("ln_out"), 10 + NORM_STEPS[q] - (q == 0) + t)
                    else:
                        sp.wait_ge(sem("ln_out_pool"), 6 + q)
                    cols = slice(q * BANK, q * BANK + BANK)
                    sp.dma_start(out_v[:, t, cols], resid[:, t, cols]).then_inc(sem("stored"), 16)
                    stores += 16
            sp.wait_ge(sem("stored"), stores)

        @block.gpsimd
        def _(pool):
            pool.memset(ident[:], 1.0).then_inc(sem("ident"), 1)
            pool.memset(half_neg[:], -0.5).then_inc(sem("pow_ready"), 1)
            pool.wait_ge(sem("ident"), 1)
            pool.affine_select(out=ident[:], in_=ident[:], compare_op=ALU.is_equal, fill=0.0, base=0,
                               pattern=[[-1, P]], channel_multiplier=1).then_inc(sem("ident"), 1)
            pool.wait_ge(sem("pow_ready"), 1)
            pool.wait_ge(unit_used, st.index(F1D, OUT_CHUNKS - 1, KT // UNIT_KT))
            norm_gains(pool, ln1_g, ln1_b)
            norm_pool(pool, 0)
            mixer_pool(pool)
            pool.wait_ge(unit_used, st.index(F2D, OUT_CHUNKS - 1, KT // UNIT_KT))
            norm_gains(pool, ln3_g, ln3_b)
            norm_pool(pool, 2)

        @block.scalar
        def _(act):
            act.dma_start(cw_rows[:], conv_w[0].rearrange("a (t p) -> (a t) p", p=P)).then_inc(sem("cw_rows"), 16)
            split_hi(act, F1GU, 0, 0)
            to_xT_act(act, 0, 0)
            for u in range(1, LEAD):
                split_hi(act, F1GU, 0, u)
            ffn_act(act, 0, False)
            mixer_act(act)
            ffn_act(act, 1, True)
            norm_act(act, 2)

        @block.vector
        def _(dve):
            split_lo(dve, F1GU, 0, 0)
            to_xT_dve(dve, 0, 0)
            for u in range(1, LEAD):
                split_lo(dve, F1GU, 0, u)
            ffn_dve(dve, 0, False)
            mixer_dve(dve)
            ffn_dve(dve, 1, True)
            norm_stats(dve, 2)
            for q in range(OUT_CHUNKS):
                norm_quarter(dve, 2, q)

        @block.tensor
        def _(pe):
            pe.wait_ge(sem("ident"), 2)
            for _ in range(START_WAIT):
                pe.matmul(acc0[:, 0, 0:P], ident[:], ident[:], start=True, stop=True)
            pe.wait_ge(sem("cw_rows"), 16)
            pe.transpose(acc1[:, 0, 0:TAPS * CONV_TILES], cw_rows[:], ident[0:TAPS * CONV_TILES, 0:TAPS * CONV_TILES])\
              .then_inc(sem("cw_ps"), 1)
            ffn_pe(pe, 0)
            mixer_pe(pe)
            ffn_pe(pe, 1)


_INS = ['x', 'ffn1_w_gate', 'ffn1_w_up', 'ffn1_w_down', 'ln1_g', 'ln1_b', 'w_in', 'q_norm_g', 'kv_norm_g',
        'w_uq', 'w_uk', 'w_uv', 'w_q_idx', 'k_idx_ln_g', 'k_idx_ln_b', 'conv_w', 'a_log', 'dt_bias', 'o_norm_g',
        'w_out', 'ln2_g', 'ln2_b', 'ffn2_w_gate', 'ffn2_w_up', 'ffn2_w_down', 'ln3_g', 'ln3_b']


def kernel(**inputs):
    import numpy as _np
    import concourse.bacc as _bacc
    from concourse import mybir as _mybir
    from concourse.bass_utils import run_bass_kernel_spmd as _run

    nc = _bacc.Bacc("TRN2", target_bir_lowering=False, num_devices=1)
    arrays, args = {}, []
    for name in _INS:
        a = _np.ascontiguousarray(inputs[name])
        arrays[f"in_{name}_dram"] = a
        args.append(nc.dram_tensor(f"in_{name}_dram", a.shape, _mybir.dt.from_np(a.dtype), kind="ExternalInput").ap())
    out = nc.dram_tensor("out_dram", arrays["in_x_dram"].shape, _mybir.dt.float32, kind="ExternalOutput").ap()
    hybrid_block(nc, *args, out)
    r = _run(nc, [arrays], core_ids=[0])
    return r.results[0]["out_dram"]
```
